# Optimizing a Trainium2 kernel written in Bass

```python
import math
import jax, jax.numpy as jnp
from jax import lax
import numpy as np

D_MODEL = 1024
BATCH = 1
SEQ = 1024
DEPTH = 1
DEC_BATCH = 8
DEC_SEQ = 1
PAST_LEN = 8192
PAGE_SIZE = 128

LRU_W = D_MODEL
LRU_HEADS = 16
LRU_BLOCK = LRU_W // LRU_HEADS
LRU_C = 8.0
CONV_W = 4
SSD_INNER = D_MODEL
SSD_HEADS = 16
SSD_HEAD_DIM = SSD_INNER // SSD_HEADS
SSD_GROUPS = 2
SSD_STATE = 128
SSD_CHUNK = 128
SSD_CONV_DIM = SSD_INNER + 2 * SSD_GROUPS * SSD_STATE
MIX_W = LRU_W + SSD_INNER
IN_COLS = 2 * LRU_W + SSD_INNER + SSD_CONV_DIM + SSD_HEADS
SPLITS = (LRU_W, 2 * LRU_W, 2 * LRU_W + SSD_INNER, 2 * LRU_W + SSD_INNER + SSD_CONV_DIM)
N_EXPERT_GROUPS = 4
EXPERTS_PER_GROUP = 8
N_EXPERTS = N_EXPERT_GROUPS * EXPERTS_PER_GROUP
TOP_K = 2
D_FF_EXPERT = D_MODEL // 2
MOE_BLOCK = 128
N_MOD = 6
LN_EPS = 1e-5
RMS_EPS = 1e-6

kernel_name = 'hymba_rglru_ssd_hmoe_step'

def layer_norm(x, g=None, b=None):
    xf = x.astype(jnp.float32)
    xc = xf - xf.mean(-1, keepdims=True)
    y = xc * lax.rsqrt((xc * xc).mean(-1, keepdims=True) + LN_EPS)
    if g is not None:
        y = y * g.astype(jnp.float32) + b.astype(jnp.float32)
    return y.astype(x.dtype)

def rms_norm(x, g):
    xf = x.astype(jnp.float32)
    y = xf * lax.rsqrt((xf * xf).mean(-1, keepdims=True) + RMS_EPS) * g.astype(jnp.float32)
    return y.astype(x.dtype)

def causal_conv(x, buf, w, b):
    L = x.shape[1]
    xp = jnp.concatenate([buf.astype(x.dtype), x], axis=1)
    y = xp[:, 0:L] * w[0]
    for k in range(1, CONV_W):
        y = y + xp[:, k:k + L] * w[k]
    return y + b, xp[:, -(CONV_W - 1):]

def rglru(x, h0, wa, ba, wx, bx, lam):
    b, L, W = x.shape
    xf = x.astype(jnp.float32)
    xb = xf.reshape(b, L, LRU_HEADS, LRU_BLOCK)
    r = jax.nn.sigmoid(jnp.einsum('blhi,hij->blhj', xb, wa.astype(jnp.float32)) + ba).reshape(b, L, W)
    i = jax.nn.sigmoid(jnp.einsum('blhi,hij->blhj', xb, wx.astype(jnp.float32)) + bx).reshape(b, L, W)
    log_a = -LRU_C * r * jax.nn.softplus(-lam.astype(jnp.float32))
    a = jnp.exp(log_a)
    u = jnp.sqrt(-jnp.expm1(2.0 * log_a)) * (i * xf)
    u = u.at[:, 0].add(a[:, 0] * h0.astype(jnp.float32))

    def combine(left, right):
        a_l, u_l = left
        a_r, u_r = right
        return a_l * a_r, a_r * u_l + u_r

    _, h = lax.associative_scan(combine, (a, u), axis=1)
    return h, h[:, -1]

def ssd_chunked(x, dt, A, bm, cm, s0):
    b, L, H, P = x.shape
    G, N = bm.shape[2], bm.shape[3]
    HG = H // G
    Q = SSD_CHUNK if L >= SSD_CHUNK else L
    nc = -(-L // Q)
    pad = nc * Q - L
    if pad:
        def padl(t):
            return jnp.pad(t, [(0, 0), (0, pad)] + [(0, 0)] * (t.ndim - 2))
        x, dt, bm, cm = padl(x), padl(dt), padl(bm), padl(cm)
    xc = x.reshape(b, nc, Q, G, HG, P)
    dtc = dt.reshape(b, nc, Q, G, HG)
    bc = bm.reshape(b, nc, Q, G, N)
    cc = cm.reshape(b, nc, Q, G, N)
    acs = jnp.cumsum(dtc * A.reshape(G, HG), axis=2)
    xdt = xc * dtc[..., None]
    causal = jnp.tril(jnp.ones((Q, Q), bool))[None, None, :, :, None, None]
    seg = acs[:, :, :, None] - acs[:, :, None, :]
    decay = jnp.where(causal, jnp.exp(jnp.where(causal, seg, 0.0)), 0.0)
    cb = jnp.einsum('bclgn,bcsgn->bclsg', cc, bc)
    y_diag = jnp.einsum('bclsgj,bcsgjp->bclgjp', cb[..., None] * decay, xdt)
    decay_end = jnp.exp(acs[:, :, -1:] - acs)
    chunk_states = jnp.einsum('bclgn,bclgj,bclgjp->bcgjpn', bc, decay_end, xdt)
    chunk_decay = jnp.exp(acs[:, :, -1])

    def step(s, inp):
        cd, cs = inp
        return cd[..., None, None] * s + cs, s

    s_fin, s_in = lax.scan(step, s0.reshape(b, G, HG, P, N),
                           (jnp.moveaxis(chunk_decay, 1, 0), jnp.moveaxis(chunk_states, 1, 0)))
    s_in = jnp.moveaxis(s_in, 0, 1)
    y_off = jnp.einsum('bclgn,bcgjpn,bclgj->bclgjp', cc, s_in, jnp.exp(acs))
    y = (y_diag + y_off).reshape(b, nc * Q, H, P)[:, :L]
    return y, s_fin.reshape(b, H, P, N)

def mixer(u, lru_conv0, lru_h0, ssd_conv0, ssd_s0, w_in, lru_conv_w, lru_conv_b, lru_wa, lru_ba,
          lru_wx, lru_bx, lru_lambda, lru_norm_g, ssd_conv_w, ssd_conv_b, ssd_dt_bias, ssd_a_log,
          ssd_d, ssd_norm_g, w_out):
    b, L, _ = u.shape
    proj = u @ w_in
    x_l, g_l, z, xbc, dt_raw = jnp.split(proj, SPLITS, axis=-1)
    x_lc, lru_conv_new = causal_conv(x_l, lru_conv0, lru_conv_w, lru_conv_b)
    h, h_last = rglru(x_lc, lru_h0, lru_wa, lru_ba, lru_wx, lru_bx, lru_lambda)
    y_l = rms_norm(h.astype(u.dtype) * jax.nn.gelu(g_l), lru_norm_g)
    xbc_c, ssd_conv_new = causal_conv(xbc, ssd_conv0, ssd_conv_w, ssd_conv_b)
    xbc_c = jax.nn.silu(xbc_c).astype(jnp.float32)
    gn = SSD_GROUPS * SSD_STATE
    xh = xbc_c[..., :SSD_INNER].reshape(b, L, SSD_HEADS, SSD_HEAD_DIM)
    bm = xbc_c[..., SSD_INNER:SSD_INNER + gn].reshape(b, L, SSD_GROUPS, SSD_STATE)
    cm = xbc_c[..., SSD_INNER + gn:].reshape(b, L, SSD_GROUPS, SSD_STATE)
    dt = jax.nn.softplus(dt_raw.astype(jnp.float32) + ssd_dt_bias.astype(jnp.float32))
    a = -jnp.exp(ssd_a_log.astype(jnp.float32))
    y, s_last = ssd_chunked(xh, dt, a, bm, cm, ssd_s0.astype(jnp.float32))
    y = (y + ssd_d.astype(jnp.float32)[:, None] * xh).reshape(b, L, SSD_INNER).astype(u.dtype)
    y_s = rms_norm(y * jax.nn.silu(z), ssd_norm_g)
    out = jnp.concatenate([y_l, y_s], axis=-1) @ w_out
    return out, (lru_conv_new, h_last.astype(u.dtype), ssd_conv_new, s_last.astype(u.dtype))

def hmoe(v, w_rg, b_rg, w_re, b_re, w_gate, w_up, w_down):
    T, D = v.shape
    vf = v.astype(jnp.float32)
    lg = vf @ w_rg.astype(jnp.float32) + b_rg.astype(jnp.float32)
    pg = jax.nn.softmax(lg, axis=-1)
    g_sel = jnp.argmax(lg, axis=-1)
    le = (vf @ w_re.astype(jnp.float32) + b_re.astype(jnp.float32)).reshape(T, N_EXPERT_GROUPS, EXPERTS_PER_GROUP)
    le_sel = jnp.take_along_axis(le, jnp.broadcast_to(g_sel[:, None, None], (T, 1, EXPERTS_PER_GROUP)), axis=1)[:, 0]
    top_v, top_i = lax.top_k(le_sel, TOP_K)
    gate = jnp.take_along_axis(pg, g_sel[:, None], axis=1) * jax.nn.softmax(top_v, axis=-1)
    eid = (g_sel[:, None] * EXPERTS_PER_GROUP + top_i).reshape(-1).astype(jnp.int32)
    tok = jnp.repeat(jnp.arange(T, dtype=jnp.int32), TOP_K)
    gw = gate.reshape(-1)
    order = jnp.argsort(eid)
    eid_s, tok_s, gw_s = eid[order], tok[order], gw[order]
    A = T * TOP_K
    counts = jnp.zeros((N_EXPERTS,), jnp.int32).at[eid].add(1)
    padded = ((counts + MOE_BLOCK - 1) // MOE_BLOCK) * MOE_BLOCK
    off = jnp.cumsum(counts) - counts
    pend = jnp.cumsum(padded)
    poff = pend - padded
    dest = poff[eid_s] + (jnp.arange(A, dtype=jnp.int32) - off[eid_s])
    NB = (A + N_EXPERTS * (MOE_BLOCK - 1) + MOE_BLOCK - 1) // MOE_BLOCK
    P = NB * MOE_BLOCK
    xpad = jnp.zeros((P, D), v.dtype).at[dest].set(v[tok_s])
    blk_e = jnp.clip(jnp.searchsorted(pend, jnp.arange(NB, dtype=jnp.int32) * MOE_BLOCK, side='right'), 0, N_EXPERTS - 1)

    def expert_block(args):
        xb, e = args
        hb = jax.nn.silu(xb @ w_gate[e]) * (xb @ w_up[e])
        return hb @ w_down[e]

    ypad = lax.map(expert_block, (xpad.reshape(NB, MOE_BLOCK, D), blk_e)).reshape(P, D)
    ys = (ypad[dest] * gw_s[:, None]).astype(v.dtype)
    return jnp.zeros((T, D), v.dtype).at[tok_s].add(ys)

def ada_mod(c, w, b):
    m = jax.nn.silu(c) @ w + b
    return m.reshape(c.shape[0], N_MOD, 1, D_MODEL)

def modulate(x, shift, scale):
    return layer_norm(x) * (1.0 + scale) + shift

def setup_inputs(seed: int = 0) -> dict:
    key = jax.random.key(seed)
    ks = iter(jax.random.split(key, 64))
    f32 = jnp.float32

    def nrm(shape, scale):
        return jax.random.normal(next(ks), shape, f32) * scale

    def unif(shape, lo, hi):
        return jax.random.uniform(next(ks), shape, f32, lo, hi)

    beta = (8.0 * DEPTH) ** -0.25
    Dp = DEPTH
    lru_a = unif((Dp, LRU_W), 0.9, 0.999) ** (1.0 / LRU_C)
    lru_lambda = jnp.log(lru_a) - jnp.log1p(-lru_a)
    dt0 = jnp.exp(unif((Dp, SSD_HEADS), math.log(1e-3), math.log(1e-1)))
    dt_bias = dt0 + jnp.log(-jnp.expm1(-dt0))
    return {
        'x_prompt': nrm((BATCH, SEQ, D_MODEL), 1.0),
        'x_sample': nrm((DEC_BATCH, DEC_SEQ, D_MODEL), 1.0),
        'c_prompt': nrm((BATCH, D_MODEL), 1.0),
        'c_sample': nrm((DEC_BATCH, D_MODEL), 1.0),
        'state_lru_conv': nrm((Dp, DEC_BATCH, CONV_W - 1, LRU_W), 1.0),
        'state_lru_h': nrm((Dp, DEC_BATCH, LRU_W), 0.5),
        'state_ssd_conv': nrm((Dp, DEC_BATCH, CONV_W - 1, SSD_CONV_DIM), 1.0),
        'state_ssd': nrm((Dp, DEC_BATCH, SSD_HEADS, SSD_HEAD_DIM, SSD_STATE), 0.5),
        'w_ada': nrm((Dp, D_MODEL, N_MOD * D_MODEL), D_MODEL ** -0.5),
        'b_ada': nrm((Dp, N_MOD * D_MODEL), 0.01),
        'w_in': nrm((Dp, D_MODEL, IN_COLS), D_MODEL ** -0.5),
        'lru_conv_w': nrm((Dp, CONV_W, LRU_W), 0.5),
        'lru_conv_b': nrm((Dp, LRU_W), 0.01),
        'lru_wa': nrm((Dp, LRU_HEADS, LRU_BLOCK, LRU_BLOCK), LRU_BLOCK ** -0.5),
        'lru_ba': nrm((Dp, LRU_HEADS, LRU_BLOCK), 0.01),
        'lru_wx': nrm((Dp, LRU_HEADS, LRU_BLOCK, LRU_BLOCK), LRU_BLOCK ** -0.5),
        'lru_bx': nrm((Dp, LRU_HEADS, LRU_BLOCK), 0.01),
        'lru_lambda': lru_lambda,
        'lru_norm_g': 1.0 + nrm((Dp, LRU_W), 0.02),
        'ssd_conv_w': nrm((Dp, CONV_W, SSD_CONV_DIM), 0.5),
        'ssd_conv_b': nrm((Dp, SSD_CONV_DIM), 0.01),
        'ssd_dt_bias': dt_bias,
        'ssd_a_log': jnp.log(unif((Dp, SSD_HEADS), 1.0, 16.0)),
        'ssd_d': 1.0 + nrm((Dp, SSD_HEADS), 0.1),
        'ssd_norm_g': 1.0 + nrm((Dp, SSD_INNER), 0.02),
        'w_out': nrm((Dp, MIX_W, D_MODEL), MIX_W ** -0.5 * beta),
        'ln1_g': 1.0 + nrm((Dp, D_MODEL), 0.02),
        'ln1_b': nrm((Dp, D_MODEL), 0.01),
        'w_rg': nrm((Dp, D_MODEL, N_EXPERT_GROUPS), D_MODEL ** -0.5),
        'b_rg': nrm((Dp, N_EXPERT_GROUPS), 0.01),
        'w_re': nrm((Dp, D_MODEL, N_EXPERTS), D_MODEL ** -0.5),
        'b_re': nrm((Dp, N_EXPERTS), 0.01),
        'w_gate': nrm((Dp, N_EXPERTS, D_MODEL, D_FF_EXPERT), D_MODEL ** -0.5),
        'w_up': nrm((Dp, N_EXPERTS, D_MODEL, D_FF_EXPERT), D_MODEL ** -0.5),
        'w_down': nrm((Dp, N_EXPERTS, D_FF_EXPERT, D_MODEL), D_FF_EXPERT ** -0.5 * beta),
        'ln2_g': 1.0 + nrm((Dp, D_MODEL), 0.02),
        'ln2_b': nrm((Dp, D_MODEL), 0.01),
    }

def reference(x_prompt, x_sample, c_prompt, c_sample, state_lru_conv, state_lru_h, state_ssd_conv,
              state_ssd, w_ada, b_ada, w_in, lru_conv_w, lru_conv_b, lru_wa, lru_ba, lru_wx, lru_bx,
              lru_lambda, lru_norm_g, ssd_conv_w, ssd_conv_b, ssd_dt_bias, ssd_a_log, ssd_d,
              ssd_norm_g, w_out, ln1_g, ln1_b, w_rg, b_rg, w_re, b_re, w_gate, w_up, w_down,
              ln2_g, ln2_b):
    alpha = (2.0 * DEPTH) ** 0.25
    xp, xs = x_prompt, x_sample
    bp = xp.shape[0]
    dtype = xp.dtype
    p_lc, p_lh, p_sc, p_ss = [], [], [], []
    s_lc, s_lh, s_sc, s_ss = [], [], [], []
    for l in range(DEPTH):
        mp = ada_mod(c_prompt, w_ada[l], b_ada[l])
        ms = ada_mod(c_sample, w_ada[l], b_ada[l])
        mix_w = (w_in[l], lru_conv_w[l], lru_conv_b[l], lru_wa[l], lru_ba[l], lru_wx[l], lru_bx[l],
                 lru_lambda[l], lru_norm_g[l], ssd_conv_w[l], ssd_conv_b[l], ssd_dt_bias[l],
                 ssd_a_log[l], ssd_d[l], ssd_norm_g[l], w_out[l])
        op, stp = mixer(modulate(xp, mp[:, 0], mp[:, 1]),
                        jnp.zeros((bp, CONV_W - 1, LRU_W), dtype),
                        jnp.zeros((bp, LRU_W), dtype),
                        jnp.zeros((bp, CONV_W - 1, SSD_CONV_DIM), dtype),
                        jnp.zeros((bp, SSD_HEADS, SSD_HEAD_DIM, SSD_STATE), dtype),
                        *mix_w)
        os_, sts = mixer(modulate(xs, ms[:, 0], ms[:, 1]),
                         state_lru_conv[l], state_lru_h[l], state_ssd_conv[l], state_ssd[l], *mix_w)
        xp = layer_norm(alpha * xp + mp[:, 2] * op, ln1_g[l], ln1_b[l])
        xs = layer_norm(alpha * xs + ms[:, 2] * os_, ln1_g[l], ln1_b[l])
        vp = modulate(xp, mp[:, 3], mp[:, 4])
        vs = modulate(xs, ms[:, 3], ms[:, 4])
        n_p = vp.shape[0] * vp.shape[1]
        f = hmoe(jnp.concatenate([vp.reshape(-1, D_MODEL), vs.reshape(-1, D_MODEL)], axis=0),
                 w_rg[l], b_rg[l], w_re[l], b_re[l], w_gate[l], w_up[l], w_down[l])
        xp = layer_norm(alpha * xp + mp[:, 5] * f[:n_p].reshape(xp.shape), ln2_g[l], ln2_b[l])
        xs = layer_norm(alpha * xs + ms[:, 5] * f[n_p:].reshape(xs.shape), ln2_g[l], ln2_b[l])
        p_lc.append(stp[0]); p_lh.append(stp[1]); p_sc.append(stp[2]); p_ss.append(stp[3])
        s_lc.append(sts[0]); s_lh.append(sts[1]); s_sc.append(sts[2]); s_ss.append(sts[3])
    return (xp, xs,
            jnp.stack(p_lc), jnp.stack(p_lh), jnp.stack(p_sc), jnp.stack(p_ss),
            jnp.stack(s_lc), jnp.stack(s_lh), jnp.stack(s_sc), jnp.stack(s_ss))


_drawn_inputs = setup_inputs


def setup_inputs(seed=0):
    import zlib

    import numpy as np

    out = dict(_drawn_inputs(seed))
    spreads = {}
    factors = {'b_ada': 3.345,
     'lru_conv_b': 3.138,
     'lru_ba': 29.557,
     'lru_bx': 8.0,
     'lru_norm_g': 58.725,
     'ssd_conv_b': 4.03,
     'ssd_d': 8.0,
     'ssd_norm_g': 27.191,
     'ln1_b': 4.948,
     'b_rg': 22.488,
     'b_re': 22.391,
     'ln2_g': 23.036,
     'ln2_b': 44.234}
    for name, (base, spread) in spreads.items():
        noise = np.random.default_rng([zlib.crc32(name.encode()), seed]).standard_normal(out[name].shape)
        drawn = base * np.exp(spread * noise) if base else spread * noise
        out[name] = __import__('jax').numpy.asarray(drawn.astype(out[name].dtype))
    for name, factor in factors.items():
        out[name] = (out[name] * factor).astype(out[name].dtype)
    return out
```

```python
from contextlib import ExitStack

import numpy as np
import concourse.bass as bass
from concourse import mybir

F32 = mybir.dt.float32
I32 = mybir.dt.int32
U32 = mybir.dt.uint32
ALU = mybir.AluOpType
ACT = mybir.ActivationFunctionType
AX = mybir.AxisListType

P = 128
D = 1024
KT = D // P
SEQ = 1024
NT = SEQ // P
DEC = 8
CONV = 4
HEADS = 16
HD = 64
STATE = 128
XBC = D + 4 * STATE
XT = XBC // P
COL_G, COL_Z, COL_XBC = D, 2 * D, 3 * D
COL_DT = COL_XBC + XBC
NE = 32
NG = 4
EG = NE // NG
FF = 512
CAP = 128
NOV = 16
NMOD = 6
TE = SEQ + DEC * CONV
CH = TE // 3
S0 = SEQ + CONV - 1
ALPHA = 2.0 ** 0.25
LN_EPS = 1e-5
RMS_EPS = 1e-6
LRU_C = 8.0


class Chain:

    def __init__(self, eng, sem, base=0):
        self.eng, self.sem, self.base, self.n = eng, sem, base, 0

    def __call__(self, ins):
        self.n += 1
        ins.then_inc(self.sem, 1)
        self.eng.wait_ge(self.sem, self.base + self.n)


def bcast_rows(row, n):
    return row.partition_broadcast(n)


def build_step(nc, x_prompt, x_sample, c_prompt, c_sample, state_lru_conv, state_lru_h, state_ssd_conv,
               state_ssd, w_ada, b_ada, w_in, lru_conv_w, lru_conv_b, lru_wa, lru_ba, lru_wx, lru_bx,
               lru_lambda, lru_norm_g, ssd_conv_w, ssd_conv_b, ssd_dt_bias, ssd_a_log, ssd_d,
               ssd_norm_g, w_out, ln1_g, ln1_b, w_rg, b_rg, w_re, b_re, w_gate, w_up, w_down,
               ln2_g, ln2_b, y_prompt, y_sample, prompt_lru_conv, prompt_lru_h, prompt_ssd_conv,
               prompt_ssd, sample_lru_conv, sample_lru_h, sample_ssd_conv, sample_ssd):
    ctx = ExitStack()

    def sb(name, shape, dt=F32):
        return ctx.enter_context(nc.sbuf_tensor(name, shape, dt))

    def dram(name, shape, dt=F32):
        return nc.dram_tensor(name, shape, dt, kind="Internal").ap()

    with ctx:
        mod_d = dram("mod_d", [1 + DEC, NMOD * D])
        x_d = dram("x_d", [KT, P, TE])
        z_d = dram("z_d", [KT, P, TE])
        y_d = dram("y_d", [2 * KT, P, SEQ])
        acs_d = dram("acs_d", [NT, HEADS * P])
        bcs_d = dram("bcs_d", [4, DEC * P])
        xp1_d = dram("xp1_d", [SEQ + DEC, D])
        v_d = dram("v_d", [SEQ + DEC, D])
        tok_d = dram("tok_d", [(NE + NOV) * CAP, 1], I32)
        ys_d = dram("ys_d", [(NE + NOV) * CAP, D])

        WORDS = 47744
        arena = sb("arena", [P, WORDS])

        def at(off, *dims, parts=P):
            n = int(np.prod(dims))
            assert off + n <= WORDS, (off, dims)
            v = arena[0:parts, off:off + n]
            if len(dims) == 2:
                v = v.rearrange("p (a b) -> p a b", a=dims[0])
            if len(dims) == 3:
                v = v.rearrange("p (a b c) -> p a b c", a=dims[0], b=dims[1])
            return v

        uT = at(0, KT, TE)
        BC = at(8448, 4, TE)
        wsl = [at(12672 + 1024 * b, KT, P) for b in range(2)]
        A0 = 14720
        adaw = [at(A0 + 4096 * b, KT, 512) for b in range(2)]
        bada = at(22912, NMOD * D, parts=9)
        mod = at(29056, NMOD * D, parts=9)
        xt = [at(35200 + 1024 * b, D) for b in range(2)]
        xn = [at(37248 + 1024 * b, D) for b in range(2)]
        ltmp = at(39296, KT, P)
        cin = at(40320, D, parts=9)
        cs = at(41344, D, parts=9)
        prow = at(42368, D, parts=42)
        prow2 = at(43392, XBC, parts=29)
        xb2 = [at(A0 + 1060 * b, 1060) for b in range(2)]
        cacc = [at(16840 + TE * b, TE) for b in range(2)]
        cth = [at(18952 + TE * b, TE) for b in range(2)]
        xo = [at(21064 + TE * b, TE) for b in range(2)]
        (Rb, SEG, ER) = [at(A0 + 2048 * i, HEADS, P) for i in range(3)]
        o = A0 + 6144
        xst, zst, xdt, xw, Sst, Sin, stmp, xD = [at(o + 1024 * i, KT, P) for i in range(8)]
        o += 8192
        bst = at(o, 2, P)
        CBm = at(o + 256, NT, 2, P)
        Btok = at(o + 2304, NT, 2, P)
        o += 4352
        xbl = at(o, 1060)
        xlc, gl, thr, thi, la, lt, la2, yl = [at(o + 1060 + TE * i, TE) for i in range(8)]
        o += 1060 + 8 * TE
        BDa, BDx = at(o, P), at(o + P, P)
        o += 256
        ysC = at(o, KT, P)
        bcsb = at(A0, 4, DEC * P)
        dsm = at(o + 1024, 64)
        s0t = [at(A0 + 4096 + 1024 * b, DEC, P) for b in range(2)]
        t1t, t2t = at(A0 + 6144, DEC, P), at(A0 + 7168, DEC, P)
        snt = [at(A0 + 8192 + 1024 * b, DEC, P) for b in range(2)]

        xzs = at(A0 + 11264, 2, KT, 4 * DEC)
        xdS = at(A0 + 11776, KT, DEC)
        yr = at(A0 + 11840, KT, DEC)
        exd = at(A0 + 11904, KT, 2 * DEC)
        dcT = at(A0 + 12032, 2 * DEC, parts=HEADS)
        bcr = at(A0 + 12160, 4 * P, parts=DEC)
        co = at(A0 + 12672, (KT + XT) * P, parts=27)
        ho = at(A0 + 15232, D, parts=9)
        So = at(A0 + 16256, KT, P)
        WO = [at(0, KT, D), at(33408, KT, D)]
        ysl = [at(8192 + 2048 * b, 2 * KT, P) for b in range(2)]
        ysq = at(12288, 2 * KT, P)
        gate1, ln1g, ln1b, sc2, sh2 = [at(41600 + 1024 * i, D) for i in range(5)]
        xr = [at(32000, D), at(46720, D)]
        ob = at(A0, D)
        xp1 = [at(A0 + 1024 + 1024 * b, D) for b in range(2)]
        vb = [at(A0 + 3072 + 1024 * b, D) for b in range(2)]
        vsl = [at(41600 + 1024 * b, D) for b in range(2)]
        vT = [at(43648 + 1024 * b, KT, P) for b in range(2)]
        NTT = NT + 1
        gtmp = [at(45696 + NE * NTT * i, NTT, NE) for i in range(7)]
        wg = [at(20864, KT, FF), at(0, KT, FF)]
        wu = [at(24960, KT, FF), at(4096, KT, FF)]
        wd = [at(29056, FF // P, D), at(8192, FF // P, D)]
        xg = [at(37504 + 1024 * b, D) for b in range(2)]
        xTs = [at(39552 + 1024 * b, KT, P) for b in range(2)]
        hth, hb, hT = at(12288, FF), at(12800, FF), at(13312, FF // P, P)
        yo = [at(A0 + 1024 * b, D) for b in range(2)]
        gate2, ln2g, ln2b = [at(41600 + 1024 * i, D) for i in range(3)]
        xl2 = [at(16768 + 1024 * b, D) for b in range(2)]
        y1s = [at(44672 + 1024 * b, D) for b in range(2)]
        y2s = [at(46720, D), at(18816, D)]
        fo = [at(19840, D), at(33408, D)]
        ident = sb("ident", [P, P])
        ones = sb("ones", [P, P])
        tri = sb("tri", [P, P])
        PT1 = sb("PT1", [P, KT, 42])
        PT2 = sb("PT2", [P, XT, 29])
        cur1 = sb("cur1", [P, 42])
        cur2 = [sb(f"cur2{b}", [P, 29]) for b in range(2)]
        cso = sb("cso", [P, KT + XT, 27])
        hso = sb("hso", [P, KT, 9])
        ssT = sb("ssT", [P, 2, KT, 9])
        spl = sb("spl", [P, KT, 2])
        dtr = sb("dtr", [P, 8, NT + 1, HEADS])
        DT, DTA, ACS, TOT, CD, DXW = [dtr[:, i, :, :] for i in range(6)]
        acsT = at(47000, P)
        wdt = sb("wdt", [P, KT, HEADS])
        dtb = sb("dtb", [P, 2, HEADS])
        Dch = sb("Dch", [P, KT])
        Dh = sb("Dh", [HEADS, 1])
        EX = at(45000, KT, P, parts=HEADS)
        triS = sb("triS", [P, P])
        acur = sb("acur", [P, HEADS])
        rs2 = sb("rs2", [P, 2])
        wr = sb("wr", [P, KT, 36])
        brb = sb("brb", [P, 36])
        Lg = sb("Lg", [P, NTT, 36])
        gat = sb("gat", [P, 2, NTT])
        slot = sb("slot", [P, 2, NTT], U32)
        gsm = sb("gsm", [P, 12, NTT])
        gon = sb("gon", [P, 4, NTT, EG])
        cnt = sb("cnt", [P, 6, NE])
        ovq = sb("ovq", [P, 2, NOV])
        ctl = sb("ctl", [P, NOV + 1], I32)
        desc = sb("desc", [P, EG])
        ebase = sb("ebase", [P, NE])
        qidx = sb("qidx", [P, NOV])
        itmp = at(46200, 3, NE).bitcast(I32)
        tokid = sb("tokid", [P, NTT], I32)
        tzero = at(46100, NE + NOV).bitcast(I32)
        tokr = at(43648, P, parts=NE + NOV).bitcast(I32)
        tokf = at(43776, P, parts=NE + NOV)
        idxT = sb("idxT", [P, NE + NOV], I32)
        icur = [sb(f"icur{b}", [P, 1], I32) for b in range(2)]
        gcur = sb("gcur", [P, 2])
        sl1 = [sb(f"sl1{b}", [P, 2], U32) for b in range(2)]
        cT = sb("cT", [P, KT, 9])
        stat = sb("stat", [P, 12])
        mv = sb("mv", [P, 2])
        rstd = sb("rstd", [P, 1])
        sm = sb("sm", [P, 8, 24])
        yS = sb("yS", [P, 2 * KT, DEC])
        PS = ctx.enter_context(nc.psum_tensor("PS", [P, 8, 512], F32))

        in_first = []

        def sem(name):
            s = nc.alloc_semaphore(name)
            in_first.append(s)
            return s

        pool_gate = sem("pool_gate")
        vector_gate = sem("vector_gate")
        c_loaded = sem("c_loaded")
        rows_loaded = sem("rows_loaded")
        rows2_loaded = sem("rows2_loaded")
        small_loaded = sem("small_loaded")
        bada_loaded = sem("bada_loaded")
        pt_mm = sem("pt_mm")
        adaw_loaded = [sem(f"adaw_loaded{b}") for b in range(2)]
        ada_mm = [sem(f"ada_mm{b}") for b in range(2)]
        ada_ready = [sem(f"ada_ready{b}") for b in range(2)]
        mod_stored = sem("mod_stored")
        xt_loaded = [sem(f"xt_loaded{b}") for b in range(3)]
        var_ready = sem("var_ready")
        std_ready = sem("std_ready")
        xn_ready = [sem(f"xn_ready{b}") for b in range(3)]
        xnT_mm = [sem(f"xnT_mm{b}") for b in range(3)]
        uT_ready = [sem(f"uT_ready{b}") for b in range(3)]
        vc = sem("vector_step")
        gc = sem("gpsimd_step")
        ac = sem("scalar_step")
        vl = sem("vector_loop_step")
        al = sem("scalar_loop_step")
        w_loaded = [sem(f"w_loaded{b}") for b in range(2)]
        proj_mm = [sem(f"proj_mm{b}") for b in range(2)]
        px_copied = [sem(f"px_copied{b}") for b in range(2)]
        hist_set = [sem(f"hist_set{b}") for b in range(2)]
        conv_done = [sem(f"conv_done{b}") for b in range(2)]
        cth_ready = [sem(f"cth_ready{b}") for b in range(2)]
        xo_ready = [sem(f"xo_ready{b}") for b in range(2)]
        xo_stored = [sem(f"xo_stored{b}") for b in range(2)]
        cur_ready = [sem(f"cur_ready{b}") for b in range(2)]
        out_stored = sem("out_stored")
        tok_zeroed = sem("tok_zeroed")
        s0_loaded = [sem(f"s0_loaded{b}") for b in range(2)]
        sn_stored = [sem(f"sn_stored{b}") for b in range(2)]
        ltmp_ready = sem("ltmp_ready")
        ys_copied = sem("ys_copied")
        bcr_stored = sem("bcr_stored")
        bcs_loaded = sem("bcs_loaded")
        xzs_loaded = sem("xzs_loaded")
        t1_ready = sem("t1_ready")
        sn_ready = sem("sn_ready")
        acs_stored = sem("acs_stored")
        i_mm = sem("i_mm")
        bd_loaded = sem("bd_loaded")
        seg_ready = sem("seg_ready")
        er_ready = sem("er_ready")
        r_loaded = sem("r_loaded")
        xt_mm = sem("xt_mm")
        xd_ready = sem("xd_ready")
        xst_loaded = sem("xst_loaded")
        ysc_ready = sem("ysc_ready")
        zst_loaded = sem("zst_loaded")
        bst_ready = sem("bst_ready")
        ec_ready = sem("ec_ready")
        sin_ready = sem("sin_ready")
        stmp_ready = sem("stmp_ready")
        segx_ready = sem("segx_ready")
        m_ready = sem("m_ready")
        xw_ready = sem("xw_ready")
        st_mm = sem("st_mm")
        state_ready = sem("state_ready")
        y_mm = sem("y_mm")
        xl_copied = sem("xl_copied")
        lhist_set = sem("lhist_set")
        xlc_ready = sem("xlc_ready")
        gl_ready = sem("gl_ready")
        r_mm = sem("r_mm")
        thr_ready = sem("thr_ready")
        thi_ready = sem("thi_ready")
        la_ready = sem("la_ready")
        lt_ready = sem("lt_ready")
        la2_ready = sem("la2_ready")
        ls_ready = sem("ls_ready")
        yl_ready = sem("yl_ready")
        yl_stored = sem("yl_stored")
        ysc_stored = sem("ysc_stored")
        tensor_once = sem("tensor_once")
        (PT1_MM, PT2_MM, CT_MM, SS_MM, DT_MM, DCH_MM, CB_MM, ACS_MM, ACST_MM, BT_MM, DC_MM, BCR_MM,
         CO_MM, EX_MM, HO_MM, SO_MM) = \
            (1, 2, 3, 4, 5, 6, 7, 8, 9, 10, 11, 12, 13, 14, 15, 16)
        vector_once = sem("vector_once")
        (CS_READY, PT_READY, CT_READY, LAM_READY, SC1_READY, SS_READY, MOD_READY, DTE_IN, DTA_READY,
         CB_READY, ACS_COPIED, DXE_IN, ACST_READY, BT_READY, DC_READY, BCR_READY, EXD_READY, YR_DONE) = \
            (1, 3, 4, 5, 6, 7, 8, 9, 10, 11, 13, 14, 15, 16, 17, 18, 19, 20)
        scalar_once = sem("scalar_once")
        (CSIG_READY, LAMEXP, DT_EXP, DXE_READY, HO_READY, CO_READY, SO_READY) = \
            (1, 2, 4, 7, 8, 9, 10)
        gpsimd_once = sem("gpsimd_once")
        (IDENT_MADE, TRI_MADE, EX_MADE, CONSTS_MADE, UZ, BD_ZEROED, XB_ZEROED) = \
            (1, 2, 3, 6, 7, 9, 13)

        win_t = w_in[0].rearrange("(k p) n -> p k n", p=P)
        wada_t = w_ada[0].rearrange("(k p) n -> p k n", p=P)

        with nc.Block() as block:
            @block.sync
            def _(sp):
                sp.dma_start(cin[0:1, :], c_prompt).then_inc(c_loaded, 16)
                sp.dma_start(cin[1:9, :], c_sample).then_inc(c_loaded, 16)
                for dst, src in ((prow[0:4, :], lru_conv_w[0]), (prow[4:5, :], lru_conv_b),
                                 (prow[5:6, :], lru_ba.rearrange("a h i -> a (h i)")),
                                 (prow[6:7, :], lru_bx.rearrange("a h i -> a (h i)")),
                                 (prow[7:8, :], lru_lambda), (prow[8:9, :], lru_norm_g),
                                 (prow[9:10, :], ssd_norm_g), (prow[10:18, :], state_lru_h[0]),
                                 (prow[18:42, :], state_lru_conv[0].rearrange("b k n -> (b k) n"))):
                    sp.dma_start(dst, src).then_inc(rows_loaded, 16)
                for dst, src in ((prow2[0:4, :], ssd_conv_w[0]), (prow2[4:5, :], ssd_conv_b),
                                 (prow2[5:29, :], state_ssd_conv[0].rearrange("b k n -> (b k) n"))):
                    sp.dma_start(dst, src).then_inc(rows2_loaded, 16)
                sp.dma_start(bada, b_ada[0:1, :].to_broadcast([9, NMOD * D])).then_inc(bada_loaded, 16)

                def load_ada(chunk, b):
                    sp.dma_start(adaw[b], wada_t[:, :, bass.ds(chunk * 512, 512)]).then_inc(adaw_loaded[b], 16)

                for b in range(2):
                    load_ada(b, b)
                with nc.allow_non_contiguous_dma(reason="one value per head"):
                    sp.dma_start(Dh[:, :], ssd_d.rearrange("a h -> h a")).then_inc(small_loaded, 16)
                sp.dma_start(dtb[:, 0, :], ssd_dt_bias[0:1, :].to_broadcast([P, HEADS])).then_inc(small_loaded, 16)
                sp.dma_start(dtb[:, 1, :], ssd_a_log[0:1, :].to_broadcast([P, HEADS])).then_inc(small_loaded, 16)
                sp.dma_start(wdt[:, :, :], win_t[:, :, COL_DT:COL_DT + HEADS]).then_inc(small_loaded, 16)
                for b in range(2):
                    sp.wait_ge(ada_mm[b], 1)
                    load_ada(2 + b, b)
                for b in range(2):
                    sp.dma_start(xt[b][:, :], x_prompt[0, b * P:(b + 1) * P, :]).then_inc(xt_loaded[b], 16)
                for b in range(2):
                    sp.dma_start(wsl[b], win_t[:, :, COL_XBC + b * P:COL_XBC + (b + 1) * P]).then_inc(w_loaded[b], 16)
                def next_x(i, b):
                    sp.wait_ge(xn_ready[b], i + 1)
                    sp.dma_start(xt[b][:, :], x_prompt[0, bass.ds((i * 2 + (2 + b)) * P, P), :])\
                        .then_inc(xt_loaded[b], 16)

                with sp.Fori(0, 3) as i:
                    for b in range(2):
                        sp.wait_ge(ada_mm[b], i + 2)
                        load_ada(i * 2 + (4 + b), b)
                        next_x(i, b)
                for b in range(2):
                    sp.wait_ge(ada_mm[b], 5)
                    load_ada(10 + b, b)
                sp.wait_ge(xn_ready[0], 4)
                sp.dma_start(xt[0][0:DEC, :], x_sample[:, 0, :]).then_inc(xt_loaded[2], 16)
                sp.wait_ge(vector_once, MOD_READY)
                sp.dma_start(mod_d, mod).then_inc(mod_stored, 16)

                def load_w(col, b):
                    sp.dma_start(wsl[b], win_t[:, :, bass.ds(col, P)]).then_inc(w_loaded[b], 16)

                with sp.Fori(0, 5) as i:
                    for b in range(2):
                        sp.wait_ge(proj_mm[b], i + 1)
                        load_w(i * (2 * P) + (COL_XBC + (2 + b) * P), b)
                with sp.Fori(0, 4) as i:
                    for b in range(2):
                        sp.wait_ge(proj_mm[b], i + 6)
                        load_w(i * (2 * P) + (COL_Z + b * P), b)
                sp.wait_ge(acs_stored, 16)
                sp.wait_ge(xo_stored[0], 16 * 8)
                sp.wait_ge(xo_stored[1], 16 * 8)
                with sp.Fori(0, NT) as j:
                    for b in range(2):
                        sp.wait_ge(proj_mm[b], j + 10)
                        load_w(j * P + b * COL_G, b)
                    sp.wait_ge(i_mm, j)
                    for wsrc, wdst in ((lru_wa, BDa), (lru_wx, BDx)):
                        for h in range(2):
                            sp.dma_start(wdst[HD * h:HD * (h + 1), HD * h:HD * (h + 1)],
                                         wsrc[0, bass.ds(j * 2 + h, 1), :, :].rearrange("a i j -> (a i) j"))\
                                .then_inc(bd_loaded, 16)
                    sp.wait_ge(seg_ready, j)
                    sp.wait_ge(er_ready, j)
                    sp.dma_start(Rb, acs_d[bass.ds(j, 1), :].to_broadcast([P, HEADS * P])
                                 .rearrange("p (h l) -> p h l", h=HEADS)).then_inc(r_loaded, 16)
                    sp.wait_ge(xt_mm, j)
                    sp.wait_ge(xd_ready, j)
                    sp.dma_start(xst, x_d[:, :, bass.ds(j * P, P)].rearrange("k p t -> p k t")).then_inc(xst_loaded, 16)
                    sp.wait_ge(ysc_ready, j)
                    sp.dma_start(zst, z_d[:, :, bass.ds(j * P, P)].rearrange("k p t -> p k t")).then_inc(zst_loaded, 16)

                sp.wait_ge(yl_ready, NT)
                sp.wait_ge(y_mm, NT)
                sp.wait_ge(m_ready, 2 * NT)
                sp.wait_ge(bcr_stored, 16)
                sp.dma_start(bcsb.rearrange("p a n -> p (a n)"),
                             bcs_d.rearrange("i n -> (i n)").unsqueeze(0).to_broadcast([P, 4 * DEC * P]))\
                    .then_inc(bcs_loaded, 16)
                for i, src in enumerate((x_d, z_d)):
                    sp.dma_start(xzs[:, i, :, :], src[:, :, SEQ:TE].rearrange("k p t -> p k t")).then_inc(xzs_loaded, 16)
                s_in = state_ssd[0].rearrange("b (k h) p n -> k (h p) b n", h=2)
                s_out = sample_ssd[0].rearrange("b (k h) p n -> k (h p) b n", h=2)
                for k in range(KT):
                    if k >= 2:
                        sp.wait_ge(t1_ready, k - 1)
                    sp.dma_start(s0t[k % 2], s_in[k]).then_inc(s0_loaded[k % 2], 16)
                    if k >= 1:
                        sp.wait_ge(sn_ready, k)
                        sp.dma_start(s_out[k - 1], snt[(k - 1) % 2]).then_inc(sn_stored[(k - 1) % 2], 16)
                sp.wait_ge(sn_ready, KT)
                sp.dma_start(s_out[KT - 1], snt[1]).then_inc(sn_stored[1], 16)
                sp.wait_ge(scalar_once, CO_READY)
                sp.dma_start(prompt_lru_conv[0, 0], co[0:3, 0:D]).then_inc(out_stored, 16)
                sp.dma_start(sample_lru_conv[0].rearrange("b k n -> (b k) n"), co[3:27, 0:D]).then_inc(out_stored, 16)
                sp.dma_start(prompt_ssd_conv[0, 0], co[0:3, D:D + XBC]).then_inc(out_stored, 16)
                sp.dma_start(sample_ssd_conv[0].rearrange("b k n -> (b k) n"), co[3:27, D:D + XBC])\
                    .then_inc(out_stored, 16)
                sp.wait_ge(scalar_once, HO_READY)
                sp.dma_start(prompt_lru_h[0], ho[0:1, :]).then_inc(out_stored, 16)
                sp.dma_start(sample_lru_h[0], ho[1:9, :]).then_inc(out_stored, 16)
                sp.wait_ge(scalar_once, SO_READY)
                sp.dma_start(prompt_ssd[0, 0].rearrange("(k h) p n -> (h p) k n", h=2), So).then_inc(out_stored, 16)
                sp.wait_ge(out_stored, 16 * 7)
                for b in range(2):
                    sp.wait_ge(sn_stored[b], 16 * 4)
                sp.wait_ge(tok_zeroed, 16)


            @block.gpsimd
            def _(gp):
                step = Chain(gp, gc)
                step(gp.memset(ident[:, :], 0.0))
                gp.affine_select(out=ident[:, :], in_=ident[:, :], compare_op=ALU.not_equal, fill=1.0, base=0,
                                 pattern=[[-1, P]], channel_multiplier=1).then_inc(gpsimd_once, 1)
                step(gp.memset(ones[:, :], 1.0))
                gp.affine_select(out=tri[:, :], in_=ones[:, :], compare_op=ALU.is_ge, fill=0.0, base=0,
                                 pattern=[[1, P]], channel_multiplier=-1).then_inc(gpsimd_once, 1)
                step(gp.memset(EX, 1.0))
                step(gp.affine_select(out=EX, in_=EX, compare_op=ALU.is_ge, fill=0.0, base=0,
                                      pattern=[[P, KT], [1, P]], channel_multiplier=-HD))
                gp.affine_select(out=EX, in_=EX, compare_op=ALU.is_ge, fill=0.0, base=HD - 1,
                                 pattern=[[-P, KT], [-1, P]], channel_multiplier=HD).then_inc(gpsimd_once, 1)
                step(gp.memset(tzero, 0))
                gp.dma_start(tok_d.rearrange("(p b) a -> p (b a)", p=P), tzero).then_inc(tok_zeroed, 16)
                gp.iota(itmp[:, 0, 0:EG], pattern=[[-1, EG]], base=EG, channel_multiplier=0).then_inc(gc, 1)
                gp.iota(itmp[:, 1, :], pattern=[[CAP, NE]], base=0, channel_multiplier=0).then_inc(gc, 1)
                gp.iota(itmp[:, 2, 0:NOV], pattern=[[1, NOV]], base=0, channel_multiplier=0).then_inc(gc, 1)
                gp.iota(tokid[:, :], pattern=[[P, NTT]], base=0, channel_multiplier=1).then_inc(gc, 1)
                step.n += 4
                gp.wait_ge(gc, step.n)
                gp.tensor_copy(desc[:, :], itmp[:, 0, 0:EG]).then_inc(gpsimd_once, 1)
                gp.tensor_copy(ebase[:, :], itmp[:, 1, :]).then_inc(gpsimd_once, 1)
                gp.tensor_copy(qidx[:, :], itmp[:, 2, 0:NOV]).then_inc(gpsimd_once, 1)
                gp.memset(uT[:, :, SEQ:TE], 0.0).then_inc(gpsimd_once, 1)
                gp.wait_ge(tensor_once, PT2_MM)
                gp.memset(BDa, 0.0).then_inc(gpsimd_once, 1)
                gp.memset(BDx, 0.0).then_inc(gpsimd_once, 1)
                for b in range(2):
                    gp.wait_ge(ada_mm[b], 6)
                for b in range(2):
                    gp.memset(xb2[b][:, 0:3], 0.0).then_inc(gpsimd_once, 1)
                with gp.Fori(0, 4) as i:
                    for b in range(2):
                        gp.wait_ge(xo_ready[b], i + 1)
                        gp.dma_start(x_d[bass.ds(i * 2 + b, 1), :, :].rearrange("a p t -> (a p) t"),
                                     xo[b]).then_inc(xo_stored[b], 16)
                        gp.wait_ge(xo_stored[b], i * 16 + 16)
                with gp.Fori(0, 4) as i:
                    for b in range(2):
                        gp.wait_ge(xo_ready[b], i + 7)
                        gp.dma_start(z_d[bass.ds(i * 2 + b, 1), :, :].rearrange("a p t -> (a p) t"),
                                     xo[b]).then_inc(xo_stored[b], 16)
                        gp.wait_ge(xo_stored[b], i * 16 + 80)

                gp.wait_ge(vector_once, ACST_READY)
                gp.dma_start(acs_d.rearrange("c (h l) -> (c h) l", h=HEADS), acsT).then_inc(acs_stored, 16)
                gp.wait_ge(vector_once, BT_READY)
                gp.wait_ge(xo_stored[0], 16 * 8)
                gp.wait_ge(xo_stored[1], 16 * 8)
                gp.memset(xbl[:, 0:3], 0.0).then_inc(gpsimd_once, 1)
                gp.memset(Sst, 0.0).then_inc(gpsimd_once, 1)
                gp.wait_ge(gpsimd_once, XB_ZEROED)
                with gp.Fori(0, NT) as j:
                    gp.wait_ge(st_mm, j)
                    gp.sem_inc(pool_gate, 1)
                    gp.tensor_copy(bst, Btok[:, bass.ds(j, 1), :, :].rearrange("p a g n -> p (a g) n"))\
                        .then_inc(bst_ready, 1)
                    gp.wait_ge(state_ready, j)
                    gp.wait_ge(y_mm, j)
                    gp.sem_inc(pool_gate, 1)
                    gp.tensor_copy(Sin, Sst).then_inc(sin_ready, 1)
                    gp.tensor_tensor(stmp.rearrange("p k (h q) -> p (k h) q", h=2),
                                     Sst.rearrange("p k (h q) -> p (k h) q", h=2),
                                     CD[:, bass.ds(j, 1), :].rearrange("p a h -> p (a h)").unsqueeze(2)
                                     .to_broadcast([P, HEADS, HD]), ALU.mult).then_inc(stmp_ready, 1)
                    gp.wait_ge(xst_loaded, j * 16 + 16)
                    gp.wait_ge(ysc_ready, j)
                    gp.tensor_tensor(xD, xst, Dch[:, :].unsqueeze(2).to_broadcast([P, KT, P]), ALU.mult)\
                        .then_inc(xd_ready, 1)
                    gp.wait_ge(er_ready, j + 1)
                    for g in range(2):
                        hs = slice(8 * g, 8 * g + 8)
                        gp.tensor_tensor(ER[:, hs, :], ER[:, hs, :],
                                         BC[:, 2 + g:3 + g, bass.ds(j * P, P)].to_broadcast([P, 8, P]),
                                         ALU.mult).then_inc(ec_ready, 1)
                    gp.wait_ge(ysc_ready, j + 1)
                    gp.dma_start(y_d[KT:2 * KT, :, bass.ds(j * P, P)].rearrange("k p t -> p k t"), ysC)\
                        .then_inc(ysc_stored, 16)
                    gp.wait_ge(yl_ready, j + 1)
                    gp.dma_start(y_d[bass.ds(j, 1), :, :].rearrange("a p t -> (a p) t"), yl[:, 0:SEQ])\
                        .then_inc(yl_stored, 16)
                    gp.wait_ge(ysc_stored, j * 16 + 16)
                    gp.wait_ge(yl_stored, j * 16 + 16)
                    gp.sem_inc(pool_gate, 1)

                gp.wait_ge(vector_once, BCR_READY)
                gp.dma_start(bcs_d.rearrange("i (b n) -> b i n", b=DEC), bcr.rearrange("p (i n) -> p i n", i=4))\
                    .then_inc(bcr_stored, 16)
                gp.wait_ge(vector_once, EXD_READY)
                for k in range(KT):
                    gp.wait_ge(s0_loaded[k % 2], 16 * (k // 2 + 1))
                    if k >= 1:
                        gp.wait_ge(sn_ready, k)
                    gp.tensor_tensor(t1t, s0t[k % 2], exd[:, k, DEC:2 * DEC].unsqueeze(2).to_broadcast([P, DEC, P]),
                                     ALU.mult).then_inc(t1_ready, 1)


            def copy3(b):
                return PS[:, b:b + 3, 0:CH]

            @block.scalar
            def _(act):
                step = Chain(act, ac)
                act.wait_ge(c_loaded, 32)
                act.activation(cs, cin, ACT.Tanh, scale=0.5).then_inc(scalar_once, 1)
                act.wait_ge(vector_once, LAM_READY)
                act.activation(sm[:, 1, 0:8], sm[:, 0, 0:8], ACT.Exp, scale=-1.0).then_inc(scalar_once, 1)
                with act.Fori(0, 4) as i:
                    for b in range(2):
                        act.wait_ge(var_ready, i * 2 + (b + 1))
                        act.activation(rstd[:, :], mv[:, 1:2], ACT.Sqrt).then_inc(std_ready, 1)
                act.wait_ge(var_ready, 9)
                act.activation(rstd[0:DEC, :], mv[0:DEC, 1:2], ACT.Sqrt).then_inc(std_ready, 1)

                def conv_tile(b, r, t):
                    act.wait_ge(proj_mm[b], r + 1)
                    act.wait_ge(gpsimd_once, XB_ZEROED - 2)
                    act.wait_ge(conv_done[b], r)
                    act.activation(xb2[b][:, 3:3 + TE].rearrange("p (a t) -> p a t", a=3), copy3(3 * b),
                                   ACT.Copy).then_inc(px_copied[b], 1)
                    act.wait_ge(px_copied[b], r + 1)
                    rows = xb2[b][:, SEQ + 3:SEQ + 3 + 4 * DEC].rearrange("p (r k) -> p r k", k=4)
                    act.wait_ge(cur_ready[b], r + 1)
                    act.activation(rows[:, :, 0:3], cur2[b][:, 5:29].rearrange("p (r k) -> p r k", k=3),
                                   ACT.Copy).then_inc(hist_set[b], 1)
                    act.wait_ge(hist_set[b], r + 1)
                    act.activation(cso[:, bass.ds(t + KT, 1), 0:3].rearrange("p a k -> p (a k)"),
                                   xb2[b][:, SEQ:SEQ + 3], ACT.Copy).then_inc(al, 1)
                    act.activation(cso[:, bass.ds(t + KT, 1), 3:27].rearrange("p a (r k) -> p (a r) k", k=3),
                                   rows[:, :, 1:4], ACT.Copy).then_inc(al, 1)
                    act.wait_ge(al, t * 2 + 2)
                    act.wait_ge(conv_done[b], r + 1)
                    act.wait_ge(xo_ready[b], r)
                    act.activation(cth[b], cacc[b], ACT.Tanh).then_inc(cth_ready[b], 1)

                with act.Fori(0, 6) as i:
                    for b in range(2):
                        conv_tile(b, i, i * 2 + b)
                with act.Fori(0, 4) as i:
                    for b in range(2):
                        act.wait_ge(proj_mm[b], i + 7)
                        act.wait_ge(xo_ready[b], i + 6)
                        act.activation(cth[b].rearrange("p (a t) -> p a t", a=3), copy3(3 * b), ACT.Tanh,
                                       scale=0.5).then_inc(cth_ready[b], 1)
                act.wait_ge(vector_once, DTE_IN)
                act.activation(dtr[:, 6, :, :], dtr[:, 7, :, :], ACT.Exp, scale=-1.0).then_inc(scalar_once, 1)
                act.activation(dtb[:, 1, :], dtb[:, 1, :], ACT.Exp).then_inc(scalar_once, 1)
                act.wait_ge(vector_once, DXE_IN)
                act.activation(DXW[:, 0:NT, :], DXW[:, 0:NT, :], ACT.Exp).then_inc(scalar_once, 1)
                act.activation(CD[:, 0:NT, :], TOT[:, 0:NT, :], ACT.Exp).then_inc(scalar_once, 1)
                act.activation(CD[:, NT, :], DTA[:, NT, :], ACT.Exp).then_inc(scalar_once, 1)

                act.wait_ge(vector_once, BT_READY)
                act.wait_ge(xo_stored[0], 16 * 8)
                act.wait_ge(xo_stored[1], 16 * 8)
                with act.Fori(0, NT) as j:
                    act.wait_ge(r_loaded, j * 16 + 16)
                    act.wait_ge(y_mm, j)
                    act.activation(ER, Rb, ACT.Exp).then_inc(er_ready, 1)
                    act.wait_ge(seg_ready, j + 1)
                    act.activation(SEG, SEG, ACT.Exp).then_inc(segx_ready, 1)
                    act.wait_ge(proj_mm[0], j + 11)
                    act.wait_ge(xlc_ready, j)
                    act.wait_ge(gpsimd_once, XB_ZEROED)
                    act.activation(xbl[:, 3:3 + TE].rearrange("p (a t) -> p a t", a=3), copy3(0),
                                   ACT.Copy).then_inc(xl_copied, 1)
                    act.wait_ge(xl_copied, j + 1)
                    rows = xbl[:, SEQ + 3:SEQ + 3 + 4 * DEC].rearrange("p (r k) -> p r k", k=4)
                    act.wait_ge(cur_ready[0], j + 7)
                    act.activation(rows[:, :, 0:3], cur1[:, 18:42].rearrange("p (r k) -> p r k", k=3),
                                   ACT.Copy).then_inc(lhist_set, 1)
                    act.wait_ge(lhist_set, j + 1)
                    act.activation(cso[:, bass.ds(j, 1), 0:3].rearrange("p a k -> p (a k)"),
                                   xbl[:, SEQ:SEQ + 3], ACT.Copy).then_inc(al, 1)
                    act.activation(cso[:, bass.ds(j, 1), 3:27].rearrange("p a (r k) -> p (a r) k", k=3),
                                   rows[:, :, 1:4], ACT.Copy).then_inc(al, 1)
                    act.wait_ge(proj_mm[1], j + 11)
                    act.wait_ge(yl_ready, j)
                    act.activation(gl.rearrange("p (a t) -> p a t", a=3), copy3(3), ACT.Gelu_apprx_tanh)\
                        .then_inc(gl_ready, 1)
                    act.wait_ge(r_mm, j + 1)
                    act.activation(thr.rearrange("p (a t) -> p a t", a=3), copy3(0), ACT.Tanh, scale=0.5,
                                   bias=cur1[:, 5:6]).then_inc(thr_ready, 1)
                    act.wait_ge(thr_ready, j + 1)
                    act.wait_ge(yl_ready, j)
                    act.activation(lt, thr, ACT.Tanh, scale=cur1[:, 7:8], bias=cur1[:, 7:8]).then_inc(lt_ready, 1)
                    act.activation(la, thr, ACT.Exp, scale=cur1[:, 8:9], bias=cur1[:, 8:9]).then_inc(la_ready, 1)
                    act.wait_ge(la_ready, j + 1)
                    act.activation(la2, la, ACT.Square).then_inc(la2_ready, 1)
                    act.wait_ge(i_mm, j + 1)
                    act.activation(thi.rearrange("p (a t) -> p a t", a=3), copy3(3), ACT.Tanh, scale=0.5,
                                   bias=cur1[:, 6:7]).then_inc(thi_ready, 1)
                    act.wait_ge(ls_ready, j * 2 + 1)
                    act.activation(lt, lt, ACT.Sqrt, scale=0.25).then_inc(ls_ready, 1)
                act.wait_ge(tensor_once, CO_MM)
                for a in range(5):
                    step(act.activation(co[:, 512 * a:512 * a + 512], PS[0:27, a, :], ACT.Copy))
                act.wait_ge(tensor_once, HO_MM)
                act.activation(ho.rearrange("p (a n) -> p a n", a=2), PS[0:9, 5:7, :], ACT.Copy).then_inc(scalar_once, 1)
                act.sem_inc(scalar_once, 1)
                act.wait_ge(tensor_once, SO_MM)
                act.activation(So, PS[:, 0:2, :].rearrange("p a (k n) -> p (a k) n", n=P), ACT.Copy).then_inc(scalar_once, 1)


            @block.tensor
            def _(pe):
                pe.wait_ge(gpsimd_once, IDENT_MADE)

                pe.wait_ge(rows_loaded, 16 * 9)
                for k in range(KT):
                    mm = pe.transpose(PS[:, 4, 42 * k:42 * k + 42], prow[:, k * P:(k + 1) * P], ident[0:42, 0:42])
                mm.then_inc(tensor_once, 1)
                pe.wait_ge(rows2_loaded, 16 * 3)
                for k in range(XT):
                    mm = pe.transpose(PS[:, 5, 29 * k:29 * k + 29], prow2[:, k * P:(k + 1) * P], ident[0:29, 0:29])
                mm.then_inc(tensor_once, 1)
                pe.wait_ge(vector_once, CS_READY)
                for k in range(KT):
                    mm = pe.transpose(PS[:, 6, 9 * k:9 * k + 9], cs[:, k * P:(k + 1) * P], ident[0:9, 0:9])
                mm.then_inc(tensor_once, 1)
                pe.wait_ge(vector_once, CT_READY)

                def ada(b, r):
                    pe.wait_ge(adaw_loaded[b], r * 16 + 16)
                    pe.wait_ge(ada_ready[b], r)
                    for k in range(KT):
                        mm = pe.matmul(PS[0:9, b, :], cT[:, k, :], adaw[b][:, k, :], start=(k == 0), stop=(k == KT - 1))
                    mm.then_inc(ada_mm[b], 1)

                with pe.Fori(0, 2) as i:
                    for b in range(2):
                        ada(b, i)
                pe.wait_ge(vector_once, SC1_READY)
                pe.wait_ge(vector_once, PT_READY)
                for s in range(2):
                    for k in range(KT):
                        mm = pe.transpose(PS[:, 6, 72 + 9 * (s * KT + k):72 + 9 * (s * KT + k) + 9],
                                          mod[:, s * D + k * P:s * D + (k + 1) * P], ident[0:9, 0:9])
                mm.then_inc(tensor_once, 1)
                with pe.Fori(0, 4) as i:
                    for b in range(2):
                        ada(b, i + 2)
                        pe.wait_ge(xn_ready[b], i + 1)
                        pe.wait_ge(uT_ready[b], i)
                        for k in range(KT):
                            mm = pe.transpose(PS[:, 2 + 2 * b + k // 4, P * (k % 4):P * (k % 4) + P],
                                              xn[b][:, k * P:(k + 1) * P], ident[:, :])
                        mm.then_inc(xnT_mm[b], 1)
                pe.wait_ge(xn_ready[2], 1)
                pe.wait_ge(vector_once, SS_READY)
                for k in range(KT):
                    mm = pe.transpose(PS[:, 6, 8 * k:8 * k + 8], xn[0][0:DEC, k * P:(k + 1) * P], ident[0:DEC, 0:DEC])
                mm.then_inc(xnT_mm[2], 1)

                def project(b, w_round):
                    pe.wait_ge(w_loaded[b], w_round * 16 + 16)
                    for k in range(KT):
                        for a in range(3):
                            mm = pe.matmul(PS[:, 3 * b + a, 0:CH], wsl[b][:, k, :], uT[:, k, a * CH:(a + 1) * CH],
                                           start=(k == 0), stop=(k == KT - 1))
                    mm.then_inc(proj_mm[b], 1)

                for b in range(2):
                    pe.wait_ge(uT_ready[b], 4)
                pe.wait_ge(uT_ready[2], 1)
                with pe.Fori(0, 6) as i:
                    for b in range(2):
                        pe.wait_ge(px_copied[b], i)
                        project(b, i)
                with pe.Fori(0, 4) as i:
                    for b in range(2):
                        pe.wait_ge(xo_ready[b], i + 6)
                        project(b, i + 6)
                pe.wait_ge(small_loaded, 64)
                for t in range(NT + 1):
                    for k in range(KT):
                        lhs = uT[:, k, t * P:(t + 1) * P] if t < NT else uT[:, k, S0:TE:CONV]
                        rows = P if t < NT else DEC
                        mm = pe.matmul(PS[0:rows, 6, 128 + HEADS * t:128 + HEADS * (t + 1)], lhs, wdt[:, k, :],
                                       start=(k == 0), stop=(k == KT - 1))
                mm.then_inc(tensor_once, 1)
                pe.wait_ge(gpsimd_once, EX_MADE)
                for k in range(KT):
                    mm = pe.matmul(PS[:, 7, 384 + k:385 + k], EX[:, k, :], Dh[:, :], start=True, stop=True)
                mm.then_inc(tensor_once, 1)
                pe.wait_ge(xo_ready[0], 10)
                pe.wait_ge(xo_ready[1], 10)
                for c in range(NT):
                    for g in range(2):
                        n = 2 * c + g
                        mm = pe.matmul(PS[:, n // 4, P * (n % 4):P * (n % 4) + P], BC[:, g, c * P:(c + 1) * P],
                                       BC[:, 2 + g, c * P:(c + 1) * P], start=True, stop=True)
                mm.then_inc(tensor_once, 1)
                pe.wait_ge(vector_once, DTA_READY)
                pe.wait_ge(gpsimd_once, TRI_MADE)
                pe.matmul(PS[:, 7, 0:P], tri[:, :], DTA[:, 0:NT, :], start=True, stop=True)
                pe.matmul(PS[:, 7, P:2 * P], ones[:, :], DTA[:, 0:NT, :], start=True, stop=True).then_inc(tensor_once, 1)
                pe.wait_ge(vector_once, ACS_COPIED)
                pe.transpose(PS[:, 7, 2 * P:3 * P], ACS[:, 0:NT, :].rearrange("p c h -> p (c h)"), ident[:, :])\
                    .then_inc(tensor_once, 1)
                pe.wait_ge(vector_once, CB_READY)
                for c in range(NT):
                    for g in range(2):
                        n = 2 * c + g
                        mm = pe.transpose(PS[:, n // 4, P * (n % 4):P * (n % 4) + P], BC[:, g, c * P:(c + 1) * P],
                                          ident[:, :])
                mm.then_inc(tensor_once, 1)
                pe.wait_ge(vector_once, BT_READY)

                pe.wait_ge(vector_once, ACST_READY)
                with pe.Fori(0, NT) as j:
                    pe.wait_ge(xst_loaded, j * 16 + 16)
                    pe.wait_ge(ysc_ready, j)
                    for k in range(KT):
                        mm = pe.transpose(PS[:, 6 + k // 4, P * (k % 4):P * (k % 4) + P], xst[:, k, :], ident[:, :])
                    mm.then_inc(xt_mm, 1)
                    pe.wait_ge(thr_ready, j)
                    project(0, j + 10)
                    pe.wait_ge(xw_ready, j + 1)
                    pe.wait_ge(bst_ready, j + 1)
                    for g in range(2):
                        mm = pe.matmul(PS[:, 6 + g, :], bst[:, g, :],
                                       xw[:, 4 * g:4 * g + 4, :].rearrange("p k c -> p (k c)"), start=True, stop=True)
                    mm.then_inc(st_mm, 1)
                    pe.wait_ge(thi_ready, j)
                    project(1, j + 10)
                    pe.wait_ge(bd_loaded, j * 64 + 64)
                    pe.wait_ge(gpsimd_once, BD_ZEROED)
                    pe.wait_ge(xlc_ready, j + 1)
                    for a in range(3):
                        mm = pe.matmul(PS[:, a, 0:CH], BDa, xlc[:, a * CH:(a + 1) * CH], start=True, stop=True)
                    mm.then_inc(r_mm, 1)
                    pe.wait_ge(m_ready, j * 2 + 2)
                    pe.wait_ge(ec_ready, j * 2 + 2)
                    pe.wait_ge(sin_ready, j + 1)
                    pe.wait_ge(state_ready, j + 1)
                    for h in range(HEADS):
                        k, q = h // 2, HD * (h % 2)
                        dst = PS[q:q + HD, 6 + k // 4, P * (k % 4):P * (k % 4) + P]
                        pe.matmul(dst, xdt[:, k, q:q + HD], SEG[:, h, :], start=True, stop=False)
                        mm = pe.matmul(dst, Sin[:, k, q:q + HD], ER[:, h, :], start=False, stop=True)
                    mm.then_inc(y_mm, 1)
                    pe.wait_ge(gl_ready, j + 1)
                    for a in range(3):
                        mm = pe.matmul(PS[:, 3 + a, 0:CH], BDx, xlc[:, a * CH:(a + 1) * CH], start=True, stop=True)
                    mm.then_inc(i_mm, 1)
                pe.wait_ge(ysc_ready, NT)
                pe.wait_ge(thi_ready, NT)
                pe.wait_ge(scalar_once, DXE_READY)
                pe.transpose(PS[0:HEADS, 7, 0:DEC], DT[0:DEC, NT, :], ident[0:DEC, 0:DEC])
                pe.transpose(PS[0:HEADS, 7, DEC:2 * DEC], CD[0:DEC, NT, :], ident[0:DEC, 0:DEC]).then_inc(tensor_once, 1)
                for i in range(4):
                    mm = pe.transpose(PS[0:DEC, 6, P * i:P * (i + 1)], BC[:, i, S0:TE:CONV], ident[:, :])
                mm.then_inc(tensor_once, 1)
                pe.wait_ge(al, 2 * (NT + XT))
                for k in range(KT + XT):
                    mm = pe.transpose(PS[0:27, k // 4, P * (k % 4):P * (k % 4) + P], cso[:, k, :], ident[:, :])
                mm.then_inc(tensor_once, 1)
                pe.wait_ge(vector_once, DC_READY)
                for k in range(KT):
                    mm = pe.matmul(PS[:, 7, 64 + 16 * k:80 + 16 * k], EX[:, k, :], dcT, start=True, stop=True)
                mm.then_inc(tensor_once, 1)
                pe.wait_ge(ys_copied, NT)
                pe.wait_ge(vector_once, BCR_READY)
                for k in range(KT):
                    mm = pe.transpose(PS[0:9, 5 + k // 4, P * (k % 4):P * (k % 4) + P], hso[:, k, :], ident[:, :])
                mm.then_inc(tensor_once, 1)
                pe.wait_ge(scalar_once, CO_READY)
                for k in range(KT):
                    mm = pe.transpose(PS[:, k // 4, P * (k % 4):P * (k % 4) + P], Sst[:, k, :], ident[:, :])
                mm.then_inc(tensor_once, 1)


            @block.vector
            def _(ve):
                step = Chain(ve, vc)

                def log1p_exp_minus(out, x, z, s, s2, q):
                    step(ve.tensor_scalar(s, z, 2.0, None, ALU.add))
                    step(ve.reciprocal(s, s))
                    step(ve.tensor_tensor(s, s, z, ALU.mult))
                    step(ve.tensor_tensor(s2, s, s, ALU.mult))
                    step(ve.tensor_scalar(q, s2, 1.0 / 15, None, ALU.mult))
                    for c in (13, 11, 9, 7, 5, 3):
                        step(ve.scalar_tensor_tensor(out=q, in0=q, scalar=1.0 / c, in1=s2, op0=ALU.add, op1=ALU.mult))
                    step(ve.scalar_tensor_tensor(out=q, in0=q, scalar=1.0, in1=s, op0=ALU.add, op1=ALU.mult))
                    step(ve.tensor_scalar(out, x, 0.0, None, ALU.max))
                    step(ve.scalar_tensor_tensor(out=out, in0=q, scalar=2.0, in1=out, op0=ALU.mult, op1=ALU.add))

                ve.wait_ge(scalar_once, CSIG_READY)
                ve.scalar_tensor_tensor(out=cs, in0=cs, scalar=1.0, in1=cin, op0=ALU.add, op1=ALU.mult)\
                    .then_inc(vector_once, 1)
                ve.wait_ge(tensor_once, PT1_MM)
                step(ve.tensor_copy(PT1[:, :, :], PS[:, 4, 0:42 * KT].rearrange("p (k c) -> p k c", k=KT)))
                ve.wait_ge(tensor_once, PT2_MM)
                step(ve.tensor_copy(PT2[:, :, :], PS[:, 5, 0:29 * XT].rearrange("p (k c) -> p k c", k=XT)))
                ve.tensor_scalar(PT1[:, :, 5:7], PT1[:, :, 5:7], 0.5, None, ALU.mult).then_inc(vector_once, 1)
                ve.tensor_scalar(PT2[:, :, 0:5], PT2[:, :, 0:5], 0.5, None, ALU.mult).then_inc(vector_once, 1)
                ve.wait_ge(tensor_once, CT_MM)
                ve.tensor_scalar(cT[:, :, :], PS[:, 6, 0:72].rearrange("p (k c) -> p k c", k=KT), 0.5, None, ALU.mult)\
                    .then_inc(vector_once, 1)
                lamv = [sm[:, i, 0:8] for i in range(6)]
                step(ve.tensor_scalar(lamv[2], PT1[:, :, 7], -1.0, None, ALU.mult))
                ve.tensor_tensor(lamv[0], lamv[2], PT1[:, :, 7], ALU.max).then_inc(vector_once, 1)
                ve.wait_ge(scalar_once, LAMEXP)
                log1p_exp_minus(lamv[0], lamv[2], lamv[1], lamv[3], lamv[4], lamv[5])
                step(ve.tensor_scalar(spl[:, :, 0], lamv[0], LRU_C / 2, None, ALU.mult))
                step(ve.tensor_scalar(spl[:, :, 1], lamv[0], -LRU_C / 2, None, ALU.mult))

                def normalise(src, dst, rows, n, done):
                    st = Chain(ve, vl, n * 4)
                    for h in range(2):
                        st(ve.bn_stats(stat[0:rows, 6 * h:6 * h + 6], src[0:rows, 512 * h:512 * h + 512]))
                    ve.sem_inc(vector_gate, 1)
                    st(ve.bn_aggr(mv[0:rows, :], stat[0:rows, :].rearrange("p (a s) -> p a s", a=2)))
                    ve.tensor_scalar(mv[0:rows, 1:2], mv[0:rows, 1:2], LN_EPS, None, ALU.add).then_inc(var_ready, 1)
                    ve.wait_ge(std_ready, n + 1)
                    st(ve.reciprocal(rstd[0:rows, :], rstd[0:rows, :]))
                    ve.tensor_scalar(dst[0:rows, :], src[0:rows, :], mv[0:rows, 0:1], rstd[0:rows, :],
                                     ALU.subtract, ALU.mult).then_inc(done, 1)

                def ada_out(b, r, chunk):
                    ve.wait_ge(ada_mm[b], r + 1)
                    part = bass.ds(chunk * 512, 512)
                    ve.tensor_tensor(mod[:, part], PS[0:9, b, :], bada[:, part], ALU.add).then_inc(ada_ready[b], 1)

                ve.wait_ge(bada_loaded, 16)
                with ve.Fori(0, 2) as i:
                    for b in range(2):
                        ada_out(b, i, i * 2 + b)
                for b in range(2):
                    ve.wait_ge(ada_ready[b], 2)
                ve.tensor_scalar(mod[:, D:2 * D], mod[:, D:2 * D], 1.0, None, ALU.add).then_inc(vector_once, 1)
                ve.wait_ge(tensor_once, SS_MM)
                ve.tensor_copy(ssT[:, :, :, :], PS[:, 6, 72:216].rearrange("p (s k c) -> p s k c", s=2, k=KT))\
                    .then_inc(vector_once, 1)
                ve.wait_ge(gpsimd_once, UZ)
                ve.wait_ge(vector_once, SS_READY)
                with ve.Fori(0, 4) as i:
                    for b in range(2):
                        ve.wait_ge(xt_loaded[b], i * 16 + 16)
                        ve.wait_ge(xnT_mm[b], i)
                        normalise(xt[b], xn[b], P, i * 2 + b, xn_ready[b])
                        ada_out(b, i + 2, i * 2 + (4 + b))
                        ve.wait_ge(xnT_mm[b], i + 1)
                        ve.tensor_tensor(ltmp, PS[:, 2 + 2 * b:4 + 2 * b, :].rearrange("p a (k t) -> p (a k) t", t=P),
                                         ssT[:, 1, :, 0:1].to_broadcast([P, KT, P]), ALU.mult).then_inc(ltmp_ready, 1)
                        ve.wait_ge(ltmp_ready, i * 2 + (b + 1))
                        ve.tensor_tensor(uT[:, :, bass.ds((i * 2 + b) * P, P)], ltmp,
                                         ssT[:, 0, :, 0:1].to_broadcast([P, KT, P]), ALU.add).then_inc(uT_ready[b], 1)
                ve.wait_ge(xt_loaded[2], 16)
                ve.wait_ge(xnT_mm[0], 4)
                normalise(xt[0], xn[0], DEC, 8, xn_ready[2])
                ve.wait_ge(xnT_mm[2], 1)
                step(ve.tensor_tensor(ltmp[:, :, 0:DEC], PS[:, 6, 0:64].rearrange("p (k t) -> p k t", k=KT),
                                      ssT[:, 1, :, 1:9], ALU.mult))
                ve.tensor_tensor(uT[:, :, S0:TE:CONV], ltmp[:, :, 0:DEC], ssT[:, 0, :, 1:9], ALU.add)\
                    .then_inc(uT_ready[2], 1)
                ve.wait_ge(ada_ready[0], 6)
                ve.wait_ge(ada_ready[1], 6)
                ve.tensor_scalar(mod[:, 4 * D:5 * D], mod[:, 4 * D:5 * D], 1.0, None, ALU.add).then_inc(vector_once, 1)

                def conv(out, row, cur, st, done):
                    st(ve.tensor_scalar(out, row[:, 0:TE], cur[:, 0:1], cur[:, 4:5], ALU.mult, ALU.add))
                    for k in (1, 2):
                        st(ve.scalar_tensor_tensor(out=out, in0=row[:, k:k + TE], scalar=cur[:, k:k + 1], in1=out,
                                                   op0=ALU.mult, op1=ALU.add))
                    ve.scalar_tensor_tensor(out=out, in0=row[:, 3:3 + TE], scalar=cur[:, 3:4], in1=out,
                                            op0=ALU.mult, op1=ALU.add).then_inc(done, 1)

                def conv_tile(b, r, t, out):
                    ve.tensor_copy(cur2[b][:, :], PT2[:, bass.ds(t, 1), :].rearrange("p a c -> p (a c)"))\
                        .then_inc(cur_ready[b], 1)
                    ve.wait_ge(cur_ready[b], r + 1)
                    ve.wait_ge(hist_set[b], r + 1)
                    ve.wait_ge(al, t * 2 + 2)
                    conv(cacc[b], xb2[b], cur2[b], Chain(ve, vl, t * 3 + 36), conv_done[b])
                    ve.wait_ge(conv_done[b], r + 1)
                    ve.wait_ge(cth_ready[b], r + 1)
                    ve.scalar_tensor_tensor(out=out, in0=cth[b], scalar=1.0, in1=cacc[b], op0=ALU.add, op1=ALU.mult)\
                        .then_inc(xo_ready[b], 1)

                with ve.Fori(0, 4) as i:
                    for b in range(2):
                        ve.wait_ge(xo_stored[b], i * 16)
                        conv_tile(b, i, i * 2 + b, xo[b])
                with ve.Fori(0, 2) as i:
                    for b in range(2):
                        conv_tile(b, i + 4, i * 2 + (8 + b),
                                  BC[:, bass.ds(i * 2 + b, 1), :].rearrange("p a t -> p (a t)"))
                with ve.Fori(0, 4) as i:
                    for b in range(2):
                        ve.wait_ge(cth_ready[b], i + 7)
                        ve.wait_ge(xo_stored[b], i * 16 + 64)
                        ve.scalar_tensor_tensor(out=xo[b].rearrange("p (a t) -> p a t", a=3),
                                                in0=cth[b].rearrange("p (a t) -> p a t", a=3), scalar=1.0, in1=copy3(3 * b),
                                                op0=ALU.add, op1=ALU.mult).then_inc(xo_ready[b], 1)

                ve.wait_ge(tensor_once, DT_MM)
                raw, az, s1, s2, q1 = dtr[:, 2, :, :], dtr[:, 7, :, :], dtr[:, 3, :, :], dtr[:, 4, :, :], dtr[:, 5, :, :]
                step(ve.memset(raw, 0.0))
                step(ve.tensor_tensor(raw[:, 0:NT, :], PS[:, 6, 128:256].rearrange("p (t h) -> p t h", h=HEADS),
                                      dtb[:, 0:1, :].to_broadcast([P, NT, HEADS]), ALU.add))
                step(ve.tensor_tensor(raw[0:DEC, NT, :], PS[0:DEC, 6, 256:272], dtb[0:DEC, 0, :], ALU.add))
                step(ve.tensor_scalar(az, raw, -1.0, None, ALU.mult))
                ve.tensor_tensor(az, az, raw, ALU.max).then_inc(vector_once, 1)
                ve.wait_ge(scalar_once, DT_EXP)
                log1p_exp_minus(DT, raw, dtr[:, 6, :, :], s1, s2, q1)
                ve.scalar_tensor_tensor(out=DTA, in0=DT, scalar=-1.0, in1=dtb[:, 1:2, :].to_broadcast([P, NT + 1, HEADS]),
                                        op0=ALU.mult, op1=ALU.mult).then_inc(vector_once, 1)
                ve.wait_ge(tensor_once, CB_MM)
                ve.wait_ge(mod_stored, 16)
                ve.wait_ge(gpsimd_once, TRI_MADE)
                ve.tensor_tensor(CBm.rearrange("p c g l -> p (c g) l"),
                                 PS[:, 0:4, :].rearrange("p a (n l) -> p (a n) l", l=P),
                                 tri[:, :].unsqueeze(1).to_broadcast([P, 2 * NT, P]), ALU.mult).then_inc(vector_once, 1)
                ve.wait_ge(tensor_once, ACS_MM)
                ve.tensor_copy(ACS[:, 0:NT, :], PS[:, 7, 0:P].rearrange("p (c h) -> p c h", h=HEADS))\
                    .then_inc(vector_once, 1)
                ve.tensor_copy(TOT[:, 0:NT, :], PS[:, 7, P:2 * P].rearrange("p (c h) -> p c h", h=HEADS))\
                    .then_inc(vector_once, 1)
                ve.wait_ge(vector_once, ACS_COPIED)
                ve.tensor_tensor(DXW[:, 0:NT, :], TOT[:, 0:NT, :], ACS[:, 0:NT, :], ALU.subtract).then_inc(vector_once, 1)
                ve.wait_ge(tensor_once, ACST_MM)
                ve.tensor_copy(acsT, PS[:, 7, 2 * P:3 * P]).then_inc(vector_once, 1)
                ve.wait_ge(tensor_once, DCH_MM)
                step(ve.tensor_copy(Dch[:, :], PS[:, 7, 384:384 + KT]))
                ve.wait_ge(scalar_once, DXE_READY)
                step(ve.tensor_tensor(DXW[:, 0:NT, :], DXW[:, 0:NT, :], DT[:, 0:NT, :], ALU.mult))
                ve.wait_ge(tensor_once, BT_MM)
                ve.tensor_copy(Btok.rearrange("p c g n -> p (c g) n"),
                               PS[:, 0:4, :].rearrange("p a (n l) -> p (a n) l", l=P)).then_inc(vector_once, 1)

                ve.wait_ge(gpsimd_once, XB_ZEROED)
                ve.wait_ge(xo_stored[0], 16 * 8)
                ve.wait_ge(xo_stored[1], 16 * 8)

                def per_head(x, j):
                    return x[:, bass.ds(j, 1), :].rearrange("p a h -> p (a h)").unsqueeze(2)

                def heads(x):
                    return x.rearrange("p k (h q) -> p (k h) q", h=2)

                with ve.Fori(0, NT) as j:
                    st = Chain(ve, vl, j * 14 + 72)
                    ve.wait_ge(thi_ready, j)
                    st(ve.tensor_copy(cur1[:, :], PT1[:, bass.ds(j, 1), :].rearrange("p a c -> p (a c)")))
                    ve.tensor_copy(cur1[:, 7:9], spl[:, bass.ds(j, 1), :].rearrange("p a c -> p (a c)"))\
                        .then_inc(cur_ready[0], 1)
                    st(ve.tensor_copy(acur[:, :], ACS[:, bass.ds(j, 1), :].rearrange("p a h -> p (a h)")))
                    ve.wait_ge(r_loaded, j * 16 + 16)
                    ve.wait_ge(y_mm, j)
                    for h in range(HEADS):
                        ins = ve.tensor_scalar(SEG[:, h, :], Rb[:, h, :], acur[:, h:h + 1], 0.0, ALU.subtract, ALU.min)
                    ins.then_inc(seg_ready, 1)
                    ve.wait_ge(xt_mm, j + 1)
                    xps = PS[:, 6:8, :].rearrange("p a (h q) -> p (a h) q", q=HD)
                    st(ve.tensor_tensor(heads(xdt), xps, per_head(DT, j).to_broadcast([P, HEADS, HD]), ALU.mult))
                    ve.tensor_tensor(heads(xw), xps, per_head(DXW, j).to_broadcast([P, HEADS, HD]), ALU.mult)\
                        .then_inc(xw_ready, 1)
                    ve.wait_ge(segx_ready, j + 1)
                    for g in range(2):
                        ve.tensor_tensor(SEG[:, 8 * g:8 * g + 8, :], SEG[:, 8 * g:8 * g + 8, :],
                                         CBm[:, bass.ds(j, 1), g, :].to_broadcast([P, 8, P]),
                                         ALU.mult).then_inc(m_ready, 1)
                    ve.wait_ge(lhist_set, j + 1)
                    ve.wait_ge(al, j * 2 + 26)
                    ve.wait_ge(cur_ready[0], j + 7)
                    conv(xlc, xbl, cur1, st, xlc_ready)
                    ve.wait_ge(st_mm, j + 1)
                    ve.wait_ge(stmp_ready, j + 1)
                    ve.tensor_tensor(Sst, stmp, PS[:, 6:8, :].rearrange("p a (k c) -> p (a k) c", c=P), ALU.add)\
                        .then_inc(state_ready, 1)
                    ve.wait_ge(y_mm, j + 1)
                    ve.wait_ge(xd_ready, j + 1)
                    ve.wait_ge(zst_loaded, j * 16 + 16)
                    ve.wait_ge(ysc_stored, j * 16)
                    st(ve.tensor_tensor(ysC, xD, PS[:, 6:8, :].rearrange("p a (k c) -> p (a k) c", c=P), ALU.add))
                    ve.scalar_tensor_tensor(out=ysC, in0=ysC, scalar=0.5, in1=zst, op0=ALU.mult, op1=ALU.mult)\
                        .then_inc(ysc_ready, 1)
                    ve.wait_ge(la2_ready, j + 1)
                    ve.scalar_tensor_tensor(out=lt, in0=la2, scalar=1.0, in1=lt, op0=ALU.add, op1=ALU.mult)\
                        .then_inc(ls_ready, 1)
                    ve.wait_ge(thi_ready, j + 1)
                    st(ve.scalar_tensor_tensor(out=thi, in0=thi, scalar=1.0, in1=xlc, op0=ALU.add, op1=ALU.mult))
                    ve.wait_ge(ls_ready, j * 2 + 2)
                    st(ve.tensor_tensor(lt, lt, thi, ALU.mult))
                    st(ve.memset(la[:, S0 - 1:TE:CONV], 0.0))
                    st(ve.tensor_copy(lt[:, S0 - 1:TE:CONV], cur1[:, 10:18]))
                    st(ve.tensor_tensor_scan(thr, la, lt, 0.0, ALU.mult, ALU.add))
                    st(ve.tensor_copy(hso[:, bass.ds(j, 1), 0:1].rearrange("p a c -> p (a c)"), thr[:, SEQ - 1:SEQ]))
                    st(ve.tensor_copy(hso[:, bass.ds(j, 1), 1:9].rearrange("p a c -> p (a c)"), thr[:, S0:TE:CONV]))
                    ve.wait_ge(gl_ready, j + 1)
                    ve.wait_ge(yl_stored, j * 16)
                    ve.tensor_tensor(yl, thr, gl, ALU.mult).then_inc(yl_ready, 1)
                    ve.wait_ge(yl_ready, j + 1)
                    ve.tensor_copy(yS[:, bass.ds(j, 1), :].rearrange("p a c -> p (a c)"), yl[:, S0:TE:CONV])\
                        .then_inc(ys_copied, 1)
                    assert st.n == 14, st.n
                ve.wait_ge(ys_copied, NT)

                ve.wait_ge(tensor_once, DC_MM)
                ve.tensor_copy(dcT, PS[0:HEADS, 7, 0:2 * DEC]).then_inc(vector_once, 1)
                ve.wait_ge(tensor_once, BCR_MM)
                ve.tensor_copy(bcr, PS[0:DEC, 6, :]).then_inc(vector_once, 1)
                ve.wait_ge(tensor_once, EX_MM)
                ve.tensor_copy(exd, PS[:, 7, 64:192].rearrange("p (k c) -> p k c", k=KT)).then_inc(vector_once, 1)
                ve.wait_ge(vector_once, EXD_READY)
                ve.wait_ge(xzs_loaded, 32)
                step(ve.tensor_tensor(xdS, xzs[:, 0, :, CONV - 1:4 * DEC:CONV], exd[:, :, 0:DEC], ALU.mult))
                ve.wait_ge(bcs_loaded, 16)
                for k in range(KT):
                    g = k // 4
                    step(ve.tensor_tensor(t2t, bcsb[:, g, :].rearrange("p (b n) -> p b n", b=DEC),
                                          xdS[:, k, :].unsqueeze(2).to_broadcast([P, DEC, P]), ALU.mult))
                    ve.wait_ge(t1_ready, k + 1)
                    if k >= 2:
                        ve.wait_ge(sn_stored[k % 2], 16 * (k // 2))
                    ve.tensor_tensor(snt[k % 2], t1t, t2t, ALU.add).then_inc(sn_ready, 1)
                    ve.wait_ge(sn_ready, k + 1)
                    step(ve.tensor_tensor(t2t, snt[k % 2], bcsb[:, 2 + g, :].rearrange("p (b n) -> p b n", b=DEC),
                                          ALU.mult))
                    step(ve.tensor_reduce(yr[:, k, :], t2t, AX.X, ALU.add))
                xdD = xdS
                step(ve.tensor_tensor(xdD, xzs[:, 0, :, CONV - 1:4 * DEC:CONV],
                                      Dch[:, :].unsqueeze(2).to_broadcast([P, KT, DEC]), ALU.mult))
                step(ve.tensor_tensor(yr, yr, xdD, ALU.add))
                ve.scalar_tensor_tensor(out=yS[:, KT:2 * KT, :], in0=yr, scalar=0.5,
                                        in1=xzs[:, 1, :, CONV - 1:4 * DEC:CONV], op0=ALU.mult, op1=ALU.mult)\
                    .then_inc(vector_once, 1)


        nc.clear_and_free_semaphores(in_first)
        nc.all_engine_barrier()

        def sem(name):
            return ctx.enter_context(nc.semaphore("b_" + name))

        pool_gate = sem("pool_gate")
        icur_ready = sem("icur_ready")
        eT_mm = sem("eT_mm")
        xe_ready = sem("xe_ready")
        hth_ready = sem("hth_ready")
        h_ready = sem("h_ready")
        h1_ready = sem("h1_ready")
        hT_mm = sem("hT_mm")
        hT_ready = sem("hT_ready")
        yo_ready = sem("yo_ready")
        sl_ready = sem("sl_ready")
        zero_made = sem("zero_made")
        zeros_stored = sem("zeros_stored")
        rows2n_loaded = sem("rows2n_loaded")
        fo_ready = sem("fo_ready")
        gcur_ready = sem("gcur_ready")
        wg_loaded = [sem(f"wg_loaded{b}") for b in range(2)]
        wu_loaded = [sem(f"wu_loaded{b}") for b in range(2)]
        wd_loaded = [sem(f"wd_loaded{b}") for b in range(2)]
        gate_mm = [sem(f"gate_mm{b}") for b in range(2)]
        up_mm = [sem(f"up_mm{b}") for b in range(2)]
        down_mm = [sem(f"down_mm{b}") for b in range(2)]
        xg_loaded = [sem(f"xg_loaded{b}") for b in range(2)]
        yo_stored = [sem(f"yo_stored{b}") for b in range(2)]
        y12_used = [sem(f"y12_used{b}") for b in range(2)]
        y12_loaded = [sem(f"y12_loaded{b}") for b in range(3)]
        xl2_loaded = [sem(f"xl2_loaded{b}") for b in range(3)]
        fo_stored = [sem(f"fo_stored{b}") for b in range(3)]
        fl = sem("row_tile_step")
        wo_loaded = sem("wo_loaded")
        xr_used = sem("xr_used")
        wog_ready = sem("wog_ready")
        rows1_loaded = sem("rows1_loaded")
        ysq_ready = sem("ysq_ready")
        pa_mm = sem("pa_mm")
        pb_mm = sem("pb_mm")
        ssq_mm = sem("ssq_mm")
        rsv_ready = sem("rsv_ready")
        rstd_ready = sem("rstd_ready")
        pa_read = sem("pa_read")
        pb_read = sem("pb_read")
        lnv_ready = sem("lnv_ready")
        lns_ready = sem("lns_ready")
        xp1_ready = sem("xp1_ready")
        v_ready = sem("v_ready")
        wr_loaded = sem("wr_loaded")
        vt_mm = sem("vt_mm")
        vT_ready = sem("vT_ready")
        lg_mm = sem("lg_mm")
        tok_scattered = sem("tok_scattered")
        tokr_loaded = sem("tokr_loaded")
        y_loaded = [sem(f"y_loaded{b}") for b in range(3)]
        xr_loaded = [sem(f"xr_loaded{b}") for b in range(3)]
        xp1_stored = [sem(f"xp1_stored{b}") for b in range(3)]
        v_stored = [sem(f"v_stored{b}") for b in range(3)]
        vs_loaded = [sem(f"vs_loaded{b}") for b in range(3)]
        vector_gate = sem("vector_gate")
        vc = sem("vector_step")
        tensor_once = sem("tensor_once")
        (RANK_MM, TOKT_MM) = \
            (1, 2)
        vector_once = sem("vector_once")
        (RSEL_READY, A_READY, RANK_READY, SLOTS_READY, CTL_READY, TOKF_READY, IDX_READY) = \
            (2, 4, 5, 7, 8, 9, 10)
        scalar_once = sem("scalar_once")
        (REXP_READY,) = \
            (2,)
        gpsimd_once = sem("gpsimd_once")
        (AM_READY,) = \
            (2,)

        with nc.Block() as block:
            @block.sync
            def _(sp):

                wo_t = w_out[0].rearrange("(s k p) n -> s p k n", s=2, p=P)

                sp.dma_start(WO[0], wo_t[0]).then_inc(wo_loaded, 16)

                def load_y(t, b):
                    sp.dma_start(ysl[b], y_d[:, :, bass.ds(t * P, P)].rearrange("k p t -> p k t")).then_inc(y_loaded[b], 16)

                for b in range(2):
                    load_y(b, b)
                sp.dma_start(WO[1], wo_t[1]).then_inc(wo_loaded, 16)
                for dst, src in ((gate1, mod_d[0:1, 2 * D:3 * D]), (ln1g, ln1_g), (ln1b, ln1_b),
                                 (sc2, mod_d[0:1, 4 * D:5 * D]), (sh2, mod_d[0:1, 3 * D:4 * D])):
                    sp.dma_start(dst, src.to_broadcast([P, D])).then_inc(rows1_loaded, 16)
                for b in range(2):
                    sp.dma_start(xr[b], x_prompt[0, b * P:(b + 1) * P, :]).then_inc(xr_loaded[b], 16)
                for dst, src in ((wr[:, :, 0:NG], w_rg[0]), (wr[:, :, NG:NG + NE], w_re[0])):
                    sp.dma_start(dst, src.rearrange("(k p) n -> p k n", p=P)).then_inc(wr_loaded, 16)
                sp.dma_start(brb[:, 0:NG], b_rg.to_broadcast([P, NG])).then_inc(wr_loaded, 16)
                sp.dma_start(brb[:, NG:NG + NE], b_re.to_broadcast([P, NE])).then_inc(wr_loaded, 16)
                def load_gu(e, b):
                    sp.dma_start(wg[b], w_gate[0, bass.ds(e, 1), :, :].rearrange("a (p c) f -> (a p) c f", c=KT))\
                        .then_inc(wg_loaded[b], 16)

                def load_up(e, b):
                    sp.dma_start(wu[b], w_up[0, bass.ds(e, 1), :, :].rearrange("a (p c) f -> (a p) c f", c=KT))\
                        .then_inc(wu_loaded[b], 16)

                def load_down(e, b):
                    sp.dma_start(wd[b], w_down[0, bass.ds(e, 1), :, :].rearrange("a (p c) n -> (a p) c n", c=FF // P))\
                        .then_inc(wd_loaded[b], 16)

                load_gu(0, 0)
                load_up(0, 0)
                with sp.Fori(0, 3) as i:
                    for b in range(2):
                        sp.wait_ge(ssq_mm, i * 2 + (b + 1))
                        sp.wait_ge(pb_mm, i * 2 + (b + 1))
                        load_y(i * 2 + (2 + b), b)
                        sp.wait_ge(xr_used, i * 2 + (b + 1))
                        sp.dma_start(xr[b], x_prompt[0, bass.ds((i * 2 + (2 + b)) * P, P), :]).then_inc(xr_loaded[b], 16)
                sp.wait_ge(xr_used, 7)
                sp.dma_start(xr[0][0:DEC, :], x_sample[:, 0, :]).then_inc(xr_loaded[2], 16)
                sp.wait_ge(v_ready, NT)
                for dst, m in ((gate1, 2), (sc2, 4), (sh2, 3)):
                    sp.dma_start(dst[0:DEC, :], mod_d[1:9, m * D:(m + 1) * D]).then_inc(rows1_loaded, 16)

                for b in range(2):
                    sp.wait_ge(v_stored[b], 16 * 4)
                sp.wait_ge(v_ready, NT + 1)
                sp.wait_ge(xp1_ready, NT + 1)
                for b in range(2):
                    sp.dma_start(vsl[b], v_d[b * P:(b + 1) * P, :]).then_inc(vs_loaded[b], 16)
                load_down(0, 0)
                sp.wait_ge(ssq_mm, NTT)
                sp.wait_ge(pb_mm, NTT)
                load_gu(1, 1)
                load_up(1, 1)
                with sp.Fori(0, 3) as i:
                    for b in range(2):
                        sp.wait_ge(vt_mm, i * 2 + (b + 1))
                        sp.dma_start(vsl[b], v_d[bass.ds((i * 2 + (2 + b)) * P, P), :]).then_inc(vs_loaded[b], 16)
                sp.wait_ge(vt_mm, 7)
                sp.wait_ge(v_stored[2], 16)
                sp.dma_start(vsl[0][0:DEC, :], v_d[SEQ:SEQ + DEC, :]).then_inc(vs_loaded[2], 16)
                sp.wait_ge(tok_scattered, 16 * 2 * NTT)
                sp.dma_start(tokr, tok_d.rearrange("(b p) a -> b (p a)", p=P)).then_inc(tokr_loaded, 16)
                load_down(1, 1)
                with sp.Fori(0, NE // 2 - 1) as i:
                    for b in range(2):
                        sp.wait_ge(gate_mm[b], i + 1)
                        load_gu(i * 2 + (2 + b), b)
                        sp.wait_ge(up_mm[b], i + 1)
                        load_up(i * 2 + (2 + b), b)
                        sp.wait_ge(down_mm[b], i + 1)
                        load_down(i * 2 + (2 + b), b)
                sp.wait_ge(vector_once, CTL_READY)
                n_extra = sp.value_load(ctl[0:1, NOV:NOV + 1], min_val=0, max_val=NOV)
                with sp.If(n_extra > 0):
                    with sp.Fori(0, n_extra) as q:
                        e = sp.value_load(ctl[0:1, bass.ds(q, 1)], min_val=0, max_val=NE - 1)
                        sp.wait_ge(down_mm[0], q + NE // 2)
                        load_gu(e, 0)
                        load_up(e, 0)
                        load_down(e, 0)
                for dst, src in ((gate2, mod_d[0:1, 5 * D:6 * D]), (ln2g, ln2_g), (ln2b, ln2_b)):
                    sp.dma_start(dst, src.to_broadcast([P, D])).then_inc(rows2n_loaded, 16)
                sp.wait_ge(down_mm[0], n_extra + NE // 2)
                sp.wait_ge(down_mm[1], NE // 2)
                for b in range(2):
                    sp.wait_ge(xp1_stored[b], 64)
                for b in range(2):
                    sp.dma_start(xl2[b], xp1_d[b * P:(b + 1) * P, :]).then_inc(xl2_loaded[b], 16)
                def store_y(t, b):
                    sp.wait_ge(fo_ready, t + 1)
                    sp.dma_start(y_prompt[0, bass.ds(t * P, P), :], fo[b]).then_inc(fo_stored[b], 16)

                with sp.Fori(0, NT // 2 - 1) as i:
                    for b in range(2):
                        store_y(i * 2 + b, b)
                        sp.dma_start(xl2[b], xp1_d[bass.ds((i * 2 + (2 + b)) * P, P), :]).then_inc(xl2_loaded[b], 16)
                for b in range(2):
                    store_y(NT - 2 + b, b)
                sp.wait_ge(xp1_stored[2], 16)
                sp.dma_start(xl2[0][0:DEC, :], xp1_d[SEQ:SEQ + DEC, :]).then_inc(xl2_loaded[2], 16)
                sp.dma_start(gate2[0:DEC, :], mod_d[1:9, 5 * D:6 * D]).then_inc(rows2n_loaded, 16)
                sp.wait_ge(fo_ready, NTT)
                sp.dma_start(y_sample[:, 0, :], fo[0][0:DEC, :]).then_inc(fo_stored[2], 16)
                for b in range(2):
                    sp.wait_ge(fo_stored[b], 16 * (NT // 2))
                sp.wait_ge(fo_stored[2], 16)

            @block.gpsimd
            def _(gp):

                def store(t, b, rows, r16):
                    gp.wait_ge(xp1_ready, t + 1)
                    gp.sem_inc(pool_gate, 1)
                    gp.dma_start(xp1_d[bass.ds(t * P, rows), :], xp1[b % 2][0:rows, :]).then_inc(xp1_stored[b], 16)
                    gp.wait_ge(v_ready, t + 1)
                    gp.sem_inc(pool_gate, 1)
                    gp.dma_start(v_d[bass.ds(t * P, rows), :], vb[b % 2][0:rows, :]).then_inc(v_stored[b], 16)
                    gp.wait_ge(xp1_stored[b], r16)
                    gp.wait_ge(v_stored[b], r16)
                    gp.sem_inc(pool_gate, 1)

                with gp.Fori(0, 4) as i:
                    for b in range(2):
                        store(i * 2 + b, b, P, i * 16 + 16)
                store(NT, 2, DEC, 16)
                gp.wait_ge(vector_once, A_READY)
                for a in range(2):
                    gp.affine_select(out=gtmp[a], in_=gtmp[a], compare_op=ALU.is_ge, fill=0.0, base=SEQ + DEC - 1,
                                     pattern=[[-P, NTT], [0, NE]], channel_multiplier=-1).then_inc(gpsimd_once, 1)
                gp.wait_ge(vector_once, SLOTS_READY)
                for t in range(NTT):
                    rows = P if t < NT else DEC
                    for a in range(2):
                        gp.indirect_dma_start(tok_d, bass.IndirectOffsetOnAxis(ap=slot[0:rows, a, t:t + 1], axis=0),
                                              tokid[0:rows, t:t + 1], None).then_inc(tok_scattered, 16)

                gp.wait_ge(vector_once, IDX_READY)
                gp.wait_ge(v_stored[2], 16)

                def gather(e, b, r):
                    gp.wait_ge(xg_loaded[b], r * 16)
                    gp.sem_inc(pool_gate, 1)
                    gp.tensor_copy(icur[b][:, :], idxT[:, bass.ds(e, 1)]).then_inc(icur_ready, 1)
                    gp.wait_ge(icur_ready, e + 1)
                    gp.sem_inc(pool_gate, 1)
                    gp.indirect_dma_start(xg[b], None, v_d, bass.IndirectOffsetOnAxis(ap=icur[b][:, :], axis=0))\
                        .then_inc(xg_loaded[b], 16)

                for b in range(2):
                    gather(b, b, 0)
                with gp.Fori(0, NE // 2 - 1) as i:
                    for b in range(2):
                        gp.wait_ge(eT_mm, i * 2 + (b + 1))
                        gather(i * 2 + (2 + b), b, i + 1)
                n_extra = gp.value_load(ctl[0:1, NOV:NOV + 1], min_val=0, max_val=NOV)
                with gp.If(n_extra > 0):
                    with gp.Fori(0, n_extra) as q:
                        gp.wait_ge(eT_mm, q + NE)
                        gather(q + NE, 0, q + NE // 2)

                gp.wait_ge(yo_stored[1], 16 * (NE // 2))
                gp.wait_ge(yo_stored[0], n_extra * 16 + 16 * (NE // 2))
                gp.sem_inc(pool_gate, 1)

                def take(src, t, b, r, rows, done):
                    gp.wait_ge(y12_used[b], r)
                    gp.sem_inc(pool_gate, 1)
                    gp.tensor_copy(sl1[b][0:rows, :].unsqueeze(2), slot[0:rows, :, bass.ds(t, 1)]).then_inc(sl_ready, 1)
                    gp.wait_ge(sl_ready, t + 1)
                    gp.sem_inc(pool_gate, 1)
                    for a, dst in enumerate((y1s[b], y2s[b])):
                        gp.indirect_dma_start(dst[0:rows, :], None, src,
                                              bass.IndirectOffsetOnAxis(ap=sl1[b][0:rows, a:a + 1], axis=0))\
                            .then_inc(done, 16)

                def take_all(src):
                    with gp.Fori(0, NT // 2) as i:
                        for b in range(2):
                            take(src, i * 2 + b, b, i, P, y12_loaded[b])
                    take(src, NT, 0, NT // 2, DEC, y12_loaded[2])

                with gp.If(n_extra > 0):
                    gp.memset(y1s[0], 0.0).then_inc(zero_made, 1)
                    gp.wait_ge(zero_made, 1)
                    with gp.Fori(0, NOV - n_extra) as q:
                        gp.dma_start(ys_d[bass.ds((q * -1 + (NE + NOV - 1)) * CAP, CAP), :], y1s[0]).then_inc(zeros_stored, 16)
                        gp.wait_ge(zeros_stored, q * 16 + 16)
                        gp.sem_inc(pool_gate, 1)
                    take_all(ys_d)
                with gp.If(n_extra == 0):
                    take_all(ys_d[0:NE * CAP, :])

            @block.scalar
            def _(act):

                act.wait_ge(wo_loaded, 32)
                for k in range(KT):
                    act.activation(WO[0][:, k, :], WO[0][:, k, :], ACT.Copy, scale=PT1[:, k, 8:9]).then_inc(wog_ready, 1)

                def rms_and_norms(t, src):
                    act.wait_ge(ssq_mm, t)
                    act.activation(ysq[:, :, 0:src.shape[2]], src, ACT.Square).then_inc(ysq_ready, 1)
                    act.wait_ge(rsv_ready, t + 1)
                    rows = src.shape[2]
                    act.activation(rs2[0:rows, :], rs2[0:rows, :], ACT.Sqrt).then_inc(rstd_ready, 1)
                    for a in range(2):
                        act.wait_ge(lnv_ready, t * 2 + (a + 1))
                        act.activation(rstd[0:rows, :], mv[0:rows, 1:2], ACT.Sqrt).then_inc(lns_ready, 1)

                with act.Fori(0, 4) as i:
                    for b in range(2):
                        act.wait_ge(y_loaded[b], i * 16 + 16)
                        rms_and_norms(i * 2 + b, ysl[b])
                rms_and_norms(NT, yS[:, :, :])
                def v_out(t, b, rows):
                    act.wait_ge(vt_mm, t + 1)
                    act.wait_ge(lg_mm, t)
                    act.activation(vT[b][:, :, 0:rows], PS[:, 0:2, :].rearrange("p a (k t) -> p (a k) t", t=P)[:, :, 0:rows],
                                   ACT.Copy).then_inc(vT_ready, 1)

                with act.Fori(0, 4) as i:
                    for b in range(2):
                        v_out(i * 2 + b, b, P)
                v_out(NT, 0, DEC)
                act.wait_ge(vector_once, RSEL_READY)
                act.activation(gon[:, 3, :, 0:NG], gon[:, 3, :, 0:NG], ACT.Exp).then_inc(scalar_once, 1)
                act.activation(gsm[:, 4, :], gsm[:, 4, :], ACT.Exp).then_inc(scalar_once, 1)

                def x_evac(e, b, r):
                    act.wait_ge(eT_mm, e + 1)
                    act.wait_ge(up_mm[b], r)
                    act.activation(xTs[b], PS[:, 0:2, :].rearrange("p a (k t) -> p (a k) t", t=P), ACT.Copy)\
                        .then_inc(xe_ready, 1)

                def half_tanh(e, b, r):
                    act.wait_ge(gate_mm[b], r + 1)
                    act.wait_ge(h_ready, e)
                    act.activation(hth, PS[:, 2, :], ACT.Tanh, scale=0.5).then_inc(hth_ready, 1)

                def y_out(e, b, r):
                    act.wait_ge(down_mm[b], r + 1)
                    act.wait_ge(yo_stored[b], r * 16)
                    act.activation(yo[b], PS[:, 5:7, :].rearrange("p a n -> p (a n)"), ACT.Copy).then_inc(yo_ready, 1)
                    act.wait_ge(yo_ready, e + 1)
                    act.dma_start(ys_d[bass.ds(e * CAP, CAP), :], yo[b]).then_inc(yo_stored[b], 16)

                act.wait_ge(scalar_once, REXP_READY)
                x_evac(0, 0, 0)
                half_tanh(0, 0, 0)
                x_evac(1, 1, 0)
                with act.Fori(0, NE // 2 - 1) as i:
                    half_tanh(i * 2 + 1, 1, i)
                    x_evac(i * 2 + 2, 0, i + 1)
                    y_out(i * 2, 0, i)
                    half_tanh(i * 2 + 2, 0, i + 1)
                    x_evac(i * 2 + 3, 1, i + 1)
                    y_out(i * 2 + 1, 1, i)
                half_tanh(NE - 1, 1, NE // 2 - 1)
                y_out(NE - 2, 0, NE // 2 - 1)
                y_out(NE - 1, 1, NE // 2 - 1)
                act.wait_ge(vector_once, CTL_READY)
                n_extra = act.value_load(ctl[0:1, NOV:NOV + 1], min_val=0, max_val=NOV)
                with act.If(n_extra > 0):
                    with act.Fori(0, n_extra) as q:
                        x_evac(q + NE, 0, q + NE // 2)
                        half_tanh(q + NE, 0, q + NE // 2)
                        y_out(q + NE, 0, q + NE // 2)
                for t in range(NTT):
                    act.wait_ge(lnv_ready, 2 * NTT + t + 1)
                    rows = P if t < NT else DEC
                    act.activation(rstd[0:rows, :], mv[0:rows, 1:2], ACT.Sqrt).then_inc(lns_ready, 1)

            @block.tensor
            def _(pe):

                pe.wait_ge(wog_ready, 2 * KT)

                def out_tile(t, y, rows):
                    for s in range(2):
                        if s == 0:
                            pe.wait_ge(pa_read, t)
                        else:
                            pe.wait_ge(pb_read, t)
                        for k in range(KT):
                            for n in range(2):
                                mm = pe.matmul(PS[0:rows, 2 * s + n, :], y[:, s * KT + k, :],
                                               WO[s][:, k, 512 * n:512 * n + 512], start=(k == 0), stop=(k == KT - 1))
                        if s == 0:
                            mm.then_inc(pa_mm, 1)
                            pe.wait_ge(ysq_ready, t + 1)
                            pe.wait_ge(rsv_ready, t)
                            for a in range(2):
                                for k in range(KT):
                                    mm = pe.matmul(PS[0:rows, 4, a:a + 1], ysq[:, a * KT + k, 0:rows], ones[:, 0:1],
                                                   start=(k == 0), stop=(k == KT - 1))
                            mm.then_inc(ssq_mm, 1)
                        else:
                            mm.then_inc(pb_mm, 1)

                with pe.Fori(0, 4) as i:
                    for b in range(2):
                        pe.wait_ge(y_loaded[b], i * 16 + 16)
                        out_tile(i * 2 + b, ysl[b], P)
                out_tile(NT, yS, DEC)

                pe.wait_ge(wr_loaded, 64)
                pe.wait_ge(pa_read, NTT)

                def router(t, b, rows):
                    pe.wait_ge(vT_ready, t)
                    for k in range(KT):
                        mm = pe.transpose(PS[:, k // 4, P * (k % 4):P * (k % 4) + rows], vsl[b][0:rows, k * P:(k + 1) * P],
                                          ident[0:rows, 0:rows])
                    mm.then_inc(vt_mm, 1)
                    pe.wait_ge(vT_ready, t + 1)
                    for k in range(KT):
                        mm = pe.matmul(PS[0:rows, 5, bass.ds(t * 36, 36)], vT[b][:, k, 0:rows], wr[:, k, :],
                                       start=(k == 0), stop=(k == KT - 1))
                    mm.then_inc(lg_mm, 1)

                with pe.Fori(0, 4) as i:
                    for b in range(2):
                        pe.wait_ge(vs_loaded[b], i * 16 + 16)
                        router(i * 2 + b, b, P)
                pe.wait_ge(vs_loaded[2], 16)
                router(NT, 0, DEC)
                pe.wait_ge(gpsimd_once, AM_READY)
                pe.wait_ge(vector_once, RANK_READY)
                A = gtmp[2].rearrange("p t e -> p (t e)")
                pe.matmul(PS[:, 0, 0:NE * NTT], triS[:, :], A, start=True, stop=True)
                pe.matmul(PS[:, 1, 0:NE * NTT], ones[:, :], A, start=True, stop=True).then_inc(tensor_once, 1)
                pe.wait_ge(vector_once, TOKF_READY)
                pe.transpose(PS[:, 2, 0:NE + NOV], tokf, ident[0:NE + NOV, 0:NE + NOV]).then_inc(tensor_once, 1)

                def x_turn(e, b, r):
                    pe.wait_ge(xg_loaded[b], r * 16 + 16)
                    pe.wait_ge(xe_ready, e)
                    for c in range(KT):
                        mm = pe.transpose(PS[:, c // 4, P * (c % 4):P * (c % 4) + P], xg[b][:, c::KT], ident[:, :])
                    mm.then_inc(eT_mm, 1)

                def gate_or_up(b, r, bank, w, loaded, done):
                    pe.wait_ge(loaded[b], r * 16 + 16)
                    for c in range(KT):
                        mm = pe.matmul(PS[:, bank, :], xTs[b][:, c, :], w[b][:, c, :], start=(c == 0), stop=(c == KT - 1))
                    mm.then_inc(done[b], 1)

                def gate(e, b, r):
                    pe.wait_ge(xe_ready, e + 1)
                    pe.wait_ge(h_ready, e)
                    gate_or_up(b, r, 2, wg, wg_loaded, gate_mm)

                def up(b, r):
                    gate_or_up(b, r, 3, wu, wu_loaded, up_mm)

                def h_turn(e):
                    pe.wait_ge(h_ready, e + 1)
                    pe.wait_ge(hT_ready, e)
                    for c in range(FF // P):
                        mm = pe.transpose(PS[:, 4, P * c:P * c + P], hb[:, c::FF // P], ident[:, :])
                    mm.then_inc(hT_mm, 1)

                def down(e, b, r):
                    pe.wait_ge(wd_loaded[b], r * 16 + 16)
                    pe.wait_ge(hT_ready, e + 1)
                    pe.wait_ge(yo_ready, e)
                    for c in range(FF // P):
                        for n in range(2):
                            mm = pe.matmul(PS[:, 5 + n, :], hT[:, c, :], wd[b][:, c, 512 * n:512 * n + 512],
                                           start=(c == 0), stop=(c == FF // P - 1))
                    mm.then_inc(down_mm[b], 1)

                x_turn(0, 0, 0)
                gate(0, 0, 0)
                up(0, 0)
                x_turn(1, 1, 0)
                with pe.Fori(0, NE // 2 - 1) as i:
                    for e, b, r, pr in ((i * 2 + 1, 1, i, i), (i * 2 + 2, 0, i + 1, i)):
                        gate(e, b, r)
                        h_turn(e - 1)
                        up(b, r)
                        x_turn(e + 1, 1 - b, pr + 1)
                        down(e - 1, 1 - b, pr)
                last = NE - 1
                gate(last, 1, NE // 2 - 1)
                h_turn(last - 1)
                up(1, NE // 2 - 1)
                down(last - 1, 0, NE // 2 - 1)
                h_turn(last)
                down(last, 1, NE // 2 - 1)
                pe.wait_ge(vector_once, CTL_READY)
                n_extra = pe.value_load(ctl[0:1, NOV:NOV + 1], min_val=0, max_val=NOV)
                with pe.If(n_extra > 0):
                    with pe.Fori(0, n_extra) as q:
                        x_turn(q + NE, 0, q + NE // 2)
                        gate(q + NE, 0, q + NE // 2)
                        up(0, q + NE // 2)
                        h_turn(q + NE)
                        down(q + NE, 0, q + NE // 2)

            @block.vector
            def _(ve):
                step = Chain(ve, vc)

                ve.wait_ge(wo_loaded, 32)
                for k in range(KT):
                    ve.tensor_scalar(WO[1][:, k, :], WO[1][:, k, :], PT1[:, k, 9:10], None, ALU.mult)\
                        .then_inc(wog_ready, 1)
                ve.wait_ge(rows1_loaded, 80)

                def norm(src, dst, rows, n, chain):
                    for h in range(2):
                        chain(ve.bn_stats(stat[0:rows, 6 * h:6 * h + 6], src[0:rows, 512 * h:512 * h + 512]))
                    ve.sem_inc(vector_gate, 1)
                    chain(ve.bn_aggr(mv[0:rows, :], stat[0:rows, :].rearrange("p (a s) -> p a s", a=2)))
                    ve.tensor_scalar(mv[0:rows, 1:2], mv[0:rows, 1:2], LN_EPS, None, ALU.add).then_inc(lnv_ready, 1)
                    ve.wait_ge(lns_ready, n + 1)
                    chain(ve.reciprocal(rstd[0:rows, :], rstd[0:rows, :]))
                    chain(ve.tensor_scalar(dst[0:rows, :], src[0:rows, :], mv[0:rows, 0:1], rstd[0:rows, :],
                                           ALU.subtract, ALU.mult))

                def row_tile(t, b, rows):
                    chain = Chain(ve, fl, t * 14)
                    r = slice(0, rows)
                    ve.wait_ge(ssq_mm, t + 1)
                    ve.tensor_scalar(rs2[r, :], PS[r, 4, 0:2], 1.0 / D, RMS_EPS, ALU.mult, ALU.add).then_inc(rsv_ready, 1)
                    ve.wait_ge(rstd_ready, t + 1)
                    chain(ve.reciprocal(rs2[r, :], rs2[r, :]))
                    ve.wait_ge(pa_mm, t + 1)
                    o2 = ob[r, :].rearrange("p (a n) -> p a n", a=2)
                    ve.tensor_scalar(o2, PS[r, 0:2, :], rs2[r, 0:1], None, ALU.mult).then_inc(pa_read, 1)
                    ve.wait_ge(pa_read, t + 1)
                    ve.wait_ge(pb_mm, t + 1)
                    ve.scalar_tensor_tensor(out=o2, in0=PS[r, 2:4, :], scalar=rs2[r, 1:2], in1=o2,
                                            op0=ALU.mult, op1=ALU.add).then_inc(pb_read, 1)
                    ve.wait_ge(pb_read, t + 1)
                    chain(ve.tensor_tensor(ob[r, :], ob[r, :], gate1[r, :], ALU.mult))
                    ve.wait_ge(xr_loaded[b], (t - b if b < 2 else t - NT) * 8 + 16)
                    ve.scalar_tensor_tensor(out=ob[r, :], in0=xr[b % 2][r, :], scalar=ALPHA, in1=ob[r, :],
                                            op0=ALU.mult, op1=ALU.add).then_inc(xr_used, 1)
                    ve.wait_ge(xr_used, t + 1)
                    if b < 2:
                        ve.wait_ge(xp1_stored[b], (t - b) * 8)
                        ve.wait_ge(v_stored[b], (t - b) * 8)
                    else:
                        ve.wait_ge(xp1_stored[0], 64)
                        ve.wait_ge(v_stored[0], 64)
                    x1, v1 = xp1[b % 2], vb[b % 2]
                    norm(ob, x1, rows, t * 2, chain)
                    chain(ve.tensor_tensor(x1[r, :], x1[r, :], ln1g[r, :], ALU.mult))
                    ve.tensor_tensor(x1[r, :], x1[r, :], ln1b[r, :], ALU.add).then_inc(xp1_ready, 1)
                    ve.wait_ge(xp1_ready, t + 1)
                    norm(x1, v1, rows, t * 2 + 1, chain)
                    chain(ve.tensor_tensor(v1[r, :], v1[r, :], sc2[r, :], ALU.mult))
                    ve.tensor_tensor(v1[r, :], v1[r, :], sh2[r, :], ALU.add).then_inc(v_ready, 1)
                    assert chain.n == 14, chain.n

                with ve.Fori(0, 4) as i:
                    for b in range(2):
                        row_tile(i * 2 + b, b, P)
                ve.wait_ge(rows1_loaded, 128)
                row_tile(NT, 2, DEC)

                step(ve.memset(Lg[:, :, :], 0.0))
                ve.wait_ge(lg_mm, NTT)
                step(ve.tensor_tensor(Lg[:, 0:NT, :], PS[:, 5, 0:36 * NT].rearrange("p (t c) -> p t c", c=36),
                                      brb[:, :].unsqueeze(1).to_broadcast([P, NT, 36]), ALU.add))
                step(ve.tensor_tensor(Lg[0:DEC, NT, :], PS[0:DEC, 5, 36 * NT:36 * NTT], brb[0:DEC, :], ALU.add))

                def first_of_max(x, n, top, tmp, red, out):
                    wide = lambda a: a.unsqueeze(2).to_broadcast([P, NTT, n])
                    step(ve.tensor_reduce(top, x, AX.X, ALU.max))
                    step(ve.tensor_tensor(tmp, x, wide(top), ALU.is_equal))
                    step(ve.tensor_tensor(tmp, tmp, desc[:, EG - n:EG].unsqueeze(1).to_broadcast([P, NTT, n]), ALU.mult))
                    step(ve.tensor_reduce(red, tmp, AX.X, ALU.max))
                    step(ve.tensor_tensor(out, tmp, wide(red), ALU.is_equal))

                gmax, red, m1, m2, ed, se, den, g1v = [gsm[:, i, :] for i in range(8)]
                ohg, o1, o2h, ext = gon[:, 0, :, 0:NG], gon[:, 1, :, :], gon[:, 2, :, :], gon[:, 3, :, 0:NG]
                tmp8, les = gtmp[3][:, :, 0:EG], gtmp[4][:, :, 0:EG]
                first_of_max(Lg[:, :, 0:NG], NG, gmax, tmp8[:, :, 0:NG], red, ohg)
                ve.tensor_tensor(ext, Lg[:, :, 0:NG], gmax.unsqueeze(2).to_broadcast([P, NTT, NG]), ALU.subtract)\
                    .then_inc(vector_once, 1)
                Le = Lg[:, :, NG:NG + NE].rearrange("p t (g e) -> p t g e", g=NG)
                prod = gtmp[5].rearrange("p t (g e) -> p t g e", g=NG)
                step(ve.tensor_tensor(prod, Le, ohg.unsqueeze(3).to_broadcast([P, NTT, NG, EG]), ALU.mult))
                step(ve.tensor_reduce(les, gtmp[5].rearrange("p t (g e) -> p t e g", g=NG), AX.X, ALU.add))
                first_of_max(les, EG, m1, tmp8, red, o1)
                step(ve.scalar_tensor_tensor(out=les, in0=o1, scalar=-3.0e38, in1=les, op0=ALU.mult, op1=ALU.add))
                first_of_max(les, EG, m2, tmp8, red, o2h)
                ve.tensor_tensor(ed, m2, m1, ALU.subtract).then_inc(vector_once, 1)
                for a, oh in enumerate((o1, o2h)):
                    ve.tensor_tensor(gtmp[a].rearrange("p t (g e) -> p t g e", g=NG),
                                     ohg.unsqueeze(3).to_broadcast([P, NTT, NG, EG]),
                                     oh.unsqueeze(2).to_broadcast([P, NTT, NG, EG]), ALU.mult).then_inc(vector_once, 1)
                ve.wait_ge(scalar_once, REXP_READY)
                step(ve.tensor_reduce(se, ext, AX.X, ALU.add))
                step(ve.scalar_tensor_tensor(out=den, in0=ed, scalar=1.0, in1=se, op0=ALU.add, op1=ALU.mult))
                step(ve.reciprocal(gat[:, 0, :], den))
                step(ve.tensor_tensor(gat[:, 1, :], gat[:, 0, :], ed, ALU.mult))
                step(ve.tensor_tensor(triS[:, :], tri[:, :], ident[:, :], ALU.subtract))
                ve.wait_ge(gpsimd_once, AM_READY)
                ve.tensor_tensor(gtmp[2], gtmp[0], gtmp[1], ALU.add).then_inc(vector_once, 1)
                ve.wait_ge(tensor_once, RANK_MM)
                tot = gtmp[3]
                rank, off, ovm = gtmp[4], gtmp[5], gtmp[6]
                step(ve.tensor_copy(tot, PS[:, 1, 0:NE * NTT].rearrange("p (t e) -> p t e", e=NE)))
                step(ve.memset(off[:, 0, :], 0.0))
                for t in range(NT):
                    step(ve.tensor_tensor(off[:, t + 1, :], off[:, t, :], tot[:, t, :], ALU.add))
                n_e, nov, ovend, delta, onesE, _ = [cnt[:, i, :] for i in range(6)]
                step(ve.tensor_tensor(n_e, off[:, NT, :], tot[:, NT, :], ALU.add))
                step(ve.tensor_tensor(rank, off, PS[:, 0, 0:NE * NTT].rearrange("p (t e) -> p t e", e=NE), ALU.add))
                step(ve.memset(nov, 0.0))
                for m in range(1, (SEQ + DEC - 1) // CAP + 1):
                    step(ve.scalar_tensor_tensor(out=nov, in0=n_e, scalar=float(CAP * m), in1=nov,
                                                 op0=ALU.is_gt, op1=ALU.add))
                step(ve.memset(onesE, 1.0))
                step(ve.tensor_tensor_scan(ovend, onesE, nov, 0.0, ALU.mult, ALU.add))
                step(ve.tensor_tensor(delta, ovend, nov, ALU.subtract))
                step(ve.tensor_scalar(delta, delta, float(NE - 1), float(CAP), ALU.add, ALU.mult))
                step(ve.tensor_tensor(delta, delta, ebase[:, :], ALU.subtract))
                wideE = lambda a: a.unsqueeze(1).to_broadcast([P, NTT, NE])
                step(ve.scalar_tensor_tensor(out=ovm, in0=rank, scalar=float(CAP), in1=wideE(delta),
                                             op0=ALU.is_ge, op1=ALU.mult))
                step(ve.tensor_tensor(rank, rank, ovm, ALU.add))
                step(ve.tensor_tensor(rank, rank, wideE(ebase[:, :]), ALU.add))
                for a in range(2):
                    step(ve.tensor_tensor(ovm, gtmp[a], rank, ALU.mult))
                    step(ve.tensor_reduce(gsm[:, 8 + a, :], ovm, AX.X, ALU.add))
                    ve.tensor_copy(slot[:, a, :], gsm[:, 8 + a, :]).then_inc(vector_once, 1)
                big = at(45696 + NE * NTT * 3, NOV, NE)
                step(ve.tensor_tensor(big, ovend.unsqueeze(1).to_broadcast([P, NOV, NE]),
                                      qidx[:, :].unsqueeze(2).to_broadcast([P, NOV, NE]), ALU.is_le))
                step(ve.tensor_reduce(ovq[:, 0, :], big, AX.X, ALU.add))
                step(ve.tensor_scalar(ovq[:, 0, :], ovq[:, 0, :], float(NE - 1), None, ALU.min))
                step(ve.tensor_copy(ctl[:, 0:NOV], ovq[:, 0, :]))
                ve.tensor_copy(ctl[:, NOV:NOV + 1], ovend[:, NE - 1:NE]).then_inc(vector_once, 1)
                ve.wait_ge(tokr_loaded, 16)
                ve.tensor_copy(tokf, tokr).then_inc(vector_once, 1)
                ve.wait_ge(tensor_once, TOKT_MM)
                ve.tensor_copy(idxT[:, :], PS[:, 2, 0:NE + NOV]).then_inc(vector_once, 1)

                def first_half(e):
                    ve.wait_ge(hth_ready, e + 1)
                    ve.scalar_tensor_tensor(out=hth, in0=hth, scalar=1.0, in1=PS[:, 2, :], op0=ALU.add, op1=ALU.mult)\
                        .then_inc(h1_ready, 1)
                    ve.wait_ge(h1_ready, e + 1)

                def second_half(e, b, r):
                    ve.wait_ge(up_mm[b], r + 1)
                    ve.wait_ge(hT_mm, e)
                    ve.scalar_tensor_tensor(out=hb, in0=hth, scalar=0.5, in1=PS[:, 3, :], op0=ALU.mult, op1=ALU.mult)\
                        .then_inc(h_ready, 1)

                def h_evac(e, b, r):
                    ve.wait_ge(hT_mm, e + 1)
                    if b is not None:
                        ve.wait_ge(down_mm[b], r)
                    ve.tensor_copy(hT.rearrange("p c t -> p (c t)"), PS[:, 4, :]).then_inc(hT_ready, 1)

                first_half(0)
                second_half(0, 0, 0)
                with ve.Fori(0, NE // 2 - 1) as i:
                    first_half(i * 2 + 1)
                    h_evac(i * 2, 1, i)
                    second_half(i * 2 + 1, 1, i)
                    first_half(i * 2 + 2)
                    h_evac(i * 2 + 1, 0, i + 1)
                    second_half(i * 2 + 2, 0, i + 1)
                first_half(NE - 1)
                h_evac(NE - 2, 1, NE // 2 - 1)
                second_half(NE - 1, 1, NE // 2 - 1)
                h_evac(NE - 1, 0, NE // 2)
                n_extra = ve.value_load(ctl[0:1, NOV:NOV + 1], min_val=0, max_val=NOV)
                with ve.If(n_extra > 0):
                    with ve.Fori(0, n_extra) as q:
                        first_half(q + NE)
                        second_half(q + NE, 0, q + NE // 2)
                        ve.wait_ge(down_mm[1], NE // 2)
                        h_evac(q + NE, 0, q + NE // 2)

                ve.wait_ge(rows2n_loaded, 48)

                def final_tile(t, b, r, rows, lb):
                    chain = Chain(ve, fl, t * 9 + NTT * 14)
                    q = slice(0, rows)
                    o = fo[b][q, :]
                    chain(ve.tensor_copy(gcur[q, :].unsqueeze(2), gat[q, :, bass.ds(t, 1)]))
                    ve.wait_ge(y12_loaded[lb], r * 32 + 32)
                    ve.wait_ge(fo_stored[b], (r if lb < 2 else NT // 2) * 16)
                    chain(ve.tensor_scalar(o, y1s[b][q, :], gcur[q, 0:1], None, ALU.mult))
                    ve.scalar_tensor_tensor(out=o, in0=y2s[b][q, :], scalar=gcur[q, 1:2], in1=o,
                                            op0=ALU.mult, op1=ALU.add).then_inc(y12_used[b], 1)
                    ve.wait_ge(y12_used[b], (r if lb < 2 else NT // 2) + 1)
                    chain(ve.tensor_tensor(o, o, gate2[q, :], ALU.mult))
                    ve.wait_ge(xl2_loaded[lb], r * 16 + 16)
                    chain(ve.scalar_tensor_tensor(out=o, in0=xl2[b][q, :], scalar=ALPHA, in1=o,
                                                  op0=ALU.mult, op1=ALU.add))
                    norm(fo[b], fo[b], rows, 2 * NTT + t, chain)
                    ve.tensor_tensor(o, o, ln2g[q, :], ALU.mult).then_inc(gcur_ready, 1)
                    ve.wait_ge(gcur_ready, t + 1)
                    ve.tensor_tensor(o, o, ln2b[q, :], ALU.add).then_inc(fo_ready, 1)
                    assert chain.n == 9, chain.n

                with ve.Fori(0, NT // 2) as i:
                    for b in range(2):
                        final_tile(i * 2 + b, b, i, P, b)
                ve.wait_ge(rows2n_loaded, 64)
                final_tile(NT, 0, 0, DEC, 2)



_INS = ['x_prompt', 'x_sample', 'c_prompt', 'c_sample', 'state_lru_conv', 'state_lru_h', 'state_ssd_conv',
        'state_ssd', 'w_ada', 'b_ada', 'w_in', 'lru_conv_w', 'lru_conv_b', 'lru_wa', 'lru_ba', 'lru_wx', 'lru_bx',
        'lru_lambda', 'lru_norm_g', 'ssd_conv_w', 'ssd_conv_b', 'ssd_dt_bias', 'ssd_a_log', 'ssd_d',
        'ssd_norm_g', 'w_out', 'ln1_g', 'ln1_b', 'w_rg', 'b_rg', 'w_re', 'b_re', 'w_gate', 'w_up', 'w_down',
        'ln2_g', 'ln2_b']
_OUTS = [('y_prompt', (1, SEQ, D)), ('y_sample', (DEC, 1, D)),
         ('prompt_lru_conv', (1, 1, CONV - 1, D)), ('prompt_lru_h', (1, 1, D)),
         ('prompt_ssd_conv', (1, 1, CONV - 1, XBC)), ('prompt_ssd', (1, 1, HEADS, HD, STATE)),
         ('sample_lru_conv', (1, DEC, CONV - 1, D)), ('sample_lru_h', (1, DEC, D)),
         ('sample_ssd_conv', (1, DEC, CONV - 1, XBC)), ('sample_ssd', (1, DEC, HEADS, HD, STATE))]


def kernel(**inputs):
    import numpy as _np
    import concourse.bacc as _bacc
    from concourse import mybir as _mybir
    from concourse.bass_utils import run_bass_kernel_spmd as _run

    nc = _bacc.Bacc("TRN2", target_bir_lowering=False, num_devices=1)
    arrays, args = {}, []
    for name in _INS:
        a = _np.ascontiguousarray(inputs[name])
        arrays[f"in_{name}_dram"] = a
        args.append(nc.dram_tensor(f"in_{name}_dram", a.shape, _mybir.dt.from_np(a.dtype), kind="ExternalInput").ap())
    for name, shape in _OUTS:
        args.append(nc.dram_tensor(f"out_{name}_dram", shape, _mybir.dt.float32, kind="ExternalOutput").ap())
    build_step(nc, *args)
    r = _run(nc, [arrays], core_ids=[0])
    return tuple(r.results[0][f"out_{name}_dram"] for name, _ in _OUTS)
```

```python
from contextlib import ExitStack

import numpy as np
import concourse.bass as bass
from concourse import mybir

F32 = mybir.dt.float32
F32R = mybir.dt.float32r
I32 = mybir.dt.int32
U32 = mybir.dt.uint32
ALU = mybir.AluOpType
ACT = mybir.ActivationFunctionType
AX = mybir.AxisListType

P = 128
D = 1024
KT = D // P
SEQ = 1024
NT = SEQ // P
DEC = 8
CONV = 4
HEADS = 16
HD = 64
STATE = 128
XBC = D + 4 * STATE
XT = XBC // P
COL_G, COL_Z, COL_XBC = D, 2 * D, 3 * D
COL_DT = COL_XBC + XBC
NE = 32
NG = 4
EG = NE // NG
FF = 512
CAP = 128
NOV = 16
NMOD = 6
TE = SEQ + DEC * CONV
CH = TE // 3
S0 = SEQ + CONV - 1
ALPHA = 2.0 ** 0.25
LN_EPS = 1e-5
RMS_EPS = 1e-6
LRU_C = 8.0


class Chain:

    def __init__(self, eng, sem, base=0):
        self.eng, self.sem, self.base, self.n = eng, sem, base, 0

    def __call__(self, ins):
        self.n += 1
        ins.then_inc(self.sem, 1)
        self.eng.wait_ge(self.sem, self.base + self.n)




def build_step(nc, x_prompt, x_sample, c_prompt, c_sample, state_lru_conv, state_lru_h, state_ssd_conv,
               state_ssd, w_ada, b_ada, w_in, lru_conv_w, lru_conv_b, lru_wa, lru_ba, lru_wx, lru_bx,
               lru_lambda, lru_norm_g, ssd_conv_w, ssd_conv_b, ssd_dt_bias, ssd_a_log, ssd_d,
               ssd_norm_g, w_out, ln1_g, ln1_b, w_rg, b_rg, w_re, b_re, w_gate, w_up, w_down,
               ln2_g, ln2_b, y_prompt, y_sample, prompt_lru_conv, prompt_lru_h, prompt_ssd_conv,
               prompt_ssd, sample_lru_conv, sample_lru_h, sample_ssd_conv, sample_ssd):
    ctx = ExitStack()

    def sb(name, shape, dt=F32, scope=None):
        return (scope or ctx).enter_context(nc.sbuf_tensor(name, shape, dt))

    def dram(name, shape, dt=F32):
        return nc.dram_tensor(name, shape, dt, kind="Internal").ap()

    with ctx:
        NTT = NT + 1
        NBLK = NE + NOV
        NO_TOKEN = 4096
        mod_d = dram("mod_d", [1 + DEC, NMOD * D])
        x_d = dram("x_d", [KT, P, TE])
        z_d = dram("z_d", [KT, P, TE])
        y_d = dram("y_d", [2 * KT, P, SEQ])
        acs_d = dram("acs_d", [NT, HEADS * P])
        bcs_d = dram("bcs_d", [4, DEC * P])
        xp1_d = dram("xp1_d", [SEQ + DEC, D])
        v_d = dram("v_d", [SEQ + DEC, D])
        ys_d = dram("ys_d", [NBLK * CAP, D])

        ident = sb("ident", [P, P])
        ones = sb("ones", [P, P])
        tri = sb("tri", [P, P])
        PT1 = sb("PT1", [P, KT, 42])
        yS = sb("yS", [P, 2 * KT, DEC])
        exd = sb("exd", [P, KT, 2 * DEC])
        Dch = sb("Dch", [P, KT])
        desc = sb("desc", [P, EG])
        eidx = sb("eidx", [P, NE])
        qidx = sb("qidx", [P, NBLK])
        tokv = sb("tokv", [P, NTT])
        stat = sb("stat", [P, 12])
        mv = sb("mv", [P, 2])
        rstd = sb("rstd", [P, 1])
        PS = ctx.enter_context(nc.psum_tensor("PS", [P, 8, 512], F32))

        WORDS, SPLIT = 47744, 23936
        first = ExitStack()
        arena = sb("arena", [P, SPLIT], scope=first)

        def at(off, *dims, parts=P, base=None):
            n = int(np.prod(dims))
            a = base
            if base is None:
                a, off = (arena, off) if off < SPLIT else (upper, off - SPLIT)
            assert off + n <= a.shape[1], (off, dims)
            v = a[0:parts, off:off + n]
            if len(dims) == 2:
                v = v.rearrange("p (a b) -> p a b", a=dims[0])
            if len(dims) == 3:
                v = v.rearrange("p (a b c) -> p a b c", a=dims[0], b=dims[1])
            return v

        PT2 = sb("PT2", [P, XT, 29], scope=first)
        cur1 = sb("cur1", [P, 42], scope=first)
        cur2 = [sb(f"cur2{b}", [P, 29], scope=first) for b in range(2)]
        cso = sb("cso", [P, KT + XT, 27], scope=first)
        hso = sb("hso", [P, KT, 9], scope=first)
        ssT = sb("ssT", [P, 2, KT, 9], scope=first)
        spl = sb("spl", [P, KT, 2], scope=first)
        dtr = sb("dtr", [P, 8, NT + 1, HEADS], scope=first)
        DT, DTA, ACS, TOT, CD, DXW = [dtr[:, i, :, :] for i in range(6)]
        wdt = sb("wdt", [P, KT, HEADS], scope=first)
        dtb = sb("dtb", [P, 2, HEADS], scope=first)
        Dh = sb("Dh", [HEADS, 1], scope=first)
        acur = sb("acur", [P, HEADS], scope=first)
        cT = sb("cT", [P, KT, 9], scope=first)
        sm = sb("sm", [P, 8, 24], scope=first)

        upper_scope = ExitStack()
        upper = sb("upper", [P, WORDS - SPLIT], scope=upper_scope)

        uT = at(0, KT, TE)
        BC = at(8448, 4, TE)
        wsl = [at(12672 + 1024 * b, KT, P) for b in range(2)]
        A0 = 14720
        adaw = [at(A0 + 4096 * b, KT, 512) for b in range(2)]
        early = [at(4096 * b, KT, 512) for b in range(2)]
        bada = at(23936, NMOD * D, parts=9)
        mod = at(30080, NMOD * D, parts=9)
        xt = [at(36224 + 1024 * b, D) for b in range(2)]
        xn = [at(38272 + 1024 * b, D) for b in range(2)]
        ltmp = at(40320, KT, P)
        cin = at(22912, D, parts=9)
        cs = at(41344, D, parts=9)
        prow = at(42368, D, parts=42)
        prow2 = at(43392, XBC, parts=29)
        xb2 = [at(A0 + 1060 * b, 1060) for b in range(2)]
        cacc = [at(16840 + TE * b, TE) for b in range(2)]
        cth = [at(18952 + TE * b, TE) for b in range(2)]
        xo = [at(21064 + TE * b, TE) for b in range(2)]
        (Rb, SEG, ER) = [at(A0 + 2048 * i, HEADS, P) for i in range(3)]
        o = A0 + 6144
        xst, zst, xdt, xw, Sst, Sin, stmp, xD = [at(o + 1024 * i, KT, P) for i in range(8)]
        o += 8192
        bst = at(o, 2, P)
        CBm = at(o + 256, NT, 2, P)
        Btok = at(o + 2304, NT, 2, P)
        o += 4352
        xbl = at(o, 1060)
        xlc, gl, thr, thi, la, lt, la2, yl = [at(o + 1060 + TE * i, TE) for i in range(8)]
        o += 1060 + 8 * TE
        BDa, BDx = at(o, P), at(o + P, P)
        o += 256
        ysC = at(o, KT, P)
        dcT = at(A0 + 12032, 2 * DEC, parts=HEADS)
        bcr = at(A0 + 12160, 4 * P, parts=DEC)
        co = at(A0 + 12672, (KT + XT) * P, parts=27)
        ho = at(A0 + 15232, D, parts=9)
        So = at(A0 + 16256, KT, P)
        acsT = at(47000, P)
        EX = at(45184, KT, P, parts=HEADS)
        itmp = at(46240, NBLK).bitcast(I32)
        dtT = [at(o, 512, parts=HEADS) for o in (23176, 47128)]
        tokid = at(46208, NTT).bitcast(I32)
        zrow = at(46300, D // 2)
        upper_scope.close()
        us = sb("us", [P, 2, KT, TE], F32R, scope=first)
        wss = [sb(f"wss{b}", [P, 2, KT, P], F32R, scope=first) for b in range(2)]
        wdts = sb("wdts", [P, 2, KT, HEADS], F32R, scope=first)

        in_first = []

        def sem(name):
            s = nc.alloc_semaphore(name)
            in_first.append(s)
            return s

        pool_gate = sem("pool_gate")
        vector_gate = sem("vector_gate")
        c_loaded = sem("c_loaded")
        rows_loaded = sem("rows_loaded")
        rows2_loaded = sem("rows2_loaded")
        small_loaded = sem("small_loaded")
        bada_loaded = sem("bada_loaded")
        adaw_loaded = [sem(f"adaw_loaded{b}") for b in range(2)]
        early_loaded = [sem(f"early_loaded{b}") for b in range(2)]
        ada_mm = [sem(f"ada_mm{b}") for b in range(2)]
        ada_ready = [sem(f"ada_ready{b}") for b in range(2)]
        mod_stored = sem("mod_stored")
        xt_loaded = [sem(f"xt_loaded{b}") for b in range(3)]
        var_ready = sem("var_ready")
        std_ready = sem("std_ready")
        xn_ready = [sem(f"xn_ready{b}") for b in range(3)]
        xnT_mm = [sem(f"xnT_mm{b}") for b in range(3)]
        uT_ready = [sem(f"uT_ready{b}") for b in range(3)]
        vc = sem("vector_step")
        gc = sem("gpsimd_step")
        ac = sem("scalar_step")
        vl = sem("vector_loop_step")
        al = sem("scalar_loop_step")
        w_loaded = [sem(f"w_loaded{b}") for b in range(2)]
        uh_ready = sem("uh_ready")
        ul_ready = sem("ul_ready")
        wh_ready = [sem(f"wh_ready{b}") for b in range(2)]
        wl_ready = [sem(f"wl_ready{b}") for b in range(2)]
        proj_mm = [sem(f"proj_mm{b}") for b in range(2)]
        px_copied = [sem(f"px_copied{b}") for b in range(2)]
        hist_set = [sem(f"hist_set{b}") for b in range(2)]
        conv_done = [sem(f"conv_done{b}") for b in range(2)]
        cth_ready = [sem(f"cth_ready{b}") for b in range(2)]
        xo_ready = [sem(f"xo_ready{b}") for b in range(2)]
        xo_stored = [sem(f"xo_stored{b}") for b in range(2)]
        cur_ready = [sem(f"cur_ready{b}") for b in range(2)]
        out_stored = sem("out_stored")
        ys_zeroed = sem("ys_zeroed")
        ltmp_ready = sem("ltmp_ready")
        ys_copied = sem("ys_copied")
        bcr_stored = sem("bcr_stored")
        acs_stored = sem("acs_stored")
        i_mm = sem("i_mm")
        bd_loaded = sem("bd_loaded")
        seg_ready = sem("seg_ready")
        er_ready = sem("er_ready")
        r_loaded = sem("r_loaded")
        xt_mm = sem("xt_mm")
        xd_ready = sem("xd_ready")
        xst_loaded = sem("xst_loaded")
        ysc_ready = sem("ysc_ready")
        zst_loaded = sem("zst_loaded")
        bst_ready = sem("bst_ready")
        ec_ready = sem("ec_ready")
        sin_ready = sem("sin_ready")
        stmp_ready = sem("stmp_ready")
        segx_ready = sem("segx_ready")
        m_ready = sem("m_ready")
        xw_ready = sem("xw_ready")
        st_mm = sem("st_mm")
        state_ready = sem("state_ready")
        y_mm = sem("y_mm")
        xl_copied = sem("xl_copied")
        lhist_set = sem("lhist_set")
        xlc_ready = sem("xlc_ready")
        gl_ready = sem("gl_ready")
        r_mm = sem("r_mm")
        thr_ready = sem("thr_ready")
        thi_ready = sem("thi_ready")
        la_ready = sem("la_ready")
        lt_ready = sem("lt_ready")
        la2_ready = sem("la2_ready")
        ls_ready = sem("ls_ready")
        yl_ready = sem("yl_ready")
        yl_stored = sem("yl_stored")
        ysc_stored = sem("ysc_stored")
        tensor_once = sem("tensor_once")
        (PT1_MM, PT2_MM, CT_MM, SS_MM, DTP_MM, DCH_MM, DT_MM, ACS_MM, ACST_MM, CB_MM, BT_MM, DC_MM, BCR_MM,
         CO_MM, EX_MM, HO_MM, SO_MM) = range(1, 18)
        vector_once = sem("vector_once")
        (CS_READY, PT_READY, CT_READY, LAM_READY, SC1_READY, SS_READY, MOD_READY, DTE_IN, DTA_READY,
         ACS_COPIED, DXE_IN, ACST_READY, CB_READY, BT_READY, DC_READY, BCR_READY, _) = \
            (1, 3, 4, 5, 6, 7, 8, 9, 10, 12, 13, 14, 15, 16, 17, 18, 19)
        scalar_once = sem("scalar_once")
        (CSIG_READY, LAMEXP, DTT_READY, DT_EXP, DXE_READY, HO_READY, CO_READY, SO_READY) = \
            (1, 2, 4, 6, 9, 10, 11, 12)
        gpsimd_once = sem("gpsimd_once")
        (IDENT_MADE, TRI_MADE, EX_MADE, _, UZ, XB2_ZEROED, XB_ZEROED, BD_ZEROED) = \
            (1, 2, 3, 6, 7, 9, 11, 13)

        win_t = w_in[0].rearrange("(k p) n -> p k n", p=P)
        wada_t = w_ada[0].rearrange("(k p) n -> p k n", p=P)

        with nc.Block() as block:
            @block.sync
            def _(sp):
                sp.dma_start(cin[0:1, :], c_prompt).then_inc(c_loaded, 16)
                sp.dma_start(cin[1:9, :], c_sample).then_inc(c_loaded, 16)
                for dst, src in ((prow[0:4, :], lru_conv_w[0]), (prow[4:5, :], lru_conv_b),
                                 (prow[5:6, :], lru_ba.rearrange("a h i -> a (h i)")),
                                 (prow[6:7, :], lru_bx.rearrange("a h i -> a (h i)")),
                                 (prow[7:8, :], lru_lambda), (prow[8:9, :], lru_norm_g),
                                 (prow[9:10, :], ssd_norm_g), (prow[10:18, :], state_lru_h[0]),
                                 (prow[18:42, :], state_lru_conv[0].rearrange("b k n -> (b k) n"))):
                    sp.dma_start(dst, src).then_inc(rows_loaded, 16)
                for dst, src in ((prow2[0:4, :], ssd_conv_w[0]), (prow2[4:5, :], ssd_conv_b),
                                 (prow2[5:29, :], state_ssd_conv[0].rearrange("b k n -> (b k) n"))):
                    sp.dma_start(dst, src).then_inc(rows2_loaded, 16)
                sp.dma_start(bada, b_ada[0:1, :].to_broadcast([9, NMOD * D])).then_inc(bada_loaded, 16)

                def load_ada(chunk, b):
                    sp.dma_start(adaw[b], wada_t[:, :, bass.ds(chunk * 512, 512)]).then_inc(adaw_loaded[b], 16)

                for b in range(2):
                    load_ada(b, b)
                with nc.allow_non_contiguous_dma(reason="one value per head"):
                    sp.dma_start(Dh[:, :], ssd_d.rearrange("a h -> h a")).then_inc(small_loaded, 16)
                sp.dma_start(dtb[:, 0, :], ssd_dt_bias[0:1, :].to_broadcast([P, HEADS])).then_inc(small_loaded, 16)
                sp.dma_start(dtb[:, 1, :], ssd_a_log[0:1, :].to_broadcast([P, HEADS])).then_inc(small_loaded, 16)
                sp.dma_start(wdt[:, :, :], win_t[:, :, COL_DT:COL_DT + HEADS]).then_inc(small_loaded, 16)
                for b in range(2):
                    sp.dma_start(early[b], wada_t[:, :, (2 + b) * 512:(3 + b) * 512]).then_inc(early_loaded[b], 16)
                for b in range(2):
                    sp.dma_start(xt[b][:, :], x_prompt[0, b * P:(b + 1) * P, :]).then_inc(xt_loaded[b], 16)
                for b in range(2):
                    sp.wait_ge(ada_mm[b], 1)
                    load_ada(4 + b, b)
                for b in range(2):
                    sp.dma_start(wsl[b], win_t[:, :, COL_XBC + b * P:COL_XBC + (b + 1) * P]).then_inc(w_loaded[b], 16)
                with sp.Fori(0, 3) as i:
                    for b in range(2):
                        sp.wait_ge(ada_mm[b], i + 3)
                        load_ada(i * 2 + (6 + b), b)
                sp.wait_ge(vector_once, MOD_READY)
                sp.dma_start(mod_d, mod).then_inc(mod_stored, 16)

                def load_w(col, b):
                    sp.dma_start(wsl[b], win_t[:, :, bass.ds(col, P)]).then_inc(w_loaded[b], 16)

                for b in range(2):
                    sp.wait_ge(proj_mm[b], 1)
                    load_w(COL_XBC + (2 + b) * P, b)
                with sp.Fori(0, 4) as i:
                    for b in range(2):
                        sp.wait_ge(wl_ready[b], i + 1)
                        load_w(i * (2 * P) + (COL_XBC + (4 + b) * P), b)
                with sp.Fori(0, 4) as i:
                    for b in range(2):
                        sp.wait_ge(wl_ready[b], i + 5)
                        load_w(i * (2 * P) + (COL_Z + b * P), b)
                with sp.Fori(0, NT) as j:
                    for b in range(2):
                        sp.wait_ge(proj_mm[b], j + 10)
                        load_w(j * P + b * COL_G, b)
                    sp.wait_ge(acs_stored, 16)
                    for b in range(2):
                        sp.wait_ge(xo_stored[b], 16 * 8)
                    sp.wait_ge(xt_mm, j)
                    sp.wait_ge(xd_ready, j)
                    sp.dma_start(xst, x_d[:, :, bass.ds(j * P, P)].rearrange("k p t -> p k t")).then_inc(xst_loaded, 16)
                    sp.wait_ge(seg_ready, j)
                    sp.wait_ge(er_ready, j)
                    sp.dma_start(Rb, acs_d[bass.ds(j, 1), :].to_broadcast([P, HEADS * P])
                                 .rearrange("p (h l) -> p h l", h=HEADS)).then_inc(r_loaded, 16)
                    sp.wait_ge(gpsimd_once, BD_ZEROED)
                    sp.wait_ge(i_mm, j)
                    for wsrc, wdst in ((lru_wa, BDa), (lru_wx, BDx)):
                        for h in range(2):
                            sp.dma_start(wdst[HD * h:HD * (h + 1), HD * h:HD * (h + 1)],
                                         wsrc[0, bass.ds(j * 2 + h, 1), :, :].rearrange("a i j -> (a i) j"))\
                                .then_inc(bd_loaded, 16)
                    sp.wait_ge(ysc_ready, j)
                    sp.dma_start(zst, z_d[:, :, bass.ds(j * P, P)].rearrange("k p t -> p k t")).then_inc(zst_loaded, 16)

                sp.wait_ge(bcr_stored, 16)
                sp.wait_ge(scalar_once, CO_READY)
                sp.dma_start(prompt_lru_conv[0, 0], co[0:3, 0:D]).then_inc(out_stored, 16)
                sp.dma_start(sample_lru_conv[0].rearrange("b k n -> (b k) n"), co[3:27, 0:D]).then_inc(out_stored, 16)
                sp.dma_start(prompt_ssd_conv[0, 0], co[0:3, D:D + XBC]).then_inc(out_stored, 16)
                sp.dma_start(sample_ssd_conv[0].rearrange("b k n -> (b k) n"), co[3:27, D:D + XBC])\
                    .then_inc(out_stored, 16)
                sp.wait_ge(scalar_once, HO_READY)
                sp.dma_start(prompt_lru_h[0], ho[0:1, :]).then_inc(out_stored, 16)
                sp.dma_start(sample_lru_h[0], ho[1:9, :]).then_inc(out_stored, 16)
                sp.wait_ge(scalar_once, SO_READY)
                sp.dma_start(prompt_ssd[0, 0].rearrange("(k h) p n -> (h p) k n", h=2), So).then_inc(out_stored, 16)
                sp.wait_ge(out_stored, 16 * 7)
                sp.wait_ge(ys_zeroed, 16 * 8)


            @block.gpsimd
            def _(gp):
                step = Chain(gp, gc)
                step(gp.memset(ident[:, :], 0.0))
                gp.affine_select(out=ident[:, :], in_=ident[:, :], compare_op=ALU.not_equal, fill=1.0, base=0,
                                 pattern=[[-1, P]], channel_multiplier=1).then_inc(gpsimd_once, 1)
                step(gp.memset(ones[:, :], 1.0))
                gp.affine_select(out=tri[:, :], in_=ones[:, :], compare_op=ALU.is_ge, fill=0.0, base=0,
                                 pattern=[[1, P]], channel_multiplier=-1).then_inc(gpsimd_once, 1)
                step(gp.memset(EX, 1.0))
                step(gp.affine_select(out=EX, in_=EX, compare_op=ALU.is_ge, fill=0.0, base=0,
                                      pattern=[[P, KT], [1, P]], channel_multiplier=-HD))
                gp.affine_select(out=EX, in_=EX, compare_op=ALU.is_ge, fill=0.0, base=HD - 1,
                                 pattern=[[-P, KT], [-1, P]], channel_multiplier=HD).then_inc(gpsimd_once, 1)
                step(gp.memset(zrow, 0.0))
                gp.iota(itmp[:, 0:NBLK], pattern=[[1, NBLK]], base=0, channel_multiplier=0).then_inc(gc, 1)
                gp.iota(tokid, pattern=[[P, NTT]], base=0, channel_multiplier=1).then_inc(gc, 1)
                step.n += 2
                gp.wait_ge(gc, step.n)
                step(gp.tensor_scalar(tokv[:, :], tokid, -float(NO_TOKEN), None, ALU.add))
                step(gp.affine_select(out=tokv[:, :], in_=tokv[:, :], compare_op=ALU.is_ge, fill=0.0,
                                      base=SEQ + DEC - 1, pattern=[[-P, NTT]], channel_multiplier=-1))
                gp.tensor_scalar(desc[:, :], itmp[:, 0:EG], -1.0, float(EG), ALU.mult, ALU.add).then_inc(gpsimd_once, 1)
                gp.tensor_copy(eidx[:, :], itmp[:, 0:NE]).then_inc(gpsimd_once, 1)
                gp.tensor_copy(qidx[:, :], itmp[:, :]).then_inc(gpsimd_once, 1)
                for b in range(2):
                    gp.wait_ge(ada_mm[b], 2)
                gp.memset(uT[:, :, SEQ:TE], 0.0).then_inc(gpsimd_once, 1)
                for b in range(2):
                    gp.wait_ge(ada_mm[b], 6)
                for b in range(2):
                    gp.memset(xb2[b][:, 0:3], 0.0).then_inc(gpsimd_once, 1)
                with gp.Fori(0, 4) as i:
                    for b in range(2):
                        gp.wait_ge(xo_ready[b], i + 1)
                        gp.dma_start(x_d[bass.ds(i * 2 + b, 1), :, :].rearrange("a p t -> (a p) t"),
                                     xo[b]).then_inc(xo_stored[b], 16)
                        gp.dma_start(ys_d[bass.ds((i * 2 + b) * (NOV // 8 * CAP) + NE * CAP, NOV // 8 * CAP), :]
                                     .rearrange("(p r) (h n) -> p (r h) n", p=P, h=2),
                                     zrow.unsqueeze(1).to_broadcast([P, NOV // 4, D // 2])).then_inc(ys_zeroed, 16)
                        gp.wait_ge(xo_stored[b], i * 16 + 16)
                        gp.wait_ge(ys_zeroed, i * 32 + (16 * b + 16))
                        gp.sem_inc(pool_gate, 1)
                with gp.Fori(0, 4) as i:
                    for b in range(2):
                        gp.wait_ge(xo_ready[b], i + 7)
                        gp.dma_start(z_d[bass.ds(i * 2 + b, 1), :, :].rearrange("a p t -> (a p) t"),
                                     xo[b]).then_inc(xo_stored[b], 16)
                        gp.wait_ge(xo_stored[b], i * 16 + 80)

                gp.wait_ge(vector_once, ACST_READY)
                gp.dma_start(acs_d.rearrange("c (h l) -> (c h) l", h=HEADS), acsT).then_inc(acs_stored, 16)
                gp.wait_ge(vector_once, BT_READY)
                gp.wait_ge(xo_stored[0], 16 * 8)
                gp.wait_ge(xo_stored[1], 16 * 8)
                gp.memset(xbl[:, 0:3], 0.0).then_inc(gpsimd_once, 1)
                gp.memset(Sst, 0.0).then_inc(gpsimd_once, 1)
                gp.memset(BDa, 0.0).then_inc(gpsimd_once, 1)
                gp.memset(BDx, 0.0).then_inc(gpsimd_once, 1)
                gp.wait_ge(gpsimd_once, XB_ZEROED)
                with gp.Fori(0, NT) as j:
                    gp.wait_ge(st_mm, j)
                    gp.sem_inc(pool_gate, 1)
                    gp.tensor_copy(bst, Btok[:, bass.ds(j, 1), :, :].rearrange("p a g n -> p (a g) n"))\
                        .then_inc(bst_ready, 1)
                    gp.wait_ge(state_ready, j)
                    gp.wait_ge(y_mm, j)
                    gp.sem_inc(pool_gate, 1)
                    gp.tensor_copy(Sin, Sst).then_inc(sin_ready, 1)
                    gp.tensor_tensor(stmp.rearrange("p k (h q) -> p (k h) q", h=2),
                                     Sst.rearrange("p k (h q) -> p (k h) q", h=2),
                                     CD[:, bass.ds(j, 1), :].rearrange("p a h -> p (a h)").unsqueeze(2)
                                     .to_broadcast([P, HEADS, HD]), ALU.mult).then_inc(stmp_ready, 1)
                    gp.wait_ge(xst_loaded, j * 16 + 16)
                    gp.wait_ge(ysc_ready, j)
                    gp.tensor_tensor(xD, xst, Dch[:, :].unsqueeze(2).to_broadcast([P, KT, P]), ALU.mult)\
                        .then_inc(xd_ready, 1)
                    gp.wait_ge(er_ready, j + 1)
                    for g in range(2):
                        hs = slice(8 * g, 8 * g + 8)
                        gp.tensor_tensor(ER[:, hs, :], ER[:, hs, :],
                                         BC[:, 2 + g:3 + g, bass.ds(j * P, P)].to_broadcast([P, 8, P]),
                                         ALU.mult).then_inc(ec_ready, 1)
                    gp.wait_ge(ysc_ready, j + 1)
                    gp.dma_start(y_d[KT:2 * KT, :, bass.ds(j * P, P)].rearrange("k p t -> p k t"), ysC)\
                        .then_inc(ysc_stored, 16)
                    gp.wait_ge(yl_ready, j + 1)
                    gp.dma_start(y_d[bass.ds(j, 1), :, :].rearrange("a p t -> (a p) t"), yl[:, 0:SEQ])\
                        .then_inc(yl_stored, 16)
                    gp.wait_ge(ysc_stored, j * 16 + 16)
                    gp.wait_ge(yl_stored, j * 16 + 16)
                    gp.sem_inc(pool_gate, 1)

                gp.wait_ge(vector_once, BCR_READY)
                gp.dma_start(bcs_d.rearrange("i (b n) -> b i n", b=DEC), bcr.rearrange("p (i n) -> p i n", i=4))\
                    .then_inc(bcr_stored, 16)
            def copy3(b):
                return PS[:, b:b + 3, 0:CH]

            @block.scalar
            def _(act):
                step = Chain(act, ac)
                act.wait_ge(c_loaded, 32)
                act.activation(cs, cin, ACT.Tanh, scale=0.5).then_inc(scalar_once, 1)
                act.wait_ge(vector_once, LAM_READY)
                act.activation(sm[:, 1, 0:8], sm[:, 0, 0:8], ACT.Exp, scale=-1.0).then_inc(scalar_once, 1)
                def x_root(t):
                    act.wait_ge(var_ready, t + 1)
                    act.activation(rstd[:, :], mv[:, 1:2], ACT.Sqrt).then_inc(std_ready, 1)

                with act.Fori(0, 3) as i:
                    for b in range(2):
                        x_root(i * 2 + b)
                        act.wait_ge(xn_ready[b], i + 1)
                        act.dma_start(xt[b], x_prompt[0, bass.ds((i * 2 + (2 + b)) * P, P), :]).then_inc(xt_loaded[b], 16)
                x_root(NT - 2)
                act.wait_ge(xn_ready[0], 4)
                act.dma_start(xt[0][0:DEC, :], x_sample[:, 0, :]).then_inc(xt_loaded[2], 16)
                x_root(NT - 1)
                act.wait_ge(var_ready, 9)
                act.activation(rstd[0:DEC, :], mv[0:DEC, 1:2], ACT.Sqrt).then_inc(std_ready, 1)

                def conv_tile(b, r, t):
                    act.wait_ge(proj_mm[b], r + 1)
                    act.wait_ge(gpsimd_once, XB2_ZEROED)
                    act.wait_ge(conv_done[b], r)
                    act.activation(xb2[b][:, 3:3 + TE].rearrange("p (a t) -> p a t", a=3), copy3(3 * b),
                                   ACT.Copy).then_inc(px_copied[b], 1)
                    act.wait_ge(px_copied[b], r + 1)
                    rows = xb2[b][:, SEQ + 3:SEQ + 3 + 4 * DEC].rearrange("p (r k) -> p r k", k=4)
                    act.wait_ge(cur_ready[b], r + 1)
                    act.activation(rows[:, :, 0:3], cur2[b][:, 5:29].rearrange("p (r k) -> p r k", k=3),
                                   ACT.Copy).then_inc(hist_set[b], 1)
                    act.wait_ge(hist_set[b], r + 1)
                    act.activation(cso[:, bass.ds(t + KT, 1), 0:3].rearrange("p a k -> p (a k)"),
                                   xb2[b][:, SEQ:SEQ + 3], ACT.Copy).then_inc(al, 1)
                    act.activation(cso[:, bass.ds(t + KT, 1), 3:27].rearrange("p a (r k) -> p (a r) k", k=3),
                                   rows[:, :, 1:4], ACT.Copy).then_inc(al, 1)
                    act.wait_ge(al, t * 2 + 2)
                    act.wait_ge(conv_done[b], r + 1)
                    act.wait_ge(xo_ready[b], r)
                    act.activation(cth[b], cacc[b], ACT.Tanh).then_inc(cth_ready[b], 1)

                act.wait_ge(mod_stored, 16)
                for b in range(2):
                    act.wait_ge(uT_ready[b], 4)
                act.wait_ge(uT_ready[2], 1)
                for a in range(3):
                    act.activation(us[:, 0, :, a * CH:(a + 1) * CH], uT[:, :, a * CH:(a + 1) * CH], ACT.Copy)\
                        .then_inc(uh_ready, 1)
                act.wait_ge(small_loaded, 64)
                act.activation(wdts[:, 0, :, :], wdt[:, :, :], ACT.Copy).then_inc(uh_ready, 1)

                def w_high(b, r):
                    act.wait_ge(w_loaded[b], r * 16 + 16)
                    act.wait_ge(proj_mm[b], r)
                    act.activation(wss[b][:, 0, :, :], wsl[b], ACT.Copy).then_inc(wh_ready[b], 1)

                def z_tile(b, i):
                    act.wait_ge(proj_mm[b], i + 7)
                    act.wait_ge(xo_ready[b], i + 6)
                    act.activation(cth[b].rearrange("p (a t) -> p a t", a=3), copy3(3 * b), ACT.Tanh,
                                   scale=0.5).then_inc(cth_ready[b], 1)

                with act.Fori(0, 6) as i:
                    for b in range(2):
                        w_high(b, i + 1)
                        conv_tile(b, i, i * 2 + b)
                act.wait_ge(tensor_once, DTP_MM)
                for a in range(2):
                    act.activation(dtT[a], PS[0:HEADS, 6 + a, :], ACT.Copy).then_inc(scalar_once, 1)
                w_high(0, 7)
                z_tile(0, 0)
                act.wait_ge(vector_once, DTE_IN)
                act.activation(dtr[:, 6, :, :], dtr[:, 7, :, :], ACT.Exp, scale=-1.0).then_inc(scalar_once, 1)
                act.activation(dtb[:, 1, :], dtb[:, 1, :], ACT.Exp).then_inc(scalar_once, 1)
                w_high(1, 7)
                z_tile(1, 0)
                with act.Fori(1, 3) as i:
                    for b in range(2):
                        w_high(b, i + 7)
                        z_tile(b, i)
                act.wait_ge(vector_once, DXE_IN)
                act.activation(DXW[:, 0:NT, :], DXW[:, 0:NT, :], ACT.Exp).then_inc(scalar_once, 1)
                act.activation(CD[:, 0:NT, :], TOT[:, 0:NT, :], ACT.Exp).then_inc(scalar_once, 1)
                act.activation(CD[:, NT, :], DTA[:, NT, :], ACT.Exp).then_inc(scalar_once, 1)
                for b in range(2):
                    z_tile(b, 3)
                act.wait_ge(vector_once, BT_READY)
                act.wait_ge(xo_stored[0], 16 * 8)
                act.wait_ge(xo_stored[1], 16 * 8)
                with act.Fori(0, NT) as j:
                    act.wait_ge(r_loaded, j * 16 + 16)
                    act.wait_ge(y_mm, j)
                    act.activation(ER, Rb, ACT.Exp).then_inc(er_ready, 1)
                    act.wait_ge(seg_ready, j + 1)
                    act.activation(SEG, SEG, ACT.Exp).then_inc(segx_ready, 1)
                    act.wait_ge(proj_mm[0], j + 11)
                    act.wait_ge(xlc_ready, j)
                    act.wait_ge(gpsimd_once, XB_ZEROED)
                    act.activation(xbl[:, 3:3 + TE].rearrange("p (a t) -> p a t", a=3), copy3(0),
                                   ACT.Copy).then_inc(xl_copied, 1)
                    act.wait_ge(xl_copied, j + 1)
                    rows = xbl[:, SEQ + 3:SEQ + 3 + 4 * DEC].rearrange("p (r k) -> p r k", k=4)
                    act.wait_ge(cur_ready[0], j + 7)
                    act.activation(rows[:, :, 0:3], cur1[:, 18:42].rearrange("p (r k) -> p r k", k=3),
                                   ACT.Copy).then_inc(lhist_set, 1)
                    act.wait_ge(lhist_set, j + 1)
                    act.activation(cso[:, bass.ds(j, 1), 0:3].rearrange("p a k -> p (a k)"),
                                   xbl[:, SEQ:SEQ + 3], ACT.Copy).then_inc(al, 1)
                    act.activation(cso[:, bass.ds(j, 1), 3:27].rearrange("p a (r k) -> p (a r) k", k=3),
                                   rows[:, :, 1:4], ACT.Copy).then_inc(al, 1)
                    act.wait_ge(proj_mm[1], j + 11)
                    act.wait_ge(yl_ready, j)
                    act.activation(gl.rearrange("p (a t) -> p a t", a=3), copy3(3), ACT.Gelu_apprx_tanh)\
                        .then_inc(gl_ready, 1)
                    act.wait_ge(r_mm, j + 1)
                    act.activation(thr.rearrange("p (a t) -> p a t", a=3), copy3(0), ACT.Tanh, scale=0.5,
                                   bias=cur1[:, 5:6]).then_inc(thr_ready, 1)
                    act.wait_ge(thr_ready, j + 1)
                    act.wait_ge(yl_ready, j)
                    act.activation(lt, thr, ACT.Tanh, scale=cur1[:, 7:8], bias=cur1[:, 7:8]).then_inc(lt_ready, 1)
                    act.activation(la, thr, ACT.Exp, scale=cur1[:, 8:9], bias=cur1[:, 8:9]).then_inc(la_ready, 1)
                    act.wait_ge(la_ready, j + 1)
                    act.activation(la2, la, ACT.Square).then_inc(la2_ready, 1)
                    act.wait_ge(i_mm, j + 1)
                    act.activation(thi.rearrange("p (a t) -> p a t", a=3), copy3(3), ACT.Tanh, scale=0.5,
                                   bias=cur1[:, 6:7]).then_inc(thi_ready, 1)
                    act.wait_ge(ls_ready, j * 2 + 1)
                    act.activation(lt, lt, ACT.Sqrt, scale=0.25).then_inc(ls_ready, 1)
                act.wait_ge(tensor_once, CO_MM)
                for a in range(5):
                    step(act.activation(co[:, 512 * a:512 * a + 512], PS[0:27, a, :], ACT.Copy))
                act.wait_ge(tensor_once, HO_MM)
                act.activation(ho.rearrange("p (a n) -> p a n", a=2), PS[0:9, 5:7, :], ACT.Copy).then_inc(scalar_once, 1)
                act.sem_inc(scalar_once, 1)
                act.wait_ge(tensor_once, SO_MM)
                act.activation(So, PS[:, 0:2, :].rearrange("p a (k n) -> p (a k) n", n=P), ACT.Copy).then_inc(scalar_once, 1)


            @block.tensor
            def _(pe):
                pe.wait_ge(gpsimd_once, IDENT_MADE)

                pe.wait_ge(rows_loaded, 16 * 9)
                for k in range(KT):
                    mm = pe.transpose(PS[:, 4, 42 * k:42 * k + 42], prow[:, k * P:(k + 1) * P], ident[0:42, 0:42])
                mm.then_inc(tensor_once, 1)
                pe.wait_ge(rows2_loaded, 16 * 3)
                for k in range(XT):
                    mm = pe.transpose(PS[:, 5, 29 * k:29 * k + 29], prow2[:, k * P:(k + 1) * P], ident[0:29, 0:29])
                mm.then_inc(tensor_once, 1)
                pe.wait_ge(vector_once, CS_READY)
                for k in range(KT):
                    mm = pe.transpose(PS[:, 6, 9 * k:9 * k + 9], cs[:, k * P:(k + 1) * P], ident[0:9, 0:9])
                mm.then_inc(tensor_once, 1)
                pe.wait_ge(vector_once, CT_READY)

                def ada(b, r, w, loaded, rounds):
                    pe.wait_ge(loaded[b], rounds * 16)
                    pe.wait_ge(ada_ready[b], r)
                    for k in range(KT):
                        mm = pe.matmul(PS[0:9, b, :], cT[:, k, :], w[b][:, k, :], start=(k == 0), stop=(k == KT - 1))
                    mm.then_inc(ada_mm[b], 1)

                for b in range(2):
                    ada(b, 0, adaw, adaw_loaded, 1)
                for b in range(2):
                    ada(b, 1, early, early_loaded, 1)
                pe.wait_ge(vector_once, SC1_READY)
                pe.wait_ge(vector_once, PT_READY)
                for s in range(2):
                    for k in range(KT):
                        mm = pe.transpose(PS[:, 6, 72 + 9 * (s * KT + k):72 + 9 * (s * KT + k) + 9],
                                          mod[:, s * D + k * P:s * D + (k + 1) * P], ident[0:9, 0:9])
                mm.then_inc(tensor_once, 1)
                with pe.Fori(0, 4) as i:
                    for b in range(2):
                        ada(b, i + 2, adaw, adaw_loaded, i + 2)
                        pe.wait_ge(xn_ready[b], i + 1)
                        pe.wait_ge(uT_ready[b], i)
                        for k in range(KT):
                            mm = pe.transpose(PS[:, 2 + 2 * b + k // 4, P * (k % 4):P * (k % 4) + P],
                                              xn[b][:, k * P:(k + 1) * P], ident[:, :])
                        mm.then_inc(xnT_mm[b], 1)
                pe.wait_ge(xn_ready[2], 1)
                pe.wait_ge(vector_once, SS_READY)
                for k in range(KT):
                    mm = pe.transpose(PS[:, 6, 8 * k:8 * k + 8], xn[0][0:DEC, k * P:(k + 1) * P], ident[0:DEC, 0:DEC])
                mm.then_inc(xnT_mm[2], 1)

                def project(b, w_round):
                    pe.wait_ge(w_loaded[b], w_round * 16 + 16)
                    for k in range(KT):
                        for a in range(3):
                            mm = pe.matmul(PS[:, 3 * b + a, 0:CH], wsl[b][:, k, :], uT[:, k, a * CH:(a + 1) * CH],
                                           start=(k == 0), stop=(k == KT - 1))
                    mm.then_inc(proj_mm[b], 1)

                for b in range(2):
                    pe.wait_ge(uT_ready[b], 4)
                pe.wait_ge(uT_ready[2], 1)
                PARTS = ((0, 0), (0, 1), (1, 0))

                def project_split(b, w_round):
                    pe.wait_ge(wh_ready[b], w_round)
                    pe.wait_ge(wl_ready[b], w_round)
                    for k in range(KT):
                        for i, j in PARTS:
                            for a in range(3):
                                mm = pe.matmul(PS[:, 3 * b + a, 0:CH], wss[b][:, i, k, :], us[:, j, k, a * CH:(a + 1) * CH],
                                               start=(k == 0 and (i, j) == PARTS[0]),
                                               stop=(k == KT - 1 and (i, j) == PARTS[-1]))
                    mm.then_inc(proj_mm[b], 1)

                for b in range(2):
                    project(b, 0)
                pe.wait_ge(uh_ready, 3)
                pe.wait_ge(ul_ready, 3)
                with pe.Fori(0, 5) as i:
                    for b in range(2):
                        pe.wait_ge(px_copied[b], i + 1)
                        project_split(b, i + 1)
                pe.wait_ge(uh_ready, 4)
                pe.wait_ge(ul_ready, 4)
                for s in range(2):
                    for k in range(KT):
                        for i, j in PARTS:
                            mm = pe.matmul(PS[0:HEADS, 6 + s, :], wdts[:, i, k, :], us[:, j, k, 512 * s:512 * s + 512],
                                           start=(k == 0 and (i, j) == PARTS[0]), stop=(k == KT - 1 and (i, j) == PARTS[-1]))
                mm.then_inc(tensor_once, 1)
                pe.wait_ge(xo_ready[0], 6)
                project_split(0, 6)
                pe.wait_ge(scalar_once, DTT_READY)
                pe.wait_ge(gpsimd_once, EX_MADE)
                pe.wait_ge(small_loaded, 64)
                for k in range(KT):
                    mm = pe.matmul(PS[:, 7, 384 + k:385 + k], EX[:, k, :], Dh[:, :], start=True, stop=True)
                mm.then_inc(tensor_once, 1)
                for t in range(NT):
                    pe.transpose(PS[:, 6, 128 + HEADS * t:128 + HEADS * (t + 1)], dtT[t // 4][:, P * (t % 4):P * (t % 4) + P],
                                 ident[0:HEADS, 0:HEADS])
                for k in range(KT):
                    mm = pe.matmul(PS[0:DEC, 6, 128 + HEADS * NT:128 + HEADS * NTT], uT[:, k, S0:TE:CONV], wdt[:, k, :],
                                   start=(k == 0), stop=(k == KT - 1))
                mm.then_inc(tensor_once, 1)
                pe.wait_ge(xo_ready[1], 6)
                project_split(1, 6)
                with pe.Fori(1, 3) as i:
                    for b in range(2):
                        pe.wait_ge(xo_ready[b], i + 6)
                        project_split(b, i + 6)
                pe.wait_ge(vector_once, DTA_READY)
                pe.wait_ge(gpsimd_once, TRI_MADE)
                pe.matmul(PS[:, 7, 0:P], tri[:, :], DTA[:, 0:NT, :], start=True, stop=True)
                pe.matmul(PS[:, 7, P:2 * P], ones[:, :], DTA[:, 0:NT, :], start=True, stop=True).then_inc(tensor_once, 1)
                pe.wait_ge(vector_once, ACS_COPIED)
                pe.transpose(PS[:, 7, 2 * P:3 * P], ACS[:, 0:NT, :].rearrange("p c h -> p (c h)"), ident[:, :])\
                    .then_inc(tensor_once, 1)
                for b in range(2):
                    pe.wait_ge(xo_ready[b], 9)
                    project_split(b, 9)
                pe.wait_ge(xo_ready[0], 10)
                pe.wait_ge(xo_ready[1], 10)
                for c in range(NT):
                    for g in range(2):
                        n = 2 * c + g
                        mm = pe.matmul(PS[:, n // 4, P * (n % 4):P * (n % 4) + P], BC[:, g, c * P:(c + 1) * P],
                                       BC[:, 2 + g, c * P:(c + 1) * P], start=True, stop=True)
                mm.then_inc(tensor_once, 1)
                pe.wait_ge(vector_once, CB_READY)
                for c in range(NT):
                    for g in range(2):
                        n = 2 * c + g
                        mm = pe.transpose(PS[:, n // 4, P * (n % 4):P * (n % 4) + P], BC[:, g, c * P:(c + 1) * P],
                                          ident[:, :])
                mm.then_inc(tensor_once, 1)
                pe.wait_ge(vector_once, BT_READY)

                pe.wait_ge(vector_once, ACST_READY)
                with pe.Fori(0, NT) as j:
                    pe.wait_ge(thr_ready, j)
                    project(0, j + 10)
                    pe.wait_ge(xst_loaded, j * 16 + 16)
                    pe.wait_ge(ysc_ready, j)
                    for k in range(KT):
                        mm = pe.transpose(PS[:, 6 + k // 4, P * (k % 4):P * (k % 4) + P], xst[:, k, :], ident[:, :])
                    mm.then_inc(xt_mm, 1)
                    pe.wait_ge(thi_ready, j)
                    project(1, j + 10)
                    pe.wait_ge(xw_ready, j + 1)
                    pe.wait_ge(bst_ready, j + 1)
                    for g in range(2):
                        mm = pe.matmul(PS[:, 6 + g, :], bst[:, g, :],
                                       xw[:, 4 * g:4 * g + 4, :].rearrange("p k c -> p (k c)"), start=True, stop=True)
                    mm.then_inc(st_mm, 1)
                    pe.wait_ge(bd_loaded, j * 64 + 64)
                    pe.wait_ge(gpsimd_once, BD_ZEROED)
                    pe.wait_ge(xlc_ready, j + 1)
                    for a in range(3):
                        mm = pe.matmul(PS[:, a, 0:CH], BDa, xlc[:, a * CH:(a + 1) * CH], start=True, stop=True)
                    mm.then_inc(r_mm, 1)
                    pe.wait_ge(m_ready, j * 2 + 2)
                    pe.wait_ge(ec_ready, j * 2 + 2)
                    pe.wait_ge(sin_ready, j + 1)
                    pe.wait_ge(state_ready, j + 1)
                    for h in range(HEADS):
                        k, q = h // 2, HD * (h % 2)
                        dst = PS[q:q + HD, 6 + k // 4, P * (k % 4):P * (k % 4) + P]
                        pe.matmul(dst, xdt[:, k, q:q + HD], SEG[:, h, :], start=True, stop=False)
                        mm = pe.matmul(dst, Sin[:, k, q:q + HD], ER[:, h, :], start=False, stop=True)
                    mm.then_inc(y_mm, 1)
                    pe.wait_ge(gl_ready, j + 1)
                    for a in range(3):
                        mm = pe.matmul(PS[:, 3 + a, 0:CH], BDx, xlc[:, a * CH:(a + 1) * CH], start=True, stop=True)
                    mm.then_inc(i_mm, 1)
                pe.wait_ge(ysc_ready, NT)
                pe.wait_ge(thi_ready, NT)
                pe.wait_ge(scalar_once, DXE_READY)
                pe.transpose(PS[0:HEADS, 7, 0:DEC], DT[0:DEC, NT, :], ident[0:DEC, 0:DEC])
                pe.transpose(PS[0:HEADS, 7, DEC:2 * DEC], CD[0:DEC, NT, :], ident[0:DEC, 0:DEC]).then_inc(tensor_once, 1)
                for i in range(4):
                    mm = pe.transpose(PS[0:DEC, 6, P * i:P * (i + 1)], BC[:, i, S0:TE:CONV], ident[:, :])
                mm.then_inc(tensor_once, 1)
                pe.wait_ge(al, 2 * (NT + XT))
                for k in range(KT + XT):
                    mm = pe.transpose(PS[0:27, k // 4, P * (k % 4):P * (k % 4) + P], cso[:, k, :], ident[:, :])
                mm.then_inc(tensor_once, 1)
                pe.wait_ge(vector_once, DC_READY)
                for k in range(KT):
                    mm = pe.matmul(PS[:, 7, 64 + 16 * k:80 + 16 * k], EX[:, k, :], dcT, start=True, stop=True)
                mm.then_inc(tensor_once, 1)
                pe.wait_ge(ys_copied, NT)
                pe.wait_ge(vector_once, BCR_READY)
                for k in range(KT):
                    mm = pe.transpose(PS[0:9, 5 + k // 4, P * (k % 4):P * (k % 4) + P], hso[:, k, :], ident[:, :])
                mm.then_inc(tensor_once, 1)
                pe.wait_ge(scalar_once, CO_READY)
                for k in range(KT):
                    mm = pe.transpose(PS[:, k // 4, P * (k % 4):P * (k % 4) + P], Sst[:, k, :], ident[:, :])
                mm.then_inc(tensor_once, 1)


            @block.vector
            def _(ve):
                step = Chain(ve, vc)

                def log1p_exp_minus(out, x, z, s, s2, q):
                    step(ve.tensor_scalar(s, z, 2.0, None, ALU.add))
                    step(ve.reciprocal(s, s))
                    step(ve.tensor_tensor(s, s, z, ALU.mult))
                    step(ve.tensor_tensor(s2, s, s, ALU.mult))
                    step(ve.tensor_scalar(q, s2, 1.0 / 15, None, ALU.mult))
                    for c in (13, 11, 9, 7, 5, 3):
                        step(ve.scalar_tensor_tensor(out=q, in0=q, scalar=1.0 / c, in1=s2, op0=ALU.add, op1=ALU.mult))
                    step(ve.scalar_tensor_tensor(out=q, in0=q, scalar=1.0, in1=s, op0=ALU.add, op1=ALU.mult))
                    step(ve.tensor_scalar(out, x, 0.0, None, ALU.max))
                    step(ve.scalar_tensor_tensor(out=out, in0=q, scalar=2.0, in1=out, op0=ALU.mult, op1=ALU.add))

                ve.wait_ge(scalar_once, CSIG_READY)
                ve.scalar_tensor_tensor(out=cs, in0=cs, scalar=1.0, in1=cin, op0=ALU.add, op1=ALU.mult)\
                    .then_inc(vector_once, 1)
                ve.wait_ge(tensor_once, PT1_MM)
                step(ve.tensor_copy(PT1[:, :, :], PS[:, 4, 0:42 * KT].rearrange("p (k c) -> p k c", k=KT)))
                ve.wait_ge(tensor_once, PT2_MM)
                step(ve.tensor_copy(PT2[:, :, :], PS[:, 5, 0:29 * XT].rearrange("p (k c) -> p k c", k=XT)))
                ve.tensor_scalar(PT1[:, :, 5:7], PT1[:, :, 5:7], 0.5, None, ALU.mult).then_inc(vector_once, 1)
                ve.tensor_scalar(PT2[:, :, 0:5], PT2[:, :, 0:5], 0.5, None, ALU.mult).then_inc(vector_once, 1)
                ve.wait_ge(tensor_once, CT_MM)
                ve.tensor_scalar(cT[:, :, :], PS[:, 6, 0:72].rearrange("p (k c) -> p k c", k=KT), 0.5, None, ALU.mult)\
                    .then_inc(vector_once, 1)
                lamv = [sm[:, i, 0:8] for i in range(6)]
                step(ve.tensor_scalar(lamv[2], PT1[:, :, 7], -1.0, None, ALU.mult))
                ve.tensor_tensor(lamv[0], lamv[2], PT1[:, :, 7], ALU.max).then_inc(vector_once, 1)
                ve.wait_ge(scalar_once, LAMEXP)
                log1p_exp_minus(lamv[0], lamv[2], lamv[1], lamv[3], lamv[4], lamv[5])
                step(ve.tensor_scalar(spl[:, :, 0], lamv[0], LRU_C / 2, None, ALU.mult))
                step(ve.tensor_scalar(spl[:, :, 1], lamv[0], -LRU_C / 2, None, ALU.mult))

                def normalise(src, dst, rows, n, done):
                    st = Chain(ve, vl, n * 4)
                    for h in range(2):
                        st(ve.bn_stats(stat[0:rows, 6 * h:6 * h + 6], src[0:rows, 512 * h:512 * h + 512]))
                    ve.sem_inc(vector_gate, 1)
                    st(ve.bn_aggr(mv[0:rows, :], stat[0:rows, :].rearrange("p (a s) -> p a s", a=2)))
                    ve.tensor_scalar(mv[0:rows, 1:2], mv[0:rows, 1:2], LN_EPS, None, ALU.add).then_inc(var_ready, 1)
                    ve.wait_ge(std_ready, n + 1)
                    st(ve.reciprocal(rstd[0:rows, :], rstd[0:rows, :]))
                    ve.tensor_scalar(dst[0:rows, :], src[0:rows, :], mv[0:rows, 0:1], rstd[0:rows, :],
                                     ALU.subtract, ALU.mult).then_inc(done, 1)

                def ada_out(b, r, chunk):
                    ve.wait_ge(ada_mm[b], r + 1)
                    part = bass.ds(chunk * 512, 512)
                    ve.tensor_tensor(mod[:, part], PS[0:9, b, :], bada[:, part], ALU.add).then_inc(ada_ready[b], 1)

                def norm_tile(t, b, r):
                    ve.wait_ge(xt_loaded[b], r * 16 + 16)
                    ve.wait_ge(xnT_mm[b], r)
                    normalise(xt[b], xn[b], P, t, xn_ready[b])

                ve.wait_ge(bada_loaded, 16)
                for b in range(2):
                    ada_out(b, 0, b)
                ada_out(0, 1, 2)
                norm_tile(0, 0, 0)
                ada_out(1, 1, 3)
                for b in range(2):
                    ve.wait_ge(ada_ready[b], 2)
                ve.tensor_scalar(mod[:, D:2 * D], mod[:, D:2 * D], 1.0, None, ALU.add).then_inc(vector_once, 1)
                ve.wait_ge(tensor_once, SS_MM)
                ve.tensor_copy(ssT[:, :, :, :], PS[:, 6, 72:216].rearrange("p (s k c) -> p s k c", s=2, k=KT))\
                    .then_inc(vector_once, 1)
                ve.wait_ge(gpsimd_once, UZ)
                ve.wait_ge(vector_once, SS_READY)

                def modulate(b, i):
                    ada_out(b, i + 2, i * 2 + (4 + b))
                    ve.wait_ge(xnT_mm[b], i + 1)
                    ve.wait_ge(uT_ready[1 - b], i + b)
                    ve.tensor_tensor(ltmp, PS[:, 2 + 2 * b:4 + 2 * b, :].rearrange("p a (k t) -> p (a k) t", t=P),
                                     ssT[:, 1, :, 0:1].to_broadcast([P, KT, P]), ALU.mult).then_inc(ltmp_ready, 1)
                    ve.wait_ge(ltmp_ready, i * 2 + (b + 1))
                    ve.tensor_tensor(uT[:, :, bass.ds((i * 2 + b) * P, P)], ltmp,
                                     ssT[:, 0, :, 0:1].to_broadcast([P, KT, P]), ALU.add).then_inc(uT_ready[b], 1)

                with ve.Fori(0, NT // 2 - 1) as i:
                    norm_tile(i * 2 + 1, 1, i)
                    modulate(0, i)
                    norm_tile(i * 2 + 2, 0, i + 1)
                    modulate(1, i)
                norm_tile(NT - 1, 1, NT // 2 - 1)
                for b in range(2):
                    modulate(b, NT // 2 - 1)
                ve.wait_ge(xt_loaded[2], 16)
                ve.wait_ge(xnT_mm[0], 4)
                normalise(xt[0], xn[0], DEC, 8, xn_ready[2])
                ve.wait_ge(xnT_mm[2], 1)
                step(ve.tensor_tensor(ltmp[:, :, 0:DEC], PS[:, 6, 0:64].rearrange("p (k t) -> p k t", k=KT),
                                      ssT[:, 1, :, 1:9], ALU.mult))
                ve.tensor_tensor(uT[:, :, S0:TE:CONV], ltmp[:, :, 0:DEC], ssT[:, 0, :, 1:9], ALU.add)\
                    .then_inc(uT_ready[2], 1)
                ve.wait_ge(ada_ready[0], 6)
                ve.wait_ge(ada_ready[1], 6)
                ve.tensor_scalar(mod[:, 4 * D:5 * D], mod[:, 4 * D:5 * D], 1.0, None, ALU.add).then_inc(vector_once, 1)

                def conv(out, row, cur, st, done):
                    st(ve.tensor_scalar(out, row[:, 0:TE], cur[:, 0:1], cur[:, 4:5], ALU.mult, ALU.add))
                    for k in (1, 2):
                        st(ve.scalar_tensor_tensor(out=out, in0=row[:, k:k + TE], scalar=cur[:, k:k + 1], in1=out,
                                                   op0=ALU.mult, op1=ALU.add))
                    ve.scalar_tensor_tensor(out=out, in0=row[:, 3:3 + TE], scalar=cur[:, 3:4], in1=out,
                                            op0=ALU.mult, op1=ALU.add).then_inc(done, 1)

                def conv_tile(b, r, t, out):
                    ve.tensor_copy(cur2[b][:, :], PT2[:, bass.ds(t, 1), :].rearrange("p a c -> p (a c)"))\
                        .then_inc(cur_ready[b], 1)
                    ve.wait_ge(cur_ready[b], r + 1)
                    ve.wait_ge(hist_set[b], r + 1)
                    ve.wait_ge(al, t * 2 + 2)
                    conv(cacc[b], xb2[b], cur2[b], Chain(ve, vl, t * 3 + 36), conv_done[b])
                    ve.wait_ge(conv_done[b], r + 1)
                    ve.wait_ge(cth_ready[b], r + 1)
                    ve.scalar_tensor_tensor(out=out, in0=cth[b], scalar=1.0, in1=cacc[b], op0=ALU.add, op1=ALU.mult)\
                        .then_inc(xo_ready[b], 1)

                for a in range(3):
                    ve.wait_ge(uh_ready, a + 1)
                    part = slice(a * CH, (a + 1) * CH)
                    ve.tensor_tensor(us[:, 1, :, part], uT[:, :, part], us[:, 0, :, part], ALU.subtract).then_inc(ul_ready, 1)
                ve.wait_ge(uh_ready, 4)
                ve.tensor_tensor(wdts[:, 1, :, :], wdt[:, :, :], wdts[:, 0, :, :], ALU.subtract).then_inc(ul_ready, 1)

                def w_low(b, r):
                    ve.wait_ge(wh_ready[b], r)
                    ve.tensor_tensor(wss[b][:, 1, :, :], wsl[b], wss[b][:, 0, :, :], ALU.subtract).then_inc(wl_ready[b], 1)

                def z_tile(b, i):
                    ve.wait_ge(cth_ready[b], i + 7)
                    ve.wait_ge(xo_stored[b], i * 16 + 64)
                    ve.scalar_tensor_tensor(out=xo[b].rearrange("p (a t) -> p a t", a=3),
                                            in0=cth[b].rearrange("p (a t) -> p a t", a=3), scalar=1.0, in1=copy3(3 * b),
                                            op0=ALU.add, op1=ALU.mult).then_inc(xo_ready[b], 1)

                with ve.Fori(0, 4) as i:
                    for b in range(2):
                        w_low(b, i + 1)
                        ve.wait_ge(xo_stored[b], i * 16)
                        conv_tile(b, i, i * 2 + b, xo[b])
                with ve.Fori(0, 2) as i:
                    for b in range(2):
                        w_low(b, i + 5)
                        conv_tile(b, i + 4, i * 2 + (8 + b),
                                  BC[:, bass.ds(i * 2 + b, 1), :].rearrange("p a t -> p (a t)"))
                w_low(0, 7)
                z_tile(0, 0)
                ve.wait_ge(tensor_once, DT_MM)
                raw, az, s1, s2, q1 = dtr[:, 2, :, :], dtr[:, 7, :, :], dtr[:, 3, :, :], dtr[:, 4, :, :], dtr[:, 5, :, :]
                step(ve.memset(raw, 0.0))
                step(ve.tensor_tensor(raw[:, 0:NT, :], PS[:, 6, 128:256].rearrange("p (t h) -> p t h", h=HEADS),
                                      dtb[:, 0:1, :].to_broadcast([P, NT, HEADS]), ALU.add))
                step(ve.tensor_tensor(raw[0:DEC, NT, :], PS[0:DEC, 6, 256:272], dtb[0:DEC, 0, :], ALU.add))
                step(ve.tensor_scalar(az, raw, -1.0, None, ALU.mult))
                ve.tensor_tensor(az, az, raw, ALU.max).then_inc(vector_once, 1)
                ve.wait_ge(scalar_once, DT_EXP)
                log1p_exp_minus(DT, raw, dtr[:, 6, :, :], s1, s2, q1)
                ve.scalar_tensor_tensor(out=DTA, in0=DT, scalar=-1.0, in1=dtb[:, 1:2, :].to_broadcast([P, NT + 1, HEADS]),
                                        op0=ALU.mult, op1=ALU.mult).then_inc(vector_once, 1)
                w_low(1, 7)
                z_tile(1, 0)
                with ve.Fori(1, 3) as i:
                    for b in range(2):
                        w_low(b, i + 7)
                        z_tile(b, i)
                ve.wait_ge(tensor_once, ACS_MM)
                ve.tensor_copy(ACS[:, 0:NT, :], PS[:, 7, 0:P].rearrange("p (c h) -> p c h", h=HEADS))\
                    .then_inc(vector_once, 1)
                ve.tensor_copy(TOT[:, 0:NT, :], PS[:, 7, P:2 * P].rearrange("p (c h) -> p c h", h=HEADS))\
                    .then_inc(vector_once, 1)
                ve.wait_ge(vector_once, ACS_COPIED)
                ve.tensor_tensor(DXW[:, 0:NT, :], TOT[:, 0:NT, :], ACS[:, 0:NT, :], ALU.subtract).then_inc(vector_once, 1)
                ve.wait_ge(tensor_once, ACST_MM)
                ve.tensor_copy(acsT, PS[:, 7, 2 * P:3 * P]).then_inc(vector_once, 1)
                ve.wait_ge(tensor_once, DCH_MM)
                step(ve.tensor_copy(Dch[:, :], PS[:, 7, 384:384 + KT]))
                ve.wait_ge(scalar_once, DXE_READY)
                step(ve.tensor_tensor(DXW[:, 0:NT, :], DXW[:, 0:NT, :], DT[:, 0:NT, :], ALU.mult))
                for b in range(2):
                    z_tile(b, 3)

                ve.wait_ge(tensor_once, CB_MM)
                ve.wait_ge(mod_stored, 16)
                ve.wait_ge(gpsimd_once, TRI_MADE)
                ve.tensor_tensor(CBm.rearrange("p c g l -> p (c g) l"),
                                 PS[:, 0:4, :].rearrange("p a (n l) -> p (a n) l", l=P),
                                 tri[:, :].unsqueeze(1).to_broadcast([P, 2 * NT, P]), ALU.mult).then_inc(vector_once, 1)
                ve.wait_ge(tensor_once, BT_MM)
                ve.tensor_copy(Btok.rearrange("p c g n -> p (c g) n"),
                               PS[:, 0:4, :].rearrange("p a (n l) -> p (a n) l", l=P)).then_inc(vector_once, 1)

                ve.wait_ge(gpsimd_once, XB_ZEROED)
                ve.wait_ge(xo_stored[0], 16 * 8)
                ve.wait_ge(xo_stored[1], 16 * 8)

                def per_head(x, j):
                    return x[:, bass.ds(j, 1), :].rearrange("p a h -> p (a h)").unsqueeze(2)

                def heads(x):
                    return x.rearrange("p k (h q) -> p (k h) q", h=2)

                with ve.Fori(0, NT) as j:
                    st = Chain(ve, vl, j * 14 + 72)
                    ve.wait_ge(thi_ready, j)
                    st(ve.tensor_copy(cur1[:, :], PT1[:, bass.ds(j, 1), :].rearrange("p a c -> p (a c)")))
                    ve.tensor_copy(cur1[:, 7:9], spl[:, bass.ds(j, 1), :].rearrange("p a c -> p (a c)"))\
                        .then_inc(cur_ready[0], 1)
                    st(ve.tensor_copy(acur[:, :], ACS[:, bass.ds(j, 1), :].rearrange("p a h -> p (a h)")))
                    ve.wait_ge(r_loaded, j * 16 + 16)
                    ve.wait_ge(y_mm, j)
                    for h in range(HEADS):
                        ins = ve.tensor_scalar(SEG[:, h, :], Rb[:, h, :], acur[:, h:h + 1], 0.0, ALU.subtract, ALU.min)
                    ins.then_inc(seg_ready, 1)
                    ve.wait_ge(segx_ready, j + 1)
                    for g in range(2):
                        ve.tensor_tensor(SEG[:, 8 * g:8 * g + 8, :], SEG[:, 8 * g:8 * g + 8, :],
                                         CBm[:, bass.ds(j, 1), g, :].to_broadcast([P, 8, P]),
                                         ALU.mult).then_inc(m_ready, 1)
                    ve.wait_ge(lhist_set, j + 1)
                    ve.wait_ge(al, j * 2 + 26)
                    ve.wait_ge(cur_ready[0], j + 7)
                    conv(xlc, xbl, cur1, st, xlc_ready)
                    ve.wait_ge(xt_mm, j + 1)
                    xps = PS[:, 6:8, :].rearrange("p a (h q) -> p (a h) q", q=HD)
                    st(ve.tensor_tensor(heads(xdt), xps, per_head(DT, j).to_broadcast([P, HEADS, HD]), ALU.mult))
                    ve.tensor_tensor(heads(xw), xps, per_head(DXW, j).to_broadcast([P, HEADS, HD]), ALU.mult)\
                        .then_inc(xw_ready, 1)
                    ve.wait_ge(st_mm, j + 1)
                    ve.wait_ge(stmp_ready, j + 1)
                    ve.tensor_tensor(Sst, stmp, PS[:, 6:8, :].rearrange("p a (k c) -> p (a k) c", c=P), ALU.add)\
                        .then_inc(state_ready, 1)
                    ve.wait_ge(y_mm, j + 1)
                    ve.wait_ge(xd_ready, j + 1)
                    ve.wait_ge(zst_loaded, j * 16 + 16)
                    ve.wait_ge(ysc_stored, j * 16)
                    st(ve.tensor_tensor(ysC, xD, PS[:, 6:8, :].rearrange("p a (k c) -> p (a k) c", c=P), ALU.add))
                    ve.scalar_tensor_tensor(out=ysC, in0=ysC, scalar=0.5, in1=zst, op0=ALU.mult, op1=ALU.mult)\
                        .then_inc(ysc_ready, 1)
                    ve.wait_ge(la2_ready, j + 1)
                    ve.scalar_tensor_tensor(out=lt, in0=la2, scalar=1.0, in1=lt, op0=ALU.add, op1=ALU.mult)\
                        .then_inc(ls_ready, 1)
                    ve.wait_ge(thi_ready, j + 1)
                    st(ve.scalar_tensor_tensor(out=thi, in0=thi, scalar=1.0, in1=xlc, op0=ALU.add, op1=ALU.mult))
                    ve.wait_ge(ls_ready, j * 2 + 2)
                    st(ve.tensor_tensor(lt, lt, thi, ALU.mult))
                    st(ve.memset(la[:, S0 - 1:TE:CONV], 0.0))
                    st(ve.tensor_copy(lt[:, S0 - 1:TE:CONV], cur1[:, 10:18]))
                    st(ve.tensor_tensor_scan(thr, la, lt, 0.0, ALU.mult, ALU.add))
                    st(ve.tensor_copy(hso[:, bass.ds(j, 1), 0:1].rearrange("p a c -> p (a c)"), thr[:, SEQ - 1:SEQ]))
                    st(ve.tensor_copy(hso[:, bass.ds(j, 1), 1:9].rearrange("p a c -> p (a c)"), thr[:, S0:TE:CONV]))
                    ve.wait_ge(gl_ready, j + 1)
                    ve.wait_ge(yl_stored, j * 16)
                    ve.tensor_tensor(yl, thr, gl, ALU.mult).then_inc(yl_ready, 1)
                    ve.wait_ge(yl_ready, j + 1)
                    ve.tensor_copy(yS[:, bass.ds(j, 1), :].rearrange("p a c -> p (a c)"), yl[:, S0:TE:CONV])\
                        .then_inc(ys_copied, 1)
                    assert st.n == 14, st.n
                ve.wait_ge(ys_copied, NT)

                ve.wait_ge(tensor_once, DC_MM)
                ve.tensor_copy(dcT, PS[0:HEADS, 7, 0:2 * DEC]).then_inc(vector_once, 1)
                ve.wait_ge(tensor_once, BCR_MM)
                ve.tensor_copy(bcr, PS[0:DEC, 6, :]).then_inc(vector_once, 1)
                ve.wait_ge(tensor_once, EX_MM)
                ve.tensor_copy(exd[:, :, :], PS[:, 7, 64:192].rearrange("p (k c) -> p k c", k=KT)).then_inc(vector_once, 1)
        nc.clear_and_free_semaphores(in_first)
        nc.all_engine_barrier()
        first.close()

        triS = sb("triS", [P, P])
        rs2 = sb("rs2", [P, 2])
        wr = sb("wr", [P, KT, 36])
        brb = sb("brb", [P, 36])
        Lg = sb("Lg", [P, NTT, 36])
        gat = sb("gat", [P, 2, NTT])
        slot = sb("slot", [P, 2, NTT], U32)
        gsm = sb("gsm", [P, 12, NTT])
        gon = sb("gon", [P, 4, NTT, EG])
        cnt = sb("cnt", [P, 6, NE])
        bexp = sb("bexp", [P, NBLK + 1])
        ctl = sb("ctl", [P, 2 * NBLK + 1], I32)
        idxT = sb("idxT", [P, NBLK], I32)
        icur = sb("icur", [P, 1], I32)
        gcur = sb("gcur", [P, 2])
        sl1 = [sb(f"sl1{b}", [P, 2], U32) for b in range(2)]
        arena2 = sb("arena2", [P, 22528])

        def at2(off, *dims, parts=P):
            return at(off, *dims, parts=parts, base=arena2)

        wg, wu, wd = at2(0, KT, FF), at2(4096, KT, FF), at2(8192, FF // P, D)
        xg, yo = at2(12288, D), at2(14336, D)
        hth, hb = at2(16384, FF), at2(16896, FF)
        R0 = 17408
        gate1, ln1g, ln1b, sc2, sh2 = [at2(R0 + 1024 * i, D) for i in range(5)]
        ysum = at2(16640, 2, P)
        xp1 = [at2(14336 + 1024 * b, D) for b in range(2)]
        bcsb = at2(0, 4, DEC * P)
        s0t = [at2(4096 + 1024 * b, DEC, P) for b in range(2)]
        t1t, t2t = at2(6144, DEC, P), at2(7168, DEC, P)
        snt = [at2(8192 + 1024 * b, DEC, P) for b in range(2)]
        xzs = at2(10240, 2, KT, 4 * DEC)
        xdS, yr = at2(10752, KT, DEC), at2(10816, KT, DEC)
        vT = [at2(12288 + 1024 * b, KT, P) for b in range(2)]
        gtmp = [at2(R0 + 2048 + NE * NTT * i, NTT, NE) for i in range(7)]
        ended = at2(14336, NBLK, NE)
        ge = at2(R0, 2 * NTT, NBLK + 1)
        inblk = at2(R0 + 900, 2 * NTT, NBLK)
        inrow = at2(R0 + 1800, 2 * NTT, P)
        rowidx = at2(16384, P)
        rowint = at2(16384 + P, P).bitcast(I32)
        gate2, ln2g, ln2b = [at2(R0 + 1024 * i, D) for i in range(3)]
        xl2 = [at2(R0 + 3072 + 1024 * b, D) for b in range(2)]
        y1s = [at2(1024 * b, D) for b in range(2)]
        y2s = [at2(2048 + 1024 * b, D) for b in range(2)]
        fo = [at2(4096 + 1024 * b, D) for b in range(2)]
        with ExitStack() as f_only:
            farena = sb("farena", [P, 27648], scope=f_only)
            WO = [at(8192 * i, KT, D, base=farena) for i in range(2)]
            ysl = [at(16384 + 2048 * b, 2 * KT, P, base=farena) for b in range(2)]
            ysq = at(20480, 2 * KT, P, base=farena)
            xr = [at(22528 + 1024 * b, D, base=farena) for b in range(2)]
            vb = [at(24576 + 1024 * b, D, base=farena) for b in range(2)]
            ob = at(26624, D, base=farena)
        wgs, wus = [sb(n, [P, 2, KT, FF], F32R) for n in ("wgs", "wus")]
        wds = sb("wds", [P, 2, FF // P, D], F32R)
        xs = sb("xs", [P, 2, KT, P], F32R)
        hs = sb("hs", [P, 2, FF // P, P], F32R)

        def sem(name):
            return ctx.enter_context(nc.semaphore("late_" + name))

        pool_gate = sem("pool_gate")
        gc = sem("gpsimd_step")
        s0_loaded = [sem(f"s0_loaded{b}") for b in range(2)]
        sn_stored = [sem(f"sn_stored{b}") for b in range(2)]
        bcs_loaded = sem("bcs_loaded")
        xzs_loaded = sem("xzs_loaded")
        icur_ready = sem("icur_ready")
        eT_mm = sem("eT_mm")
        xh_ready = sem("xh_ready")
        xl_ready = sem("xl_ready")
        gh_ready = sem("gh_ready")
        gl_ready = sem("gl_ready")
        uh_ready = sem("uh_ready")
        ul_ready = sem("ul_ready")
        dh_ready = sem("dh_ready")
        dl_ready = sem("dl_ready")
        hh_ready = sem("hh_ready")
        hth_ready = sem("hth_ready")
        h_ready = sem("h_ready")
        h1_ready = sem("h1_ready")
        hT_mm = sem("hT_mm")
        hT_ready = sem("hT_ready")
        yo_ready = sem("yo_ready")
        sl_ready = sem("sl_ready")
        rows2n_loaded = sem("rows2n_loaded")
        fo_ready = sem("fo_ready")
        gcur_ready = sem("gcur_ready")
        g1_ready = sem("g1_ready")
        y1_scaled = sem("y1_scaled")
        fg_ready = sem("fg_ready")
        wg_loaded = sem("wg_loaded")
        wu_loaded = sem("wu_loaded")
        wd_loaded = sem("wd_loaded")
        gate_mm = sem("gate_mm")
        up_mm = sem("up_mm")
        down_mm = sem("down_mm")
        xg_loaded = sem("xg_loaded")
        yo_stored = sem("yo_stored")
        y12_used = [sem(f"y12_used{b}") for b in range(2)]
        y12_loaded = [sem(f"y12_loaded{b}") for b in range(3)]
        xl2_loaded = [sem(f"xl2_loaded{b}") for b in range(3)]
        fo_stored = [sem(f"fo_stored{b}") for b in range(3)]
        fl = sem("row_tile_step")
        wo_loaded = [sem(f"wo_loaded{i}") for i in range(4)]
        xr_used = sem("xr_used")
        wog_ready = [sem(f"wog_ready{s}") for s in range(2)]
        rows1_loaded = sem("rows1_loaded")
        ysq_ready = sem("ysq_ready")
        ysum_ready = sem("ysum_ready")
        pa_mm = sem("pa_mm")
        pb_mm = sem("pb_mm")
        ssq_mm = sem("ssq_mm")
        rsv_ready = sem("rsv_ready")
        rstd_ready = sem("rstd_ready")
        pa_read = sem("pa_read")
        pb_read = sem("pb_read")
        lnv_ready = sem("lnv_ready")
        lns_ready = sem("lns_ready")
        xp1_ready = sem("xp1_ready")
        v_ready = sem("v_ready")
        wr_loaded = sem("wr_loaded")
        vt_mm = sem("vt_mm")
        vT_ready = sem("vT_ready")
        lg_mm = sem("lg_mm")
        y_loaded = [sem(f"y_loaded{b}") for b in range(3)]
        xr_loaded = [sem(f"xr_loaded{b}") for b in range(3)]
        xp1_stored = [sem(f"xp1_stored{b}") for b in range(3)]
        v_stored = [sem(f"v_stored{b}") for b in range(3)]
        vector_gate = sem("vector_gate")
        vc = sem("vector_step")
        tensor_once = sem("tensor_once")
        (RANK_MM, TOKT_MM) = \
            (1, 2)
        vector_once = sem("vector_once")
        (RSEL_READY, A_READY, RANK_READY, _, APART_READY, CTL_READY, IDX_READY) = \
            (2, 4, 5, 7, 8, 9, 10)
        scalar_once = sem("scalar_once")
        (REXP_READY,) = \
            (2,)
        gpsimd_once = sem("gpsimd_once")
        ROWIDX_MADE, YS_READY, AM_READY, XG_ZEROED = 1, 2, 4, 5

        with nc.Block() as block:
            @block.sync
            def _(sp):

                wo_t = w_out[0].rearrange("(s k p) n -> s p k n", s=2, p=P)

                def load_y(t, b):
                    sp.dma_start(ysl[b], y_d[:, :, bass.ds(t * P, P)].rearrange("k p t -> p k t")).then_inc(y_loaded[b], 16)

                load_y(0, 0)
                for s in range(2):
                    for h in range(2):
                        sp.dma_start(WO[s][:, 4 * h:4 * h + 4, :], wo_t[s][:, 4 * h:4 * h + 4, :])\
                            .then_inc(wo_loaded[2 * s + h], 16)
                load_y(1, 1)
                for dst, src in ((gate1, mod_d[0:1, 2 * D:3 * D]), (ln1g, ln1_g), (ln1b, ln1_b),
                                 (sc2, mod_d[0:1, 4 * D:5 * D]), (sh2, mod_d[0:1, 3 * D:4 * D])):
                    sp.dma_start(dst, src.to_broadcast([P, D])).then_inc(rows1_loaded, 16)
                for b in range(2):
                    sp.dma_start(xr[b], x_prompt[0, b * P:(b + 1) * P, :]).then_inc(xr_loaded[b], 16)
                for dst, src in ((wr[:, :, 0:NG], w_rg[0]), (wr[:, :, NG:NG + NE], w_re[0])):
                    sp.dma_start(dst, src.rearrange("(k p) n -> p k n", p=P)).then_inc(wr_loaded, 16)
                sp.dma_start(brb[:, 0:NG], b_rg.to_broadcast([P, NG])).then_inc(wr_loaded, 16)
                sp.dma_start(brb[:, NG:NG + NE], b_re.to_broadcast([P, NE])).then_inc(wr_loaded, 16)
                def load(dst, src, e, rows, done):
                    sp.dma_start(dst, src[0, bass.ds(e, 1), :, :].rearrange("a (p c) f -> (a p) c f", c=rows))\
                        .then_inc(done, 16)

                def store(t, b, rows):
                    sp.wait_ge(xp1_ready, t + 1)
                    sp.dma_start(xp1_d[bass.ds(t * P, rows), :], xp1[b % 2][0:rows, :]).then_inc(xp1_stored[b], 16)
                    sp.wait_ge(v_ready, t + 1)
                    sp.dma_start(v_d[bass.ds(t * P, rows), :], vb[b % 2][0:rows, :]).then_inc(v_stored[b], 16)

                with sp.Fori(0, 3) as i:
                    for b in range(2):
                        sp.wait_ge(ssq_mm, i * 2 + (b + 1))
                        sp.wait_ge(pb_mm, i * 2 + (b + 1))
                        load_y(i * 2 + (2 + b), b)
                        sp.wait_ge(xr_used, i * 2 + (b + 1))
                        sp.dma_start(xr[b], x_prompt[0, bass.ds((i * 2 + (2 + b)) * P, P), :]).then_inc(xr_loaded[b], 16)
                        store(i * 2 + b, b, P)
                sp.wait_ge(xr_used, 7)
                sp.dma_start(xr[0][0:DEC, :], x_sample[:, 0, :]).then_inc(xr_loaded[2], 16)
                store(NT - 2, 0, P)
                sp.wait_ge(gpsimd_once, YS_READY)
                for b in range(2):
                    sp.wait_ge(sn_stored[b], 16 * 4)
                load(wg, w_gate, 0, KT, wg_loaded)
                load(wu, w_up, 0, KT, wu_loaded)
                load(wd, w_down, 0, FF // P, wd_loaded)
                store(NT - 1, 1, P)
                for dst, m in ((gate1, 2), (sc2, 4), (sh2, 3)):
                    sp.dma_start(dst[0:DEC, :], mod_d[1:9, m * D:(m + 1) * D]).then_inc(rows1_loaded, 16)
                store(NT, 2, DEC)

                sp.wait_ge(vector_once, CTL_READY)
                n_extra = sp.value_load(ctl[0:1, 2 * NBLK:2 * NBLK + 1], min_val=0, max_val=NOV)

                def next_weights(e, part):
                    expert = sp.value_load(ctl[0:1, bass.ds(e + 1, 1)], min_val=0, max_val=NE - 1)
                    new = sp.value_load(ctl[0:1, bass.ds(e + (NBLK + 1), 1)], min_val=0, max_val=1)
                    for dst, src, rows, done, split in part:
                        with sp.If(new > 0):
                            sp.wait_ge(split, e + 1)
                            load(dst, src, expert, rows, done)
                        with sp.If(new < 1):
                            sp.wait_ge(split, e + 1)
                            sp.sem_inc(done, 16)

                GATE_UP = ((wg, w_gate, KT, wg_loaded, gl_ready), (wu, w_up, KT, wu_loaded, ul_ready))
                DOWN = ((wd, w_down, FF // P, wd_loaded, dl_ready),)
                next_weights(0, GATE_UP)
                with sp.Fori(0, n_extra + (NE - 2)) as e:
                    next_weights(e + 1, GATE_UP)
                    next_weights(e, DOWN)
                next_weights(n_extra + (NE - 2), DOWN)
                for dst, src in ((gate2, mod_d[0:1, 5 * D:6 * D]), (ln2g, ln2_g), (ln2b, ln2_b)):
                    sp.dma_start(dst, src.to_broadcast([P, D])).then_inc(rows2n_loaded, 16)
                for b in range(2):
                    sp.wait_ge(xp1_stored[b], 64)
                for b in range(2):
                    sp.dma_start(xl2[b], xp1_d[b * P:(b + 1) * P, :]).then_inc(xl2_loaded[b], 16)
                def store_y(t, b):
                    sp.wait_ge(fo_ready, t + 1)
                    sp.dma_start(y_prompt[0, bass.ds(t * P, P), :], fo[b]).then_inc(fo_stored[b], 16)

                with sp.Fori(0, NT // 2 - 1) as i:
                    for b in range(2):
                        store_y(i * 2 + b, b)
                        sp.dma_start(xl2[b], xp1_d[bass.ds((i * 2 + (2 + b)) * P, P), :]).then_inc(xl2_loaded[b], 16)
                for b in range(2):
                    store_y(NT - 2 + b, b)
                sp.wait_ge(xp1_stored[2], 16)
                sp.dma_start(xl2[0][0:DEC, :], xp1_d[SEQ:SEQ + DEC, :]).then_inc(xl2_loaded[2], 16)
                sp.dma_start(gate2[0:DEC, :], mod_d[1:9, 5 * D:6 * D]).then_inc(rows2n_loaded, 16)
                sp.wait_ge(fo_ready, NTT)
                sp.dma_start(y_sample[:, 0, :], fo[0][0:DEC, :]).then_inc(fo_stored[2], 16)
                for b in range(2):
                    sp.wait_ge(fo_stored[b], 16 * (NT // 2))
                sp.wait_ge(fo_stored[2], 16)

            @block.gpsimd
            def _(gp):
                step = Chain(gp, gc)
                step(gp.iota(rowint, pattern=[[1, P]], base=-CAP, channel_multiplier=0))
                gp.tensor_copy(rowidx, rowint).then_inc(gpsimd_once, 1)
                s_in = state_ssd[0].rearrange("b (k h) p n -> k (h p) b n", h=2)
                s_out = sample_ssd[0].rearrange("b (k h) p n -> k (h p) b n", h=2)
                gp.wait_ge(wo_loaded[3], 16)
                gp.dma_start(s0t[0], s_in[0]).then_inc(s0_loaded[0], 16)
                for i, src in enumerate((x_d, z_d)):
                    gp.dma_start(xzs[:, i, :, :], src[:, :, SEQ:TE].rearrange("k p t -> p k t")).then_inc(xzs_loaded, 16)
                gp.dma_start(bcsb.rearrange("p a n -> p (a n)"),
                             bcs_d.rearrange("i n -> (i n)").unsqueeze(0).to_broadcast([P, 4 * DEC * P]))\
                    .then_inc(bcs_loaded, 16)
                gp.dma_start(s0t[1], s_in[1]).then_inc(s0_loaded[1], 16)
                gp.wait_ge(xzs_loaded, 32)
                step(gp.tensor_tensor(xdS, xzs[:, 0, :, CONV - 1:4 * DEC:CONV], exd[:, :, 0:DEC], ALU.mult))
                gp.wait_ge(bcs_loaded, 16)
                for k in range(KT):
                    g, b = k // 4, k % 2
                    step(gp.tensor_tensor(t2t, bcsb[:, g, :].rearrange("p (b n) -> p b n", b=DEC),
                                          xdS[:, k, :].unsqueeze(2).to_broadcast([P, DEC, P]), ALU.mult))
                    gp.wait_ge(s0_loaded[b], 16 * (k // 2 + 1))
                    step(gp.tensor_tensor(t1t, s0t[b], exd[:, k, DEC:2 * DEC].unsqueeze(2).to_broadcast([P, DEC, P]),
                                          ALU.mult))
                    if k + 2 < KT:
                        gp.dma_start(s0t[b], s_in[k + 2]).then_inc(s0_loaded[b], 16)
                    if k >= 2:
                        gp.wait_ge(sn_stored[b], 16 * (k // 2))
                    step(gp.tensor_tensor(snt[b], t1t, t2t, ALU.add))
                    gp.dma_start(s_out[k], snt[b]).then_inc(sn_stored[b], 16)
                    step(gp.tensor_tensor(t2t, snt[b], bcsb[:, 2 + g, :].rearrange("p (b n) -> p b n", b=DEC), ALU.mult))
                    n = P // 2
                    while n > 1:
                        step(gp.tensor_tensor(t2t[:, :, 0:n], t2t[:, :, 0:n], t2t[:, :, n:2 * n], ALU.add))
                        n //= 2
                    step(gp.tensor_tensor(yr[:, k, :].unsqueeze(2), t2t[:, :, 0:1], t2t[:, :, 1:2], ALU.add))
                step(gp.tensor_tensor(xdS, xzs[:, 0, :, CONV - 1:4 * DEC:CONV],
                                      Dch[:, :].unsqueeze(2).to_broadcast([P, KT, DEC]), ALU.mult))
                step(gp.tensor_tensor(yr, yr, xdS, ALU.add))
                step(gp.tensor_scalar(yr, yr, 0.5, None, ALU.mult))
                gp.tensor_tensor(yS[:, KT:2 * KT, :], yr, xzs[:, 1, :, CONV - 1:4 * DEC:CONV], ALU.mult)\
                    .then_inc(gpsimd_once, 1)
                gp.wait_ge(vector_once, A_READY)
                for a in range(2):
                    gp.affine_select(out=gtmp[a], in_=gtmp[a], compare_op=ALU.is_ge, fill=0.0, base=SEQ + DEC - 1,
                                     pattern=[[-P, NTT], [0, NE]], channel_multiplier=-1).then_inc(gpsimd_once, 1)
                gp.memset(xg, 0.0).then_inc(gpsimd_once, 1)
                gp.wait_ge(gpsimd_once, XG_ZEROED)
                gp.wait_ge(vector_once, IDX_READY)
                for b in range(2):
                    gp.wait_ge(v_stored[b], 64)
                gp.wait_ge(v_stored[2], 16)

                n_extra = gp.value_load(ctl[0:1, 2 * NBLK:2 * NBLK + 1], min_val=0, max_val=NOV)

                def gather(e):
                    gp.tensor_copy(icur[:, :], idxT[:, bass.ds(e, 1)]).then_inc(icur_ready, 1)
                    gp.wait_ge(icur_ready, e + 1)
                    gp.sem_inc(pool_gate, 1)
                    gp.indirect_dma_start(xg, None, v_d, bass.IndirectOffsetOnAxis(ap=icur[:, :], axis=0),
                                          bounds_check=SEQ + DEC - 1, oob_is_err=False)\
                        .then_inc(xg_loaded, 16)

                gather(0)
                with gp.Fori(0, n_extra + (NE - 1)) as e:
                    gp.wait_ge(xg_loaded, e * 16 + 16)
                    gp.wait_ge(eT_mm, e + 1)
                    gp.sem_inc(pool_gate, 1)
                    gather(e + 1)

                gp.wait_ge(yo_stored, n_extra * 16 + 16 * NE)
                gp.sem_inc(pool_gate, 1)

                def take(t, b, r, rows, done):
                    gp.wait_ge(y12_used[b], r)
                    gp.sem_inc(pool_gate, 1)
                    gp.tensor_copy(sl1[b][0:rows, :].unsqueeze(2), slot[0:rows, :, bass.ds(t, 1)]).then_inc(sl_ready, 1)
                    gp.wait_ge(sl_ready, t + 1)
                    gp.sem_inc(pool_gate, 1)
                    for a, dst in enumerate((y1s[b], y2s[b])):
                        gp.indirect_dma_start(dst[0:rows, :], None, ys_d,
                                              bass.IndirectOffsetOnAxis(ap=sl1[b][0:rows, a:a + 1], axis=0))\
                            .then_inc(done, 16)

                def shift(t, b, rows):
                    gp.wait_ge(fg_ready, t + 1)
                    gp.tensor_tensor(fo[b][0:rows, :], fo[b][0:rows, :], ln2b[0:rows, :], ALU.add).then_inc(fo_ready, 1)

                for b in range(2):
                    take(b, b, 0, P, y12_loaded[b])
                with gp.Fori(0, NT // 2 - 1) as i:
                    for b in range(2):
                        take(i * 2 + (2 + b), b, i + 1, P, y12_loaded[b])
                        shift(i * 2 + b, b, P)
                take(NT, 0, NT // 2, DEC, y12_loaded[2])
                shift(NT - 2, 0, P)
                shift(NT - 1, 1, P)
                shift(NT, 0, DEC)

            @block.scalar
            def _(act):

                for k in range(KT):
                    act.wait_ge(wo_loaded[k // 4], 16)
                    act.activation(WO[0][:, k, :], WO[0][:, k, :], ACT.Copy, scale=PT1[:, k, 8:9]).then_inc(wog_ready[0], 1)

                def squares(t, src):
                    act.wait_ge(ysum_ready, t)
                    act.activation(ysq[:, :, 0:src.shape[2]], src, ACT.Square).then_inc(ysq_ready, 1)
                    act.wait_ge(rsv_ready, t + 1)
                    rows = src.shape[2]
                    act.activation(rs2[0:rows, :], rs2[0:rows, :], ACT.Sqrt).then_inc(rstd_ready, 1)

                def v_out(t, b, rows):
                    act.wait_ge(vt_mm, t + 1)
                    act.activation(vT[b][:, :, 0:rows], PS[:, 6:8, :].rearrange("p a (k t) -> p (a k) t", t=P)[:, :, 0:rows],
                                   ACT.Copy).then_inc(vT_ready, 1)

                def norm_roots(t, rows):
                    for a in range(2):
                        act.wait_ge(lnv_ready, t * 2 + (a + 1))
                        act.activation(rstd[0:rows, :], mv[0:rows, 1:2], ACT.Sqrt).then_inc(lns_ready, 1)

                act.wait_ge(y_loaded[0], 16)
                squares(0, ysl[0])
                norm_roots(0, P)
                with act.Fori(0, 3) as i:
                    for b in range(2):
                        act.wait_ge(y_loaded[1 - b], i * 16 + (16 + 16 * b))
                        squares(i * 2 + (1 + b), ysl[1 - b])
                        v_out(i * 2 + b, b, P)
                        norm_roots(i * 2 + (1 + b), P)
                act.wait_ge(y_loaded[1], 64)
                squares(NT - 1, ysl[1])
                v_out(NT - 2, 0, P)
                norm_roots(NT - 1, P)
                act.wait_ge(gpsimd_once, YS_READY)
                squares(NT, yS[:, :, :])
                v_out(NT - 1, 1, P)
                norm_roots(NT, DEC)
                v_out(NT, 0, DEC)
                act.wait_ge(vector_once, RSEL_READY)
                act.activation(gon[:, 3, :, 0:NG], gon[:, 3, :, 0:NG], ACT.Exp).then_inc(scalar_once, 1)
                act.activation(gsm[:, 4, :], gsm[:, 4, :], ACT.Exp).then_inc(scalar_once, 1)

                def is_new(e):
                    return act.value_load(ctl[0:1, bass.ds(e + NBLK, 1)], min_val=0, max_val=1)

                def high(new, e, src, loaded, used, part, done):
                    def make():
                        act.wait_ge(loaded, e * 16 + 16)
                        act.wait_ge(used, e)
                        act.activation(part, src, ACT.Copy).then_inc(done, 1)

                    if new is None:
                        make()
                        return
                    with act.If(new > 0):
                        make()
                    with act.If(new < 1):
                        act.wait_ge(loaded, e * 16 + 16)
                        act.sem_inc(done, 1)

                def gate_high(e, new=None):
                    high(new, e, wg, wg_loaded, gate_mm, wgs[:, 0, :, :], gh_ready)

                def up_high(e, new=None):
                    high(new, e, wu, wu_loaded, up_mm, wus[:, 0, :, :], uh_ready)

                def down_high(e, new=None):
                    high(new, e, wd, wd_loaded, down_mm, wds[:, 0, :, :], dh_ready)

                def x_high(e):
                    act.wait_ge(eT_mm, e + 1)
                    act.activation(xs[:, 0, :, :], PS[:, 0:2, :].rearrange("p a (k t) -> p (a k) t", t=P), ACT.Copy)\
                        .then_inc(xh_ready, 1)

                def half_tanh(e):
                    act.wait_ge(gate_mm, e + 1)
                    act.wait_ge(h_ready, e)
                    act.activation(hth, PS[:, 2, :], ACT.Tanh, scale=0.5).then_inc(hth_ready, 1)

                def y_out(e):
                    act.wait_ge(down_mm, e + 1)
                    act.wait_ge(yo_stored, e * 16)
                    act.activation(yo, PS[:, 5:7, :].rearrange("p a n -> p (a n)"), ACT.Copy).then_inc(yo_ready, 1)
                    act.wait_ge(yo_ready, e + 1)
                    act.dma_start(ys_d[bass.ds(e * CAP, CAP), :], yo).then_inc(yo_stored, 16)

                act.wait_ge(pb_mm, NTT)
                act.wait_ge(xr_used, NTT)
                for s in range(2):
                    act.wait_ge(v_stored[s], 64)
                act.wait_ge(v_stored[2], 16)
                gate_high(0)
                up_high(0)
                act.wait_ge(vector_once, CTL_READY)
                n_extra = act.value_load(ctl[0:1, 2 * NBLK:2 * NBLK + 1], min_val=0, max_val=NOV)
                x_high(0)
                half_tanh(0)
                new = is_new(1)
                gate_high(1, new)
                x_high(1)
                up_high(1, new)
                down_high(0)
                with act.Fori(0, n_extra + (NE - 2)) as i:
                    new_down, new = is_new(i + 1), is_new(i + 2)
                    half_tanh(i + 1)
                    gate_high(i + 2, new)
                    x_high(i + 2)
                    up_high(i + 2, new)
                    down_high(i + 1, new_down)
                    y_out(i)
                half_tanh(n_extra + (NE - 1))
                down_high(n_extra + (NE - 1), is_new(n_extra + (NE - 1)))
                y_out(n_extra + (NE - 2))
                y_out(n_extra + (NE - 1))

                def scale_y1(t, b, r, rows, loaded):
                    q = slice(0, rows)
                    act.wait_ge(y1_scaled, t)
                    act.activation(gcur[q, 0:1].unsqueeze(2), gat[q, 0:1, bass.ds(t, 1)], ACT.Copy).then_inc(g1_ready, 1)
                    act.wait_ge(g1_ready, t + 1)
                    act.wait_ge(loaded, r * 32 + 32)
                    act.activation(y1s[b][q, :], y1s[b][q, :], ACT.Copy, scale=gcur[q, 0:1]).then_inc(y1_scaled, 1)

                def root(t, rows):
                    act.wait_ge(lnv_ready, t + (2 * NTT + 1))
                    act.activation(rstd[0:rows, :], mv[0:rows, 1:2], ACT.Sqrt).then_inc(lns_ready, 1)

                scale_y1(0, 0, 0, P, y12_loaded[0])
                with act.Fori(0, NT // 2 - 1) as i:
                    scale_y1(i * 2 + 1, 1, i, P, y12_loaded[1])
                    root(i * 2, P)
                    scale_y1(i * 2 + 2, 0, i + 1, P, y12_loaded[0])
                    root(i * 2 + 1, P)
                scale_y1(NT - 1, 1, NT // 2 - 1, P, y12_loaded[1])
                root(NT - 2, P)
                root(NT - 1, P)
                scale_y1(NT, 0, 0, DEC, y12_loaded[2])
                root(NT, DEC)

            @block.tensor
            def _(pe):

                def out_tile(t, y, rows, logits_of=None, turn_of=None):
                    for s in range(2):
                        if s == 0:
                            pe.wait_ge(pa_read, t)
                        else:
                            pe.wait_ge(pb_read, t)
                        for k in range(KT):
                            if s == 1 and k == KT - 2:
                                pe.wait_ge(ysum_ready, t + 1)
                                pe.wait_ge(rsv_ready, t)
                                for a in range(2):
                                    mm = pe.matmul(PS[0:rows, 4, a:a + 1], ysum[:, a, 0:rows], ones[:, 0:1],
                                                   start=True, stop=True)
                                mm.then_inc(ssq_mm, 1)
                            pe.wait_ge(wog_ready[s], k + 1)
                            for n in range(2):
                                mm = pe.matmul(PS[0:rows, 2 * s + n, :], y[:, s * KT + k, :],
                                               WO[s][:, k, 512 * n:512 * n + 512], start=(k == 0), stop=(k == KT - 1))
                        if s == 0:
                            mm.then_inc(pa_mm, 1)
                            if logits_of is not None:
                                logits(*logits_of)
                        else:
                            mm.then_inc(pb_mm, 1)
                    if turn_of is not None:
                        v_turn(*turn_of)

                def v_turn(t, b, rows):
                    pe.wait_ge(v_ready, t + 1)
                    pe.wait_ge(vT_ready, t)
                    for k in range(KT):
                        mm = pe.transpose(PS[:, 6 + k // 4, P * (k % 4):P * (k % 4) + rows],
                                          vb[b][0:rows, k * P:(k + 1) * P], ident[0:rows, 0:rows])
                    mm.then_inc(vt_mm, 1)

                def logits(t, b, rows):
                    pe.wait_ge(vT_ready, t + 1)
                    for k in range(KT):
                        mm = pe.matmul(PS[0:rows, 5, bass.ds(t * 36, 36)], vT[b][:, k, 0:rows], wr[:, k, :],
                                       start=(k == 0), stop=(k == KT - 1))
                    mm.then_inc(lg_mm, 1)

                pe.wait_ge(y_loaded[0], 16)
                out_tile(0, ysl[0], P)
                pe.wait_ge(y_loaded[1], 16)
                out_tile(1, ysl[1], P, turn_of=(0, 0, P))
                pe.wait_ge(wr_loaded, 64)
                with pe.Fori(0, 3) as i:
                    for b in range(2):
                        pe.wait_ge(y_loaded[b], i * 16 + 32)
                        out_tile(i * 2 + (2 + b), ysl[b], P, logits_of=(i * 2 + b, b, P),
                                 turn_of=(i * 2 + (1 + b), 1 - b, P))
                pe.wait_ge(gpsimd_once, YS_READY)
                out_tile(NT, yS, DEC, logits_of=(NT - 2, 0, P), turn_of=(NT - 1, 1, P))
                logits(NT - 1, 1, P)
                v_turn(NT, 0, DEC)
                logits(NT, 0, DEC)
                pe.wait_ge(gpsimd_once, AM_READY)
                pe.wait_ge(vector_once, RANK_READY)
                A = gtmp[2].rearrange("p t e -> p (t e)")
                pe.matmul(PS[:, 0, 0:NE * NTT], triS[:, :], A, start=True, stop=True)
                pe.matmul(PS[:, 1, 0:NE * NTT], ones[:, :], A, start=True, stop=True).then_inc(tensor_once, 1)
                pe.wait_ge(vector_once, APART_READY)
                for n in range(2 * NTT):
                    mm = pe.matmul(PS[:, 2, 0:NBLK], inrow[:, n, :], inblk[:, n, :], start=(n == 0), stop=(n == 2 * NTT - 1))
                mm.then_inc(tensor_once, 1)

                def x_turn(e):
                    pe.wait_ge(xg_loaded, e * 16 + 16)
                    pe.wait_ge(xh_ready, e)
                    pe.wait_ge(xl_ready, e)
                    for c in range(KT):
                        mm = pe.transpose(PS[:, c // 4, P * (c % 4):P * (c % 4) + P], xg[:, c::KT], ident[:, :])
                    mm.then_inc(eT_mm, 1)

                PARTS = ((0, 0), (0, 1), (1, 0))

                def gate_or_up(bank, w, done):
                    for c in range(KT):
                        for i, j in PARTS:
                            mm = pe.matmul(PS[:, bank, :], xs[:, i, c, :], w[:, j, c, :],
                                           start=(c == 0 and (i, j) == PARTS[0]),
                                           stop=(c == KT - 1 and (i, j) == PARTS[-1]))
                    mm.then_inc(done, 1)

                def gate(e):
                    pe.wait_ge(xh_ready, e + 1)
                    pe.wait_ge(xl_ready, e + 1)
                    pe.wait_ge(gh_ready, e + 1)
                    pe.wait_ge(gl_ready, e + 1)
                    pe.wait_ge(h_ready, e)
                    gate_or_up(2, wgs, gate_mm)

                def up(e):
                    pe.wait_ge(uh_ready, e + 1)
                    pe.wait_ge(ul_ready, e + 1)
                    gate_or_up(3, wus, up_mm)

                def h_turn(e):
                    pe.wait_ge(h_ready, e + 1)
                    pe.wait_ge(hT_ready, e)
                    for c in range(FF // P):
                        mm = pe.transpose(PS[:, 4, P * c:P * c + P], hb[:, c::FF // P], ident[:, :])
                    mm.then_inc(hT_mm, 1)

                def down(e):
                    pe.wait_ge(dh_ready, e + 1)
                    pe.wait_ge(dl_ready, e + 1)
                    pe.wait_ge(hT_ready, e + 1)
                    pe.wait_ge(yo_ready, e)
                    for c in range(FF // P):
                        for i, j in PARTS:
                            for n in range(2):
                                mm = pe.matmul(PS[:, 5 + n, :], hs[:, i, c, :], wds[:, j, c, 512 * n:512 * n + 512],
                                               start=(c == 0 and (i, j) == PARTS[0]),
                                               stop=(c == FF // P - 1 and (i, j) == PARTS[-1]))
                    mm.then_inc(down_mm, 1)

                pe.wait_ge(vector_once, CTL_READY)
                n_extra = pe.value_load(ctl[0:1, 2 * NBLK:2 * NBLK + 1], min_val=0, max_val=NOV)
                x_turn(0)
                gate(0)
                up(0)
                x_turn(1)
                with pe.Fori(0, n_extra + (NE - 2)) as i:
                    gate(i + 1)
                    h_turn(i)
                    up(i + 1)
                    x_turn(i + 2)
                    down(i)
                gate(n_extra + (NE - 1))
                h_turn(n_extra + (NE - 2))
                up(n_extra + (NE - 1))
                down(n_extra + (NE - 2))
                h_turn(n_extra + (NE - 1))
                down(n_extra + (NE - 1))

            @block.vector
            def _(ve):
                step = Chain(ve, vc)

                for k in range(KT):
                    ve.wait_ge(wo_loaded[2 + k // 4], 16)
                    ve.tensor_scalar(WO[1][:, k, :], WO[1][:, k, :], PT1[:, k, 9:10], None, ALU.mult)\
                        .then_inc(wog_ready[1], 1)
                ve.wait_ge(rows1_loaded, 80)

                def norm(src, dst, rows, n, chain):
                    for h in range(2):
                        chain(ve.bn_stats(stat[0:rows, 6 * h:6 * h + 6], src[0:rows, 512 * h:512 * h + 512]))
                    ve.sem_inc(vector_gate, 1)
                    chain(ve.bn_aggr(mv[0:rows, :], stat[0:rows, :].rearrange("p (a s) -> p a s", a=2)))
                    ve.tensor_scalar(mv[0:rows, 1:2], mv[0:rows, 1:2], LN_EPS, None, ALU.add).then_inc(lnv_ready, 1)
                    ve.wait_ge(lns_ready, n + 1)
                    chain(ve.reciprocal(rstd[0:rows, :], rstd[0:rows, :]))
                    chain(ve.tensor_scalar(dst[0:rows, :], src[0:rows, :], mv[0:rows, 0:1], rstd[0:rows, :],
                                           ALU.subtract, ALU.mult))

                def row_tile(t, b, rows):
                    chain = Chain(ve, fl, t * 14)
                    r = slice(0, rows)
                    ve.wait_ge(ysq_ready, t + 1)
                    ve.tensor_reduce(ysum[:, :, 0:rows], ysq[:, :, 0:rows].rearrange("p (s k) t -> p s t k", s=2),
                                     AX.X, ALU.add).then_inc(ysum_ready, 1)
                    ve.wait_ge(ssq_mm, t + 1)
                    ve.tensor_scalar(rs2[r, :], PS[r, 4, 0:2], 1.0 / D, RMS_EPS, ALU.mult, ALU.add).then_inc(rsv_ready, 1)
                    ve.wait_ge(rstd_ready, t + 1)
                    chain(ve.reciprocal(rs2[r, :], rs2[r, :]))
                    ve.wait_ge(pa_mm, t + 1)
                    o2 = ob[r, :].rearrange("p (a n) -> p a n", a=2)
                    ve.tensor_scalar(o2, PS[r, 0:2, :], rs2[r, 0:1], None, ALU.mult).then_inc(pa_read, 1)
                    ve.wait_ge(pa_read, t + 1)
                    ve.wait_ge(pb_mm, t + 1)
                    ve.scalar_tensor_tensor(out=o2, in0=PS[r, 2:4, :], scalar=rs2[r, 1:2], in1=o2,
                                            op0=ALU.mult, op1=ALU.add).then_inc(pb_read, 1)
                    ve.wait_ge(pb_read, t + 1)
                    chain(ve.tensor_tensor(ob[r, :], ob[r, :], gate1[r, :], ALU.mult))
                    ve.wait_ge(xr_loaded[b], (t - b if b < 2 else t - NT) * 8 + 16)
                    ve.scalar_tensor_tensor(out=ob[r, :], in0=xr[b % 2][r, :], scalar=ALPHA, in1=ob[r, :],
                                            op0=ALU.mult, op1=ALU.add).then_inc(xr_used, 1)
                    ve.wait_ge(xr_used, t + 1)
                    if b < 2:
                        ve.wait_ge(xp1_stored[b], (t - b) * 8)
                        ve.wait_ge(v_stored[b], (t - b) * 8)
                    else:
                        ve.wait_ge(xp1_stored[0], 64)
                        ve.wait_ge(v_stored[0], 64)
                    x1, v1 = xp1[b % 2], vb[b % 2]
                    norm(ob, x1, rows, t * 2, chain)
                    chain(ve.tensor_tensor(x1[r, :], x1[r, :], ln1g[r, :], ALU.mult))
                    ve.tensor_tensor(x1[r, :], x1[r, :], ln1b[r, :], ALU.add).then_inc(xp1_ready, 1)
                    ve.wait_ge(xp1_ready, t + 1)
                    norm(x1, v1, rows, t * 2 + 1, chain)
                    chain(ve.tensor_tensor(v1[r, :], v1[r, :], sc2[r, :], ALU.mult))
                    ve.tensor_tensor(v1[r, :], v1[r, :], sh2[r, :], ALU.add).then_inc(v_ready, 1)
                    assert chain.n == 14, chain.n

                with ve.Fori(0, 4) as i:
                    for b in range(2):
                        row_tile(i * 2 + b, b, P)
                ve.wait_ge(rows1_loaded, 128)
                row_tile(NT, 2, DEC)

                step(ve.memset(Lg[:, :, :], 0.0))
                ve.wait_ge(lg_mm, NTT)
                step(ve.tensor_tensor(Lg[:, 0:NT, :], PS[:, 5, 0:36 * NT].rearrange("p (t c) -> p t c", c=36),
                                      brb[:, :].unsqueeze(1).to_broadcast([P, NT, 36]), ALU.add))
                step(ve.tensor_tensor(Lg[0:DEC, NT, :], PS[0:DEC, 5, 36 * NT:36 * NTT], brb[0:DEC, :], ALU.add))

                def first_of_max(x, n, top, tmp, red, out):
                    wide = lambda a: a.unsqueeze(2).to_broadcast([P, NTT, n])
                    step(ve.tensor_reduce(top, x, AX.X, ALU.max))
                    step(ve.tensor_tensor(tmp, x, wide(top), ALU.is_equal))
                    step(ve.tensor_tensor(tmp, tmp, desc[:, EG - n:EG].unsqueeze(1).to_broadcast([P, NTT, n]), ALU.mult))
                    step(ve.tensor_reduce(red, tmp, AX.X, ALU.max))
                    step(ve.tensor_tensor(out, tmp, wide(red), ALU.is_equal))

                gmax, red, m1, m2, ed, se, den, g1v = [gsm[:, i, :] for i in range(8)]
                ohg, o1, o2h, ext = gon[:, 0, :, 0:NG], gon[:, 1, :, :], gon[:, 2, :, :], gon[:, 3, :, 0:NG]
                tmp8, les = gtmp[3][:, :, 0:EG], gtmp[4][:, :, 0:EG]
                first_of_max(Lg[:, :, 0:NG], NG, gmax, tmp8[:, :, 0:NG], red, ohg)
                ve.tensor_tensor(ext, Lg[:, :, 0:NG], gmax.unsqueeze(2).to_broadcast([P, NTT, NG]), ALU.subtract)\
                    .then_inc(vector_once, 1)
                Le = Lg[:, :, NG:NG + NE].rearrange("p t (g e) -> p t g e", g=NG)
                prod = gtmp[5].rearrange("p t (g e) -> p t g e", g=NG)
                step(ve.tensor_tensor(prod, Le, ohg.unsqueeze(3).to_broadcast([P, NTT, NG, EG]), ALU.mult))
                step(ve.tensor_reduce(les, gtmp[5].rearrange("p t (g e) -> p t e g", g=NG), AX.X, ALU.add))
                first_of_max(les, EG, m1, tmp8, red, o1)
                step(ve.scalar_tensor_tensor(out=les, in0=o1, scalar=-3.0e38, in1=les, op0=ALU.mult, op1=ALU.add))
                first_of_max(les, EG, m2, tmp8, red, o2h)
                ve.tensor_tensor(ed, m2, m1, ALU.subtract).then_inc(vector_once, 1)
                for a, oh in enumerate((o1, o2h)):
                    ve.tensor_tensor(gtmp[a].rearrange("p t (g e) -> p t g e", g=NG),
                                     ohg.unsqueeze(3).to_broadcast([P, NTT, NG, EG]),
                                     oh.unsqueeze(2).to_broadcast([P, NTT, NG, EG]), ALU.mult).then_inc(vector_once, 1)
                ve.wait_ge(scalar_once, REXP_READY)
                step(ve.tensor_reduce(se, ext, AX.X, ALU.add))
                step(ve.scalar_tensor_tensor(out=den, in0=ed, scalar=1.0, in1=se, op0=ALU.add, op1=ALU.mult))
                step(ve.reciprocal(gat[:, 0, :], den))
                step(ve.tensor_tensor(gat[:, 1, :], gat[:, 0, :], ed, ALU.mult))
                step(ve.tensor_tensor(triS[:, :], tri[:, :], ident[:, :], ALU.subtract))
                ve.wait_ge(gpsimd_once, AM_READY)
                ve.tensor_tensor(gtmp[2], gtmp[0], gtmp[1], ALU.add).then_inc(vector_once, 1)
                ve.wait_ge(tensor_once, RANK_MM)
                tot = gtmp[3]
                rank, off, ovm = gtmp[4], gtmp[5], gtmp[6]
                step(ve.tensor_copy(tot, PS[:, 1, 0:NE * NTT].rearrange("p (t e) -> p t e", e=NE)))
                step(ve.memset(off[:, 0, :], 0.0))
                for t in range(NT):
                    step(ve.tensor_tensor(off[:, t + 1, :], off[:, t, :], tot[:, t, :], ALU.add))
                n_e, nov, bend, bstart, onesE, _ = [cnt[:, i, :] for i in range(6)]
                step(ve.tensor_tensor(n_e, off[:, NT, :], tot[:, NT, :], ALU.add))
                step(ve.tensor_tensor(rank, off, PS[:, 0, 0:NE * NTT].rearrange("p (t e) -> p t e", e=NE), ALU.add))
                MORE = (SEQ + DEC - 1) // CAP
                full = ge[:, 0:MORE, 0:NE]
                step(ve.scalar_tensor_tensor(out=full, in0=qidx[:, 1:MORE + 1].unsqueeze(2).to_broadcast([P, MORE, NE]),
                                             scalar=float(CAP), in1=n_e.unsqueeze(1).to_broadcast([P, MORE, NE]),
                                             op0=ALU.mult, op1=ALU.is_lt))
                step(ve.tensor_reduce(nov, full.rearrange("p m e -> p e m"), AX.X, ALU.add))
                step(ve.memset(onesE, 1.0))
                step(ve.tensor_tensor_scan(bend, onesE, nov, 0.0, ALU.mult, ALU.add))
                step(ve.tensor_tensor(bend, bend, eidx[:, :], ALU.add))
                step(ve.tensor_tensor(bstart, bend, nov, ALU.subtract))
                step(ve.tensor_scalar(bend, bend, 1.0, None, ALU.add))
                step(ve.scalar_tensor_tensor(out=rank, in0=bstart.unsqueeze(1).to_broadcast([P, NTT, NE]),
                                             scalar=float(CAP), in1=rank, op0=ALU.mult, op1=ALU.add))
                for a in range(2):
                    step(ve.tensor_tensor(ovm, gtmp[a], rank, ALU.mult))
                    step(ve.tensor_reduce(gsm[:, 8 + a, :], ovm, AX.X, ALU.add))
                    ve.tensor_copy(slot[:, a, :], gsm[:, 8 + a, :]).then_inc(vector_once, 1)
                places = gsm[:, 8:10, :].rearrange("p a t -> p (a t)")
                wideS = lambda n: places.unsqueeze(2).to_broadcast([P, 2 * NTT, n])
                step(ve.memset(ge[:, :, NBLK:NBLK + 1], 0.0))
                step(ve.scalar_tensor_tensor(out=ge[:, :, 0:NBLK], in0=qidx[:, :].unsqueeze(1).to_broadcast([P, 2 * NTT, NBLK]),
                                             scalar=float(CAP), in1=wideS(NBLK), op0=ALU.mult, op1=ALU.is_le))
                step(ve.tensor_tensor(inblk, ge[:, :, 0:NBLK], ge[:, :, 1:NBLK + 1], ALU.subtract))
                inb4 = inblk.rearrange("p (a t) q -> p a t q", a=2)
                step(ve.tensor_tensor(inb4, inb4, tokv[:, :].unsqueeze(1).unsqueeze(3).to_broadcast([P, 2, NTT, NBLK]),
                                      ALU.mult))
                nblk = gsm[:, 10:12, :].rearrange("p a t -> p (a t)")
                step(ve.tensor_reduce(nblk, ge[:, :, 0:NBLK], AX.X, ALU.add))
                step(ve.scalar_tensor_tensor(out=nblk, in0=nblk, scalar=-float(CAP), in1=places, op0=ALU.mult, op1=ALU.add))
                ve.wait_ge(gpsimd_once, ROWIDX_MADE)
                ve.tensor_tensor(inrow, rowidx.unsqueeze(1).to_broadcast([P, 2 * NTT, P]),
                                 nblk.unsqueeze(2).to_broadcast([P, 2 * NTT, P]), ALU.is_equal).then_inc(vector_once, 1)
                for b in range(2):
                    ve.wait_ge(xp1_stored[b], 64)
                ve.wait_ge(xp1_stored[2], 16)
                step(ve.tensor_tensor(ended, bend.unsqueeze(1).to_broadcast([P, NBLK, NE]),
                                      qidx[:, :].unsqueeze(2).to_broadcast([P, NBLK, NE]), ALU.is_le))
                step(ve.memset(bexp[:, 0:1], -1.0))
                step(ve.tensor_reduce(bexp[:, 1:NBLK + 1], ended, AX.X, ALU.add))
                step(ve.tensor_scalar(bexp[:, 1:NBLK + 1], bexp[:, 1:NBLK + 1], float(NE - 1), None, ALU.min))
                step(ve.tensor_copy(ctl[:, 0:NBLK], bexp[:, 1:NBLK + 1]))
                step(ve.tensor_tensor(ctl[:, NBLK:2 * NBLK], bexp[:, 1:NBLK + 1], bexp[:, 0:NBLK], ALU.is_gt))
                ve.tensor_scalar(ctl[:, 2 * NBLK:2 * NBLK + 1], bend[:, NE - 1:NE], -float(NE), None, ALU.add)\
                    .then_inc(vector_once, 1)
                ve.wait_ge(tensor_once, TOKT_MM)
                ve.tensor_scalar(idxT[:, :], PS[:, 2, 0:NBLK], float(NO_TOKEN), None, ALU.add).then_inc(vector_once, 1)

                def is_new(e):
                    return ve.value_load(ctl[0:1, bass.ds(e + NBLK, 1)], min_val=0, max_val=1)

                def low(new, e, src, high, used, whole, part, done):
                    def make():
                        ve.wait_ge(high, e + 1)
                        ve.wait_ge(used, e)
                        ve.tensor_tensor(part, src, whole, ALU.subtract).then_inc(done, 1)

                    if new is None:
                        make()
                        return
                    with ve.If(new > 0):
                        make()
                    with ve.If(new < 1):
                        ve.wait_ge(high, e + 1)
                        ve.sem_inc(done, 1)

                def gate_low(e, new=None):
                    low(new, e, wg, gh_ready, gate_mm, wgs[:, 0, :, :], wgs[:, 1, :, :], gl_ready)

                def up_low(e, new=None):
                    low(new, e, wu, uh_ready, up_mm, wus[:, 0, :, :], wus[:, 1, :, :], ul_ready)

                def down_low(e, new=None):
                    low(new, e, wd, dh_ready, down_mm, wds[:, 0, :, :], wds[:, 1, :, :], dl_ready)

                def x_low(e):
                    ve.wait_ge(eT_mm, e + 1)
                    ve.wait_ge(xh_ready, e + 1)
                    ve.tensor_tensor(xs[:, 1, :, :], PS[:, 0:2, :].rearrange("p a (k t) -> p (a k) t", t=P),
                                     xs[:, 0, :, :], ALU.subtract).then_inc(xl_ready, 1)

                def h_out(e):
                    ve.wait_ge(hth_ready, e + 1)
                    ve.scalar_tensor_tensor(out=hth, in0=hth, scalar=1.0, in1=PS[:, 2, :], op0=ALU.add, op1=ALU.mult)\
                        .then_inc(h1_ready, 1)
                    ve.wait_ge(h1_ready, e + 1)
                    ve.wait_ge(up_mm, e + 1)
                    ve.wait_ge(hT_mm, e)
                    ve.scalar_tensor_tensor(out=hb, in0=hth, scalar=0.5, in1=PS[:, 3, :], op0=ALU.mult, op1=ALU.mult)\
                        .then_inc(h_ready, 1)

                def h_parts(e):
                    ve.wait_ge(hT_mm, e + 1)
                    turned = PS[:, 4, :].rearrange("p (c t) -> p c t", t=P)
                    ve.tensor_copy(hs[:, 0, :, :], turned).then_inc(hh_ready, 1)
                    ve.wait_ge(hh_ready, e + 1)
                    ve.tensor_tensor(hs[:, 1, :, :], turned, hs[:, 0, :, :], ALU.subtract).then_inc(hT_ready, 1)

                ve.wait_ge(vector_once, CTL_READY)
                n_extra = ve.value_load(ctl[0:1, 2 * NBLK:2 * NBLK + 1], min_val=0, max_val=NOV)
                gate_low(0)
                up_low(0)
                x_low(0)
                new = is_new(1)
                gate_low(1, new)
                h_out(0)
                x_low(1)
                up_low(1, new)
                down_low(0)
                with ve.Fori(0, n_extra + (NE - 2)) as i:
                    new_down, new = is_new(i + 1), is_new(i + 2)
                    h_parts(i)
                    gate_low(i + 2, new)
                    h_out(i + 1)
                    x_low(i + 2)
                    up_low(i + 2, new)
                    down_low(i + 1, new_down)
                h_parts(n_extra + (NE - 2))
                h_out(n_extra + (NE - 1))
                down_low(n_extra + (NE - 1), is_new(n_extra + (NE - 1)))
                h_parts(n_extra + (NE - 1))

                ve.wait_ge(rows2n_loaded, 48)

                def final_tile(t, b, r, rows, lb):
                    chain = Chain(ve, fl, t * 7 + NTT * 14)
                    q = slice(0, rows)
                    x = xl2[b][q, :]
                    chain(ve.tensor_copy(gcur[q, 1:2].unsqueeze(2), gat[q, 1:2, bass.ds(t, 1)]))
                    ve.wait_ge(y1_scaled, t + 1)
                    chain(ve.scalar_tensor_tensor(out=y2s[b][q, :], in0=y2s[b][q, :], scalar=gcur[q, 1:2],
                                                  in1=y1s[b][q, :], op0=ALU.mult, op1=ALU.add))
                    ve.tensor_tensor(y2s[b][q, :], y2s[b][q, :], gate2[q, :], ALU.mult).then_inc(gcur_ready, 1)
                    ve.wait_ge(gcur_ready, t + 1)
                    ve.wait_ge(xl2_loaded[lb], r * 16 + 16)
                    ve.scalar_tensor_tensor(out=x, in0=x, scalar=ALPHA, in1=y2s[b][q, :],
                                            op0=ALU.mult, op1=ALU.add).then_inc(y12_used[b], 1)
                    ve.wait_ge(y12_used[b], (r if lb < 2 else NT // 2) + 1)
                    ve.wait_ge(fo_stored[b], (r if lb < 2 else NT // 2) * 16)
                    norm(xl2[b], fo[b], rows, 2 * NTT + t, chain)
                    ve.tensor_tensor(fo[b][q, :], fo[b][q, :], ln2g[q, :], ALU.mult).then_inc(fg_ready, 1)
                    assert chain.n == 7, chain.n

                with ve.Fori(0, NT // 2) as i:
                    for b in range(2):
                        final_tile(i * 2 + b, b, i, P, b)
                ve.wait_ge(rows2n_loaded, 64)
                final_tile(NT, 0, 0, DEC, 2)



_INS = ['x_prompt', 'x_sample', 'c_prompt', 'c_sample', 'state_lru_conv', 'state_lru_h', 'state_ssd_conv',
        'state_ssd', 'w_ada', 'b_ada', 'w_in', 'lru_conv_w', 'lru_conv_b', 'lru_wa', 'lru_ba', 'lru_wx', 'lru_bx',
        'lru_lambda', 'lru_norm_g', 'ssd_conv_w', 'ssd_conv_b', 'ssd_dt_bias', 'ssd_a_log', 'ssd_d',
        'ssd_norm_g', 'w_out', 'ln1_g', 'ln1_b', 'w_rg', 'b_rg', 'w_re', 'b_re', 'w_gate', 'w_up', 'w_down',
        'ln2_g', 'ln2_b']
_OUTS = [('y_prompt', (1, SEQ, D)), ('y_sample', (DEC, 1, D)),
         ('prompt_lru_conv', (1, 1, CONV - 1, D)), ('prompt_lru_h', (1, 1, D)),
         ('prompt_ssd_conv', (1, 1, CONV - 1, XBC)), ('prompt_ssd', (1, 1, HEADS, HD, STATE)),
         ('sample_lru_conv', (1, DEC, CONV - 1, D)), ('sample_lru_h', (1, DEC, D)),
         ('sample_ssd_conv', (1, DEC, CONV - 1, XBC)), ('sample_ssd', (1, DEC, HEADS, HD, STATE))]


def kernel(**inputs):
    import numpy as _np
    import concourse.bacc as _bacc
    from concourse import mybir as _mybir
    from concourse.bass_utils import run_bass_kernel_spmd as _run

    nc = _bacc.Bacc("TRN2", target_bir_lowering=False, num_devices=1)
    arrays, args = {}, []
    for name in _INS:
        a = _np.ascontiguousarray(inputs[name])
        arrays[f"in_{name}_dram"] = a
        args.append(nc.dram_tensor(f"in_{name}_dram", a.shape, _mybir.dt.from_np(a.dtype), kind="ExternalInput").ap())
    for name, shape in _OUTS:
        args.append(nc.dram_tensor(f"out_{name}_dram", shape, _mybir.dt.float32, kind="ExternalOutput").ap())
    build_step(nc, *args)
    r = _run(nc, [arrays], core_ids=[0])
    return tuple(r.results[0][f"out_{name}_dram"] for name, _ in _OUTS)
```
